# Optimizing a Trainium2 kernel written in Bass

```python
import math
import jax
import jax.numpy as jnp
from jax import lax
import numpy as np

D_MODEL = 1024
BATCH = 1
SEQ = 256
DEPTH = 2

HEAD_DIM = 64
MIX_WIDTH = D_MODEL
N_HEADS_A = (MIX_WIDTH // 2) // (2 * HEAD_DIM)
DV_A = 2 * HEAD_DIM
N_HEADS_B = (MIX_WIDTH // 2) // HEAD_DIM
DILATED_PATTERNS = ((128, 1), (512, 4), (2048, 16))
N_HEADS_C = (MIX_WIDTH // 2) // HEAD_DIM
MOBA_BLOCK = 256
MOBA_TOPK = 3
MOBA_Q_CHUNK = 16
N_HEADS_D = (MIX_WIDTH // 2) // HEAD_DIM
FORGET_BIAS_INIT = 4.0
Q_BLOCK = 128
NUM_BUCKETS = 32
MAX_DISTANCE = 128
N_BIAS_HEADS = max(N_HEADS_A + N_HEADS_B, N_HEADS_C)
D_FF = -(-8 * D_MODEL // (3 * 256)) * 256
LN_EPS = 1e-5
DEEPNORM_ALPHA = (2 * DEPTH) ** 0.25
DEEPNORM_BETA = (8 * DEPTH) ** -0.25
ATTN_SCALE = HEAD_DIM ** -0.5

AB_SIZES = [N_HEADS_A * 2 * HEAD_DIM, N_HEADS_A * 2 * HEAD_DIM, N_HEADS_A * DV_A,
            N_HEADS_B * HEAD_DIM, N_HEADS_B * HEAD_DIM, N_HEADS_B * HEAD_DIM]
CD_SIZES = [N_HEADS_C * HEAD_DIM] * 3 + [N_HEADS_D * HEAD_DIM] * 3 + [N_HEADS_D]
AB_SPLITS = [int(s) for s in np.cumsum(AB_SIZES)[:-1]]
CD_SPLITS = [int(s) for s in np.cumsum(CD_SIZES)[:-1]]
IN_AB = sum(AB_SIZES)
IN_CD = sum(CD_SIZES)


f32 = jnp.float32

def t5_bucket(dist):
    n = jnp.maximum(dist, 0)
    max_exact = NUM_BUCKETS // 2
    nf = jnp.maximum(n, 1).astype(f32)
    large = max_exact + (jnp.log(nf / max_exact) / math.log(MAX_DISTANCE / max_exact)
                         * (NUM_BUCKETS - max_exact)).astype(jnp.int32)
    large = jnp.minimum(large, NUM_BUCKETS - 1)
    return jnp.where(n < max_exact, n, large)

def t5_bias(table_cols, dist):
    return jnp.moveaxis(table_cols[t5_bucket(dist)], -1, 0).astype(f32)

def layer_norm(x, g, b):
    xf = x.astype(f32)
    mu = xf.mean(-1, keepdims=True)
    var = jnp.square(xf - mu).mean(-1, keepdims=True)
    return ((xf - mu) * lax.rsqrt(var + LN_EPS) * g + b).astype(x.dtype)

def causal_block_attention(q, k, v, map_w, bias_fn):
    B, H, M, T, _ = q.shape
    k_pos = jnp.arange(T)

    def block(q0):
        qb = lax.dynamic_slice_in_dim(q, q0, Q_BLOCK, axis=3)
        q_pos = q0 + jnp.arange(Q_BLOCK)
        s = jnp.einsum('bhmqd,bhmkd->bhmqk', qb, k).astype(f32) + bias_fn(q_pos)
        s = jnp.where(k_pos[None, :] <= q_pos[:, None], s, -jnp.inf)
        p = jnp.einsum('bhmqk,m->bhqk', jax.nn.softmax(s, axis=-1), map_w)
        return jnp.einsum('bhqk,bhkd->bhqd', p.astype(v.dtype), v)

    out = lax.map(block, jnp.arange(T // Q_BLOCK) * Q_BLOCK)
    return jnp.moveaxis(out, 0, 2).reshape(B, H, T, v.shape[-1])

def dilated_attention(q, k, v, table_cols):
    B, H, T, dh = q.shape
    outs, lses = [], []
    for window, dil in DILATED_PATTERNS:
        W = window // dil
        L = T // dil
        nb = -(-L // W)
        pad = nb * W - L

        def strided(a):
            a = a.reshape(B, H, L, dil, a.shape[-1]).swapaxes(2, 3)
            return jnp.pad(a, ((0, 0), (0, 0), (0, 0), (0, pad), (0, 0)))

        def with_prev(a):
            ab = a.reshape(B, H, dil, nb, W, a.shape[-1])
            prev = jnp.pad(ab, ((0, 0), (0, 0), (0, 0), (1, 0), (0, 0), (0, 0)))[:, :, :, :-1]
            return jnp.concatenate([prev, ab], axis=4)

        qb = strided(q).reshape(B, H, dil, nb, W, dh)
        kb = with_prev(strided(k))
        vb = with_prev(strided(v))
        u_q = jnp.arange(nb)[:, None] * W + jnp.arange(W)[None, :]
        u_k = jnp.arange(nb)[:, None] * W + jnp.arange(-W, W)[None, :]
        du = u_q[:, :, None] - u_k[:, None, :]
        valid = (du >= 0) & (du <= W) & (u_k[:, None, :] >= 0)
        bias = t5_bias(table_cols, du * dil)
        s = jnp.einsum('bhrnqd,bhrnkd->bhrnqk', qb, kb).astype(f32) + bias[None, :, None]
        s = jnp.where(valid, s, -jnp.inf)
        m = s.max(-1, keepdims=True)
        p = jnp.exp(s - m)
        den = p.sum(-1)
        o = jnp.einsum('bhrnqk,bhrnkd->bhrnqd', p.astype(vb.dtype), vb) / den[..., None]
        o = o.reshape(B, H, dil, nb * W, dh)[:, :, :, :L].swapaxes(2, 3).reshape(B, H, T, dh)
        lse = (m[..., 0] + jnp.log(den)).reshape(B, H, dil, nb * W)[..., :L]
        outs.append(o)
        lses.append(lse.swapaxes(2, 3).reshape(B, H, T))
    w = jax.nn.softmax(jnp.stack(lses), axis=0)
    return jnp.sum(w[..., None] * jnp.stack(outs), axis=0).astype(q.dtype)

def moba_attention(q, k, v, table_cols):
    B, H, T, dh = q.shape
    n_blk = -(-T // MOBA_BLOCK)
    pad = n_blk * MOBA_BLOCK - T
    kp = jnp.pad(k, ((0, 0), (0, 0), (0, pad), (0, 0)))
    vp = jnp.pad(v, ((0, 0), (0, 0), (0, pad), (0, 0)))
    k_blk = kp.reshape(B, H, n_blk, MOBA_BLOCK, dh)
    v_blk = vp.reshape(B, H, n_blk, MOBA_BLOCK, dh)
    k_mean = k_blk.mean(axis=3)
    top = min(MOBA_TOPK, n_blk)
    b_idx = jnp.arange(B)[:, None, None, None]
    h_idx = jnp.arange(H)[None, :, None, None]
    bias_flat = table_cols.T.reshape(-1).astype(f32)
    in_blk = jnp.arange(MOBA_BLOCK)

    def chunk(q0):
        qc = lax.dynamic_slice_in_dim(q, q0, MOBA_Q_CHUNK, axis=2)
        q_pos = q0 + jnp.arange(MOBA_Q_CHUNK)
        own = q0 // MOBA_BLOCK
        gate = jnp.einsum('bhcd,bhnd->bhcn', qc, k_mean).astype(f32)
        gate = jnp.where(jnp.arange(n_blk) < own, gate, -jnp.inf)
        top_s, top_i = lax.top_k(gate, top)
        sel_ok = jnp.isfinite(top_s)
        k_sel = k_blk[b_idx, h_idx, top_i]
        v_sel = v_blk[b_idx, h_idx, top_i]
        sel_pos = top_i[..., None] * MOBA_BLOCK + in_blk
        sel_bucket = t5_bucket(q_pos[:, None, None] - sel_pos)
        s_sel = (jnp.einsum('bhcd,bhcnkd->bhcnk', qc, k_sel).astype(f32)
                 + bias_flat[h_idx[..., None] * NUM_BUCKETS + sel_bucket])
        s_sel = jnp.where(sel_ok[..., None], s_sel, -jnp.inf)
        own_start = own * MOBA_BLOCK
        k_own = lax.dynamic_slice_in_dim(kp, own_start, MOBA_BLOCK, axis=2)
        v_own = lax.dynamic_slice_in_dim(vp, own_start, MOBA_BLOCK, axis=2)
        own_dist = q_pos[:, None] - (own_start + in_blk)[None, :]
        s_own = (jnp.einsum('bhcd,bhkd->bhck', qc, k_own).astype(f32)
                 + t5_bias(table_cols, own_dist)[None])
        s_own = jnp.where(own_dist >= 0, s_own, -jnp.inf)
        s = jnp.concatenate([s_sel.reshape(B, H, MOBA_Q_CHUNK, top * MOBA_BLOCK), s_own], axis=-1)
        p = jax.nn.softmax(s, axis=-1).astype(v.dtype)
        p_sel = p[..., :top * MOBA_BLOCK].reshape(B, H, MOBA_Q_CHUNK, top, MOBA_BLOCK)
        p_own = p[..., top * MOBA_BLOCK:]
        return (jnp.einsum('bhcnk,bhcnkd->bhcd', p_sel, v_sel)
                + jnp.einsum('bhck,bhkd->bhcd', p_own, v_own))

    out = lax.map(chunk, jnp.arange(T // MOBA_Q_CHUNK) * MOBA_Q_CHUNK)
    return jnp.moveaxis(out, 0, 2).reshape(B, H, T, dh)

def split_heads(a, dh):
    B, T, _ = a.shape
    return a.reshape(B, T, -1, dh).transpose(0, 2, 1, 3)

def merge_heads(a):
    B, H, T, dh = a.shape
    return a.transpose(0, 2, 1, 3).reshape(B, T, H * dh)

def mixer_ab(h, w_in, w_o, lam, subln_g, table, lambda_init):
    B, T, _ = h.shape
    qa, ka, va, qb, kb, vb = jnp.split(h @ w_in, AB_SPLITS, axis=-1)
    qa = qa.reshape(B, T, N_HEADS_A, 2, HEAD_DIM).transpose(0, 2, 3, 1, 4) * ATTN_SCALE
    ka = ka.reshape(B, T, N_HEADS_A, 2, HEAD_DIM).transpose(0, 2, 3, 1, 4)
    va = split_heads(va, DV_A)
    lamf = lam.astype(f32)
    lam_full = (jnp.exp(jnp.sum(lamf[0] * lamf[1])) - jnp.exp(jnp.sum(lamf[2] * lamf[3]))
                + lambda_init)
    map_w = jnp.stack([jnp.ones((), f32), -lam_full])
    table_a = table[:, :N_HEADS_A]
    k_pos = jnp.arange(T)
    bias_a = lambda q_pos: t5_bias(table_a, q_pos[:, None] - k_pos[None, :])[None, :, None]
    oa = causal_block_attention(qa, ka, va, map_w, bias_a).astype(f32)
    oa = oa * lax.rsqrt(jnp.mean(jnp.square(oa), -1, keepdims=True) + LN_EPS)
    oa = (oa * subln_g * (1.0 - lambda_init)).astype(h.dtype)
    ob = dilated_attention(split_heads(qb, HEAD_DIM) * ATTN_SCALE, split_heads(kb, HEAD_DIM),
                           split_heads(vb, HEAD_DIM), table[:, N_HEADS_A:N_HEADS_A + N_HEADS_B])
    return jnp.concatenate([merge_heads(oa), merge_heads(ob)], axis=-1) @ w_o

def mixer_cd(h, w_in, w_o, forget_b, table):
    qc, kc, vc, qd, kd, vd, fd = jnp.split(h @ w_in, CD_SPLITS, axis=-1)
    oc = moba_attention(split_heads(qc, HEAD_DIM) * ATTN_SCALE, split_heads(kc, HEAD_DIM),
                        split_heads(vc, HEAD_DIM), table[:, :N_HEADS_C])
    log_f = jax.nn.log_sigmoid((fd + forget_b).astype(f32)).transpose(0, 2, 1)
    cum = jnp.cumsum(log_f, axis=-1)
    fox_bias = lambda q_pos: (cum[:, :, q_pos, None] - cum[:, :, None, :])[:, :, None]
    od = causal_block_attention((split_heads(qd, HEAD_DIM) * ATTN_SCALE)[:, :, None],
                                split_heads(kd, HEAD_DIM)[:, :, None],
                                split_heads(vd, HEAD_DIM), jnp.ones((1,), f32), fox_bias)
    return jnp.concatenate([merge_heads(oc), merge_heads(od)], axis=-1) @ w_o

def swiglu(h, w_in, w_out):
    g, u = jnp.split(h @ w_in, 2, axis=-1)
    return (jax.nn.silu(g) * u) @ w_out

def first_inputs(seed: int = 0) -> dict:
    key = jax.random.key(seed)
    ks = jax.random.split(key, 15)
    n_even = (DEPTH + 1) // 2
    n_odd = DEPTH // 2
    nrm = lambda k, shape, std: jax.random.normal(k, shape, f32) * std
    return {
        "x": nrm(ks[0], (BATCH, SEQ, D_MODEL), 1.0),
        "c": nrm(ks[1], (BATCH, D_MODEL), 1.0),
        "rel_bias": nrm(ks[2], (NUM_BUCKETS, N_BIAS_HEADS), 0.5),
        "w_ada": nrm(ks[3], (DEPTH, D_MODEL, 6 * D_MODEL), 0.1 * D_MODEL ** -0.5),
        "b_ada": nrm(ks[4], (DEPTH, 6 * D_MODEL), 0.01),
        "ln_g": 1.0 + nrm(ks[5], (DEPTH, 2, D_MODEL), 0.01),
        "ln_b": nrm(ks[6], (DEPTH, 2, D_MODEL), 0.01),
        "w_in_ab": nrm(ks[7], (n_even, D_MODEL, IN_AB), D_MODEL ** -0.5),
        "diff_lambda": nrm(ks[8], (n_even, 4, HEAD_DIM), 0.1),
        "diff_subln_g": 1.0 + nrm(ks[9], (n_even, DV_A), 0.01),
        "w_in_cd": nrm(ks[10], (n_odd, D_MODEL, IN_CD), D_MODEL ** -0.5),
        "forget_b": FORGET_BIAS_INIT + nrm(ks[11], (n_odd, N_HEADS_D), 0.5),
        "w_o": nrm(ks[12], (DEPTH, MIX_WIDTH, D_MODEL), DEEPNORM_BETA * MIX_WIDTH ** -0.5),
        "w_ffn_in": nrm(ks[13], (DEPTH, D_MODEL, 2 * D_FF), D_MODEL ** -0.5),
        "w_ffn_out": nrm(ks[14], (DEPTH, D_FF, D_MODEL), DEEPNORM_BETA * D_FF ** -0.5),
    }

def first_block(x, c, rel_bias, w_ada, b_ada, ln_g, ln_b, w_in_ab, diff_lambda, diff_subln_g,
              w_in_cd, forget_b, w_o, w_ffn_in, w_ffn_out):
    for l in range(DEPTH):
        ada = jax.nn.silu(c) @ w_ada[l] + b_ada[l]
        sh1, sc1, g1, sh2, sc2, g2 = [a[:, None, :] for a in jnp.split(ada, 6, axis=-1)]
        h = x * (1.0 + sc1) + sh1
        if l % 2 == 0:
            i = l // 2
            lambda_init = 0.8 - 0.6 * math.exp(-0.3 * l)
            y = mixer_ab(h, w_in_ab[i], w_o[l], diff_lambda[i], diff_subln_g[i], rel_bias,
                         lambda_init)
        else:
            i = l // 2
            y = mixer_cd(h, w_in_cd[i], w_o[l], forget_b[i], rel_bias)
        x = layer_norm(DEEPNORM_ALPHA * x + (1.0 + g1) * y, ln_g[l, 0], ln_b[l, 0])
        h = x * (1.0 + sc2) + sh2
        y = swiglu(h, w_ffn_in[l], w_ffn_out[l])
        x = layer_norm(DEEPNORM_ALPHA * x + (1.0 + g2) * y, ln_g[l, 1], ln_b[l, 1])
    return x


CHUNK = 64
EPS = 1e-6
D_FF_2 = 2816

SSD_HEADS = 8
SSD_HEAD_DIM = 64
SSD_INNER = SSD_HEADS * SSD_HEAD_DIM
SSD_GROUPS = 2
SSD_STATE = 128
SSD_CONV = 4
SSD_XBC = SSD_INNER + 2 * SSD_GROUPS * SSD_STATE
SSD_HPG = SSD_HEADS // SSD_GROUPS

S5_WIDTH = 512
S5_GROUP = 16
S5_GROUPS = S5_WIDTH // S5_GROUP
S5_STATE = 64

ATT_HEADS = 8
ATT_HEAD_DIM = 64
ATT_WIDTH = ATT_HEADS * ATT_HEAD_DIM
LEFT_CHUNKS = 8
BAND_CHUNKS = LEFT_CHUNKS + 1
BAND = BAND_CHUNKS * CHUNK
MAX_REL = 128

POOL_WINDOWS = (2, 4, 8, 16)
POOL_GROUPS = len(POOL_WINDOWS)
POOL_WIDTH = 512
POOL_GROUP = POOL_WIDTH // POOL_GROUPS
POOL_MAX = max(POOL_WINDOWS)

EVEN_IN = SSD_INNER + SSD_XBC + SSD_HEADS + S5_WIDTH
EVEN_OUT = SSD_INNER + S5_WIDTH
ODD_IN = 3 * ATT_WIDTH + POOL_WIDTH
ODD_OUT = ATT_WIDTH + POOL_WIDTH
N_EVEN = (DEPTH + 1) // 2
N_ODD = DEPTH // 2


def _rmsnorm(x, gain):
    xf = x.astype(jnp.float32)
    y = xf * lax.rsqrt(jnp.mean(xf * xf, axis=-1, keepdims=True) + EPS)
    return (y * gain.astype(jnp.float32)).astype(x.dtype)

def _swiglu(h, w_gate, w_up, w_down):
    return (jax.nn.silu(h @ w_gate) * (h @ w_up)) @ w_down

def _causal_depthwise_conv(x, w, b):
    c = x.shape[-1]
    y = lax.conv_general_dilated(
        x.astype(jnp.float32), w.astype(jnp.float32)[:, None, :],
        window_strides=(1,), padding=[(SSD_CONV - 1, 0)],
        dimension_numbers=('NWC', 'WIO', 'NWC'), feature_group_count=c)
    return y + b.astype(jnp.float32)

def _ssd_mixer(zxbcdt, conv_w, conv_b, dt_bias, a_log, d_skip, norm_gain):
    f32 = jnp.float32
    bsz, s, _ = zxbcdt.shape
    nc = s // CHUNK
    z, xbc, dt = jnp.split(zxbcdt, [SSD_INNER, SSD_INNER + SSD_XBC], axis=-1)
    xbc = jax.nn.silu(_causal_depthwise_conv(xbc, conv_w, conv_b))
    xs, bm, cm = jnp.split(xbc, [SSD_INNER, SSD_INNER + SSD_GROUPS * SSD_STATE], axis=-1)
    xs = xs.reshape(bsz, nc, CHUNK, SSD_GROUPS, SSD_HPG, SSD_HEAD_DIM)
    bm = bm.reshape(bsz, nc, CHUNK, SSD_GROUPS, SSD_STATE)
    cm = cm.reshape(bsz, nc, CHUNK, SSD_GROUPS, SSD_STATE)
    dt = jax.nn.softplus(dt.astype(f32) + dt_bias.astype(f32))
    dt = dt.reshape(bsz, nc, CHUNK, SSD_GROUPS, SSD_HPG)
    a = -jnp.exp(a_log.astype(f32)).reshape(SSD_GROUPS, SSD_HPG)
    a_cs = jnp.cumsum(dt * a, axis=2)
    xdt = xs * dt[..., None]
    causal = jnp.tril(jnp.ones((CHUNK, CHUNK), dtype=bool))[:, :, None, None]
    seg = a_cs[:, :, :, None] - a_cs[:, :, None, :]
    decay = jnp.exp(jnp.where(causal, seg, -jnp.inf))
    cb = jnp.einsum('bclgn,bcsgn->bclsg', cm, bm)
    y_diag = jnp.einsum('bclsg,bclsgj,bcsgjp->bclgjp', cb, decay, xdt)
    to_end = jnp.exp(a_cs[:, :, -1:] - a_cs)
    states = jnp.einsum('bclgn,bclgj,bclgjp->bcgjpn', bm, to_end, xdt)
    chunk_decay = jnp.exp(a_cs[:, :, -1])

    def step(h, inp):
        st, dec = inp
        return dec[..., None, None] * h + st, h

    h0 = jnp.zeros((bsz, SSD_GROUPS, SSD_HPG, SSD_HEAD_DIM, SSD_STATE), f32)
    _, h_prev = lax.scan(step, h0, (jnp.moveaxis(states, 1, 0), jnp.moveaxis(chunk_decay, 1, 0)))
    h_prev = jnp.moveaxis(h_prev, 0, 1)
    y_off = jnp.einsum('bclgn,bcgjpn,bclgj->bclgjp', cm, h_prev, jnp.exp(a_cs))
    y = y_diag + y_off + d_skip.astype(f32).reshape(SSD_GROUPS, SSD_HPG, 1) * xs
    y = y.reshape(bsz, s, SSD_INNER) * jax.nn.silu(z.astype(f32))
    yg = y.reshape(bsz, s, SSD_GROUPS, SSD_INNER // SSD_GROUPS)
    yg = yg * lax.rsqrt(jnp.mean(yg * yg, axis=-1, keepdims=True) + EPS)
    return (yg.reshape(bsz, s, SSD_INNER) * norm_gain.astype(f32)).astype(zxbcdt.dtype)

def _complex_affine_combine(e1, e2):
    a1r, a1i, x1r, x1i = e1
    a2r, a2i, x2r, x2i = e2
    return (a2r * a1r - a2i * a1i,
            a2r * a1i + a2i * a1r,
            a2r * x1r - a2i * x1i + x2r,
            a2r * x1i + a2i * x1r + x2i)

def _s5_mixer(u, a_re, a_im, log_dt, b_re, b_im, c_re, c_im, d_skip, w_glu, b_glu):
    f32 = jnp.float32
    bsz, s, _ = u.shape
    uf = u.astype(f32).reshape(bsz, s, S5_GROUPS, S5_GROUP)
    ar = a_re.astype(f32)
    ai = a_im.astype(f32)
    dt = jnp.exp(log_dt.astype(f32))[:, None]
    mag = jnp.exp(dt * ar)
    abar_re = mag * jnp.cos(dt * ai)
    abar_im = mag * jnp.sin(dt * ai)
    den = ar * ar + ai * ai
    f_re = ((abar_re - 1.0) * ar + abar_im * ai) / den
    f_im = (abar_im * ar - (abar_re - 1.0) * ai) / den
    br = b_re.astype(f32)
    bi = b_im.astype(f32)
    bb_re = f_re[..., None] * br - f_im[..., None] * bi
    bb_im = f_re[..., None] * bi + f_im[..., None] * br
    drive_re = jnp.einsum('bsgi,gpi->sbgp', uf, bb_re)
    drive_im = jnp.einsum('bsgi,gpi->sbgp', uf, bb_im)
    shape_a = (s, 1, S5_GROUPS, S5_STATE)
    dec_re = jnp.broadcast_to(abar_re, shape_a)
    dec_im = jnp.broadcast_to(abar_im, shape_a)
    _, _, h_re, h_im = lax.associative_scan(
        _complex_affine_combine, (dec_re, dec_im, drive_re, drive_im), axis=0)
    y = (jnp.einsum('gip,sbgp->bsgi', c_re.astype(f32), h_re)
         - jnp.einsum('gip,sbgp->bsgi', c_im.astype(f32), h_im)
         + d_skip.astype(f32) * uf)
    y = y.reshape(bsz, s, S5_WIDTH)
    gate = jax.nn.gelu(y) @ w_glu.astype(f32) + b_glu.astype(f32)
    return (y * jax.nn.sigmoid(gate)).astype(u.dtype)

def _chunk_band_attention(q, k, v, q_gain, k_gain, rel_bias):
    f32 = jnp.float32
    bsz, s, _ = q.shape
    nc = s // CHUNK
    q = _rmsnorm(q.reshape(bsz, nc, CHUNK, ATT_HEADS, ATT_HEAD_DIM), q_gain)
    k = _rmsnorm(k.reshape(bsz, s, ATT_HEADS, ATT_HEAD_DIM), k_gain)
    v = v.reshape(bsz, s, ATT_HEADS, ATT_HEAD_DIM)
    front = ((0, 0), (LEFT_CHUNKS * CHUNK, 0), (0, 0), (0, 0))
    kp = jnp.pad(k, front).reshape(bsz, nc + LEFT_CHUNKS, CHUNK, ATT_HEADS, ATT_HEAD_DIM)
    vp = jnp.pad(v, front).reshape(bsz, nc + LEFT_CHUNKS, CHUNK, ATT_HEADS, ATT_HEAD_DIM)
    band_idx = jnp.arange(nc)[:, None] + jnp.arange(BAND_CHUNKS)[None, :]
    kb = kp[:, band_idx].reshape(bsz, nc, BAND, ATT_HEADS, ATT_HEAD_DIM)
    vb = vp[:, band_idx].reshape(bsz, nc, BAND, ATT_HEADS, ATT_HEAD_DIM)
    scores = jnp.einsum('bclhd,bckhd->bhclk', q.astype(f32), kb.astype(f32)) * (ATT_HEAD_DIM ** -0.5)
    q_off = LEFT_CHUNKS * CHUNK + jnp.arange(CHUNK)
    dist = q_off[:, None] - jnp.arange(BAND)[None, :]
    bias = rel_bias.astype(f32)[:, jnp.clip(dist, -MAX_REL, MAX_REL) + MAX_REL]
    valid = jnp.repeat(band_idx >= LEFT_CHUNKS, CHUNK, axis=1)
    scores = jnp.where(valid[None, None, :, None, :], scores + bias[None, :, None], -jnp.inf)
    probs = jax.nn.softmax(scores, axis=-1)
    out = jnp.einsum('bhclk,bckhd->bclhd', probs, vb.astype(f32))
    return out.reshape(bsz, s, ATT_WIDTH).astype(q.dtype)

def _multiscale_pool(u, w_pool, scale):
    f32 = jnp.float32
    bsz, s, _ = u.shape
    uf = u.astype(f32).reshape(bsz, s, POOL_GROUPS, POOL_GROUP)
    csum = jnp.pad(jnp.cumsum(uf, axis=1), ((0, 0), (POOL_MAX, 0), (0, 0), (0, 0)))
    pos = jnp.arange(s)
    means = []
    for g, w in enumerate(POOL_WINDOWS):
        win = csum[:, POOL_MAX:, g] - csum[:, POOL_MAX - w:POOL_MAX - w + s, g]
        count = jnp.minimum(pos + 1, w).astype(f32)[None, :, None]
        means.append(win / count)
    pooled = jnp.stack(means, axis=2) - uf
    y = jnp.einsum('bsgi,gio->bsgo', pooled, w_pool.astype(f32)).reshape(bsz, s, POOL_WIDTH)
    return (y * scale.astype(f32)).astype(u.dtype)

def second_inputs(seed: int = 0) -> dict:
    key = jax.random.key(seed)
    keys = iter(jax.random.split(key, 48))
    f32 = jnp.float32

    def normal(shape, scale):
        return scale * jax.random.normal(next(keys), shape, f32)

    def gain(shape):
        return 1.0 + 0.05 * jax.random.normal(next(keys), shape, f32)

    def log_uniform(shape, lo, hi):
        return jax.random.uniform(next(keys), shape, f32, math.log(lo), math.log(hi))

    ssd_dt = jnp.exp(log_uniform((N_EVEN, SSD_HEADS), 1e-3, 1e-1))
    ssd_dt_bias = ssd_dt + jnp.log(-jnp.expm1(-ssd_dt))
    ssd_a_log = jnp.log(jax.random.uniform(next(keys), (N_EVEN, SSD_HEADS), f32, 1.0, 16.0))
    s5_shape = (N_EVEN, S5_GROUPS, S5_STATE)
    s5_a_re = -0.5 + normal(s5_shape, 0.01)
    s5_a_im = math.pi * jnp.arange(S5_STATE, dtype=f32) + normal(s5_shape, 0.01)
    s5_log_dt = log_uniform((N_EVEN, S5_GROUPS), 1e-3, 1e-1)
    return {
        'x': normal((BATCH, SEQ, D_MODEL), 1.0),
        'ffn1_norm': gain((DEPTH, D_MODEL)),
        'ffn1_w_gate': normal((DEPTH, D_MODEL, D_FF_2), D_MODEL ** -0.5),
        'ffn1_w_up': normal((DEPTH, D_MODEL, D_FF_2), D_MODEL ** -0.5),
        'ffn1_w_down': normal((DEPTH, D_FF_2, D_MODEL), D_FF_2 ** -0.5),
        'mix_norm': gain((DEPTH, D_MODEL)),
        'even_w_in': normal((N_EVEN, D_MODEL, EVEN_IN), D_MODEL ** -0.5),
        'even_w_out': normal((N_EVEN, EVEN_OUT, D_MODEL), EVEN_OUT ** -0.5),
        'ssd_conv_w': normal((N_EVEN, SSD_CONV, SSD_XBC), SSD_CONV ** -0.5),
        'ssd_conv_b': normal((N_EVEN, SSD_XBC), 0.02),
        'ssd_dt_bias': ssd_dt_bias,
        'ssd_a_log': ssd_a_log,
        'ssd_d': gain((N_EVEN, SSD_HEADS)),
        'ssd_norm': gain((N_EVEN, SSD_INNER)),
        's5_a_re': s5_a_re,
        's5_a_im': s5_a_im,
        's5_log_dt': s5_log_dt,
        's5_b_re': normal((N_EVEN, S5_GROUPS, S5_STATE, S5_GROUP), (2 * S5_GROUP) ** -0.5),
        's5_b_im': normal((N_EVEN, S5_GROUPS, S5_STATE, S5_GROUP), (2 * S5_GROUP) ** -0.5),
        's5_c_re': normal((N_EVEN, S5_GROUPS, S5_GROUP, S5_STATE), S5_STATE ** -0.5),
        's5_c_im': normal((N_EVEN, S5_GROUPS, S5_GROUP, S5_STATE), S5_STATE ** -0.5),
        's5_d': normal((N_EVEN, S5_GROUPS, S5_GROUP), 1.0),
        's5_w_glu': normal((N_EVEN, S5_WIDTH, S5_WIDTH), S5_WIDTH ** -0.5),
        's5_b_glu': normal((N_EVEN, S5_WIDTH), 0.02),
        'odd_w_in': normal((N_ODD, D_MODEL, ODD_IN), D_MODEL ** -0.5),
        'odd_w_out': normal((N_ODD, ODD_OUT, D_MODEL), ODD_OUT ** -0.5),
        'attn_q_norm': gain((N_ODD, ATT_HEAD_DIM)),
        'attn_k_norm': gain((N_ODD, ATT_HEAD_DIM)),
        'attn_rel_bias': normal((N_ODD, ATT_HEADS, 2 * MAX_REL + 1), 0.1),
        'pool_w': normal((N_ODD, POOL_GROUPS, POOL_GROUP, POOL_GROUP), POOL_GROUP ** -0.5),
        'pool_scale': gain((N_ODD, POOL_WIDTH)),
        'ffn2_norm': gain((DEPTH, D_MODEL)),
        'ffn2_w_gate': normal((DEPTH, D_MODEL, D_FF_2), D_MODEL ** -0.5),
        'ffn2_w_up': normal((DEPTH, D_MODEL, D_FF_2), D_MODEL ** -0.5),
        'ffn2_w_down': normal((DEPTH, D_FF_2, D_MODEL), D_FF_2 ** -0.5),
    }

def second_block(x, ffn1_norm, ffn1_w_gate, ffn1_w_up, ffn1_w_down, mix_norm,
              even_w_in, even_w_out, ssd_conv_w, ssd_conv_b, ssd_dt_bias, ssd_a_log, ssd_d, ssd_norm,
              s5_a_re, s5_a_im, s5_log_dt, s5_b_re, s5_b_im, s5_c_re, s5_c_im, s5_d, s5_w_glu, s5_b_glu,
              odd_w_in, odd_w_out, attn_q_norm, attn_k_norm, attn_rel_bias, pool_w, pool_scale,
              ffn2_norm, ffn2_w_gate, ffn2_w_up, ffn2_w_down):
    for layer in range(DEPTH):
        i = layer // 2
        h = _rmsnorm(x, ffn1_norm[layer])
        x = x + 0.5 * _swiglu(h, ffn1_w_gate[layer], ffn1_w_up[layer], ffn1_w_down[layer])
        h = _rmsnorm(x, mix_norm[layer])
        if layer % 2 == 0:
            proj = h @ even_w_in[i]
            zxbcdt, u = jnp.split(proj, [SSD_INNER + SSD_XBC + SSD_HEADS], axis=-1)
            y_a = _ssd_mixer(zxbcdt, ssd_conv_w[i], ssd_conv_b[i], ssd_dt_bias[i],
                             ssd_a_log[i], ssd_d[i], ssd_norm[i])
            y_b = _s5_mixer(u, s5_a_re[i], s5_a_im[i], s5_log_dt[i], s5_b_re[i], s5_b_im[i],
                            s5_c_re[i], s5_c_im[i], s5_d[i], s5_w_glu[i], s5_b_glu[i])
            mixed = jnp.concatenate([y_a, y_b], axis=-1).astype(x.dtype) @ even_w_out[i]
        else:
            proj = h @ odd_w_in[i]
            q, k, v, u = jnp.split(proj, [ATT_WIDTH, 2 * ATT_WIDTH, 3 * ATT_WIDTH], axis=-1)
            y_c = _chunk_band_attention(q, k, v, attn_q_norm[i], attn_k_norm[i], attn_rel_bias[i])
            y_d = _multiscale_pool(u, pool_w[i], pool_scale[i])
            mixed = jnp.concatenate([y_c, y_d], axis=-1).astype(x.dtype) @ odd_w_out[i]
        x = x + mixed.astype(x.dtype)
        h = _rmsnorm(x, ffn2_norm[layer])
        x = x + 0.5 * _swiglu(h, ffn2_w_gate[layer], ffn2_w_up[layer], ffn2_w_down[layer])
    return x


def setup_inputs(seed=0):
    out = dict(first_inputs(seed))
    for name, value in second_inputs(seed + 1).items():
        if name != "x":
            out[name + "_2"] = value
    return out


def reference(
    x, c, rel_bias, w_ada, b_ada, ln_g, ln_b, w_in_ab, diff_lambda, diff_subln_g, w_in_cd,
    forget_b, w_o, w_ffn_in, w_ffn_out, ffn1_norm_2, ffn1_w_gate_2, ffn1_w_up_2, ffn1_w_down_2,
    mix_norm_2, even_w_in_2, even_w_out_2, ssd_conv_w_2, ssd_conv_b_2, ssd_dt_bias_2,
    ssd_a_log_2, ssd_d_2, ssd_norm_2, s5_a_re_2, s5_a_im_2, s5_log_dt_2, s5_b_re_2, s5_b_im_2,
    s5_c_re_2, s5_c_im_2, s5_d_2, s5_w_glu_2, s5_b_glu_2, odd_w_in_2, odd_w_out_2,
    attn_q_norm_2, attn_k_norm_2, attn_rel_bias_2, pool_w_2, pool_scale_2, ffn2_norm_2,
    ffn2_w_gate_2, ffn2_w_up_2, ffn2_w_down_2,
):
    x = first_block(
        x, c, rel_bias, w_ada, b_ada, ln_g, ln_b, w_in_ab, diff_lambda, diff_subln_g, w_in_cd,
        forget_b, w_o, w_ffn_in, w_ffn_out,
    )
    return second_block(
        x, ffn1_norm_2, ffn1_w_gate_2, ffn1_w_up_2, ffn1_w_down_2, mix_norm_2, even_w_in_2,
        even_w_out_2, ssd_conv_w_2, ssd_conv_b_2, ssd_dt_bias_2, ssd_a_log_2, ssd_d_2,
        ssd_norm_2, s5_a_re_2, s5_a_im_2, s5_log_dt_2, s5_b_re_2, s5_b_im_2, s5_c_re_2,
        s5_c_im_2, s5_d_2, s5_w_glu_2, s5_b_glu_2, odd_w_in_2, odd_w_out_2, attn_q_norm_2,
        attn_k_norm_2, attn_rel_bias_2, pool_w_2, pool_scale_2, ffn2_norm_2, ffn2_w_gate_2,
        ffn2_w_up_2, ffn2_w_down_2,
    )


_drawn_inputs = setup_inputs


def setup_inputs(seed=0):
    import zlib

    import numpy as np

    out = dict(_drawn_inputs(seed))
    spreads = {}
    factors = {'b_ada': 2.987,
     'diff_subln_g': 8.0,
     'forget_b': 24.696,
     'ssd_conv_b_2': 3.359,
     's5_a_re_2': 64.0,
     's5_b_re_2': 2.892,
     's5_b_im_2': 2.887,
     's5_c_re_2': 2.883,
     's5_c_im_2': 2.886,
     's5_b_glu_2': 8.0,
     'attn_q_norm_2': 8.0,
     'attn_k_norm_2': 8.0,
     'attn_rel_bias_2': 8.0,
     'pool_scale_2': 3.12}
    for name, (base, spread) in spreads.items():
        noise = np.random.default_rng([zlib.crc32(name.encode()), seed]).standard_normal(out[name].shape)
        drawn = base * np.exp(spread * noise) if base else spread * noise
        out[name] = jnp.asarray(drawn.astype(out[name].dtype))
    for name, factor in factors.items():
        out[name] = (out[name] * factor).astype(out[name].dtype)
    return out
```

```python
from contextlib import ExitStack

import numpy as np

import concourse.bass as bass
from concourse import mybir

F32 = mybir.dt.float32
F32R = mybir.dt.float32r
BF16 = mybir.dt.bfloat16
ACT = mybir.ActivationFunctionType
ALU = mybir.AluOpType
AX = mybir.AxisListType

P = 128
T = 256
TT = T // P
D = 1024
KC = D // P
FF = 2816
UC = 256
FC = FF // UC
UNIT = 2048
RING = 3
HD = 64
NUM_BUCKETS, MAX_DISTANCE = 32, 128
ATTN_SCALE = HD ** -0.5
ALPHA = 4 ** 0.25
LAMBDA_INIT = 0.2
LN_EPS, RMS_EPS = 1e-5, 1e-6
NEG = -1.0e30
TOEP = 384

_PHASES = [("ab", 12), ("o_ab", 4), ("ff0", 33), ("cd", 12), ("o_cd", 4), ("ff1", 33), ("f1a", 33), ("even", 8),
           ("o_even", 4), ("f2a", 33), ("f1b", 33), ("odd", 8), ("o_odd", 4), ("f2b", 33)]
START, _n = {}, 0
for _name, _count in _PHASES:
    START[_name] = _n
    _n += _count
UNITS = _n
PROJ = {"ab": 0, "cd": 12, "even": 24, "odd": 32}
TR = {n: i for i, n in enumerate(["ab", "o_ab", "ff0", "cd", "o_cd", "ff1", "f1a", "even", "o_even", "f2a", "f1b",
                                  "odd", "o_odd", "f2b"])}
FFN = {n: i for i, n in enumerate(["ff0", "ff1", "f1a", "f2a", "f1b", "f2b"])}
LO0 = USED0 = EVAC0 = 3

C_FF1, C_MIX, C_FF2, C_CONVB, C_CONVW, C_SSDN, C_GLUB, C_PSCALE, C_S5D, C_SUBLN, C_QN, C_KN = (
    0, 16, 32, 48, 56, 88, 92, 96, 100, 104, 105, 106)
NCOL = 107
TWO_PI_PARTS = (6.28125, 1.93500518798828125e-3, 3.0199159819567528e-7)
ROUND_MAGIC = 12582912.0


def constants():
    d = 255 - np.arange(TOEP)
    n = np.maximum(d, 0)
    nf = np.maximum(n, 1).astype(np.float32)
    exact = NUM_BUCKETS // 2
    large = exact + (np.log(nf / np.float32(exact)) / np.float32(np.log(MAX_DISTANCE / exact))
                     * np.float32(NUM_BUCKETS - exact)).astype(np.int32)
    bucket = np.where(n < exact, n, np.minimum(large, NUM_BUCKETS - 1))
    onehot = ((bucket[None, :] == np.arange(NUM_BUCKETS)[:, None]) & (d >= 0)).astype(np.float32)
    causal = np.where(d >= 0, 0.0, NEG)
    many = (d <= 128).astype(int) + (d % 4 == 0) + (d % 16 == 0)
    many = np.where(d >= 0, many, 0)
    dilated = np.where(many > 0, np.log(np.maximum(many, 1)), NEG)
    add = np.stack([causal] * 4 + [dilated] * 8 + [causal] * 8).astype(np.float32)
    i = np.arange(P)
    lower = np.where(i[None, :] <= i[:, None], 0.0, NEG).astype(np.float32)
    t = np.arange(16)
    pool = np.stack([1.0 / np.minimum(t + 1, w) for w in (2, 4, 8, 16)]).astype(np.float32).reshape(1, 64)
    return {"k_flip": np.ascontiguousarray(np.eye(P, dtype=np.float32)[::-1]), "k_ident": np.eye(P, dtype=np.float32), "k_onehot": onehot, "k_add": add, "k_lower": lower,
            "k_upper": np.ascontiguousarray(lower.T), "k_pool": pool}


def build_program(nc, a, out):
    ctx = ExitStack()
    with ctx:
        def sb(name, shape, dt=F32):
            return ctx.enter_context(nc.sbuf_tensor("s_" + name, shape, dt))

        def sem(name):
            return ctx.enter_context(nc.semaphore(name))

        bank = [ctx.enter_context(nc.psum_tensor(f"bank{i}", [P, 512], F32)) for i in range(8)]

        raw = sb("raw", [P, RING, UNIT])
        wH = sb("wH", [P, RING, UNIT], F32R)
        wL = sb("wL", [P, RING, UNIT], F32R)
        x = sb("x", [P, TT, D])
        t32 = sb("t32", [P, KC, T])
        hH = sb("hH", [P, KC, T], F32R)
        hL = sb("hL", [P, KC, T], F32R)
        mix = sb("mix", [P, 10368])
        aH = sb("aH", [P, 2, T], F32R)
        aL = sb("aL", [P, 2, T], F32R)
        late = sb("late", [P, 10240])
        ident = sb("ident", [P, P])
        ones = sb("ones", [P, P])
        zeros = sb("zeros", [P, 640], BF16)
        cols = sb("cols", [P, NCOL])
        colC = sb("colC", [P, 48])
        adaC = sb("adaC", [P, 2, 32])
        flip = sb("flip", [P, P])
        lower = sb("lower", [P, P])
        upper = sb("upper", [P, P])
        silc = sb("silc", [P, KC])
        wsmall = sb("wsmall", [P, 2, KC, 8])
        small = sb("small", [P, 512])
        s5c = sb("s5c", [P, 12, 16])
        poolc = sb("poolc", [P, 64])
        nat = t32[:].rearrange("p k t -> p (k t)").rearrange("p (a n) -> p a n", a=TT)

        def carve(region, at, *shape):
            size = int(np.prod(shape))
            v = region[:, at:at + size]
            if len(shape) == 2:
                return v.rearrange("p (a b) -> p a b", a=shape[0])
            if len(shape) == 3:
                return v.rearrange("p (a b c) -> p a b c", a=shape[0], b=shape[1])
            return v

        qT = carve(mix, 0, KC, T)
        kT = carve(mix, 2048, KC, T)
        v = carve(mix, 4096, TT, D)
        bias = carve(mix, 6144, 12, T)
        sP = carve(mix, 9216, 3, 384)
        sil = carve(mix, 0, 512)
        act = carve(mix, 512, 512)
        ada_raw = carve(late, 0, 2, KC * 512)
        ada_acc = carve(late, 8192, 2, 512)
        lnv = carve(mix, 1024, 2, D)
        PT = carve(late, 4096, 2, 384)
        foxb = carve(late, 4096 + 768, 2, 384)
        gate1 = sb("gate1", [P, 2, D])
        ada_b = carve(late, 9216, 2, 512)

        raw_full = [sem(f"raw_full{i}") for i in range(RING)]
        ada_full = [sem(f"ada_full{i}") for i in range(2)]
        hi_ready, lo_ready, unit_used = sem("hi_ready"), sem("lo_ready"), sem("unit_used")
        proj_evac = sem("proj_evac")
        ada_step = [sem(f"ada_step{i}") for i in range(2)]
        ada_mm = [sem(f"ada_mm{i}") for i in range(2)]
        ada_out = [sem(f"ada_out{i}") for i in range(2)]
        nat_ready, tr_done, t32_ready, th_ready, tl_ready = (
            sem(s) for s in ("nat_ready", "tr_done", "t32_ready", "th_ready", "tl_ready"))
        y_ready = sem("y_ready")
        sil_done, act_mul, act_hi, act_lo = (sem(s) for s in ("sil_done", "act_mul", "act_hi", "act_lo"))
        flip_mm, flip_out = sem("flip_mm"), sem("flip_out")
        s_ready, s_max, p_ready, pT_ready, pT_copied, o_ready, o_done = (
            sem(s) for s in ("s_ready", "s_max", "p_ready", "pT_ready", "pT_copied", "o_ready", "o_done"))
        var_ready, std_ready, ln_loaded, ln_used = (sem(s) for s in ("var_ready", "std_ready", "ln_loaded", "ln_used"))
        v_step, a_step, g_step, p_step = sem("v_step"), sem("a_step"), sem("g_step"), sem("p_step")
        setup_in, toep_out, toep_in, out_done = (sem(s) for s in ("setup_in", "toep_out", "toep_in", "out_done"))
        events = {}

        def ev(name):
            if name not in events:
                events[name] = sem("e_" + name)
            return events[name]

        class Chain:

            def __init__(self, eng, s):
                self.eng, self.s, self.n = eng, s, 0

            def __call__(self, ins):
                ins.then_inc(self.s, 1)
                self.n += 1
                self.eng.wait_ge(self.s, self.n)

        def col_unit(w, c0):
            return w[:, bass.ds(c0, UC)].rearrange("(k p) c -> p k c", p=P)

        def row_unit(w, r0):
            return w[bass.ds(r0, UC), :].rearrange("(k p) c -> p k c", p=P)

        ffn_w = {
            "ff0": (a["w_ffn_in"][0], 0, a["w_ffn_in"][0], FF, a["w_ffn_out"][0]),
            "ff1": (a["w_ffn_in"][1], 0, a["w_ffn_in"][1], FF, a["w_ffn_out"][1]),
        }
        for l, s in ((0, "a"), (1, "b")):
            for f in ("1", "2"):
                ffn_w[f"f{f}{s}"] = (a[f"ffn{f}_w_gate_2"][l], 0, a[f"ffn{f}_w_up_2"][l], 0, a[f"ffn{f}_w_down_2"][l])
        o_w = {"o_ab": a["w_o"][0], "o_cd": a["w_o"][1], "o_even": a["even_w_out_2"][0], "o_odd": a["odd_w_out_2"][0]}
        EVEN_COLS = [0, 256] + [512 + 256 * i for i in range(4)] + [1544, 1800]
        ODD_COLS = [256 * i for i in range(8)]

        toep = nc.dram_tensor("toep_scratch", [28, TOEP], F32, kind="Internal")

        def toep_tile(row, heads):
            return bass.AP(toep, row * TOEP, [[1, P], [TOEP, heads], [1, T]])

        HEADS = {
            "ab": [(h, 64 * m, 128 * h, 128, h, 128 * h) for h in range(4) for m in range(2)]
            + [(4 + b // 2, 64 * (b % 2), 512 + 64 * b, 64, 4 + b, 512 + 64 * b) for b in range(8)],
            "cd": [(h // 2, 64 * (h % 2), 64 * h, 64, h, 64 * h) for h in range(8)]
            + [(4 + h // 2, 64 * (h % 2), 512 + 64 * h, 64, None, 512 + 64 * h) for h in range(8)],
            "odd": [(h // 2, 64 * (h % 2), 64 * h, 64, h, 64 * h) for h in range(8)],
        }
        HEAD0 = {"ab": 0, "cd": 16, "odd": 32}
        FLIPS = {"ab": 6, "cd": 4, "odd": 4}
        FLIP0 = {"ab": 0, "cd": 6, "odd": 10}

        ones_col = ones[:, 0:1]
        mx = carve(small, 0, 3, 2)
        sums = carve(small, 8, 4, 2)
        rs = carve(small, 16, 4, 2)
        stat = carve(small, 24, 2, 16)
        mv = carve(small, 56, 2, 2)
        std = carve(small, 60, 2)
        rstd = carve(small, 62, 2)
        lam = carve(small, 64, 8)
        hstat = carve(small, 72, 2, 16)
        hstd = carve(small, 104, 2, 16)
        eps_ln = small[:, 136:137]
        eps_rms = small[:, 137:138]
        neg_lam = small[:, 138:139]
        ccol = carve(small, 140, 2, 16)
        a8 = small[0:8, 172:175]
        dsk = carve(small, 176, 8)
        lamrow = small[0:1, 192:448]
        xss = carve(small, 448, 2)

        SET = 6144
        rows = mix[0:NCOL, SET:SET + P]
        rowC = mix[0:48, SET + 128:SET + 256]
        onehot = mix[0:NUM_BUCKETS, SET + 256:SET + 640]
        addc = mix[0:20, SET + 640:SET + 1024]
        table = mix[0:NUM_BUCKETS, SET + 1024:SET + 1044]
        relrow = mix[0:8, SET + 1044:SET + 1301]
        toepA = mix[0:20, SET + 1304:SET + 1688]
        toepE = mix[0:8, SET + 1688:SET + 2072]
        dt2 = mix[32:48, SET + 2072:SET + 2074]
        SETUP_LOADS, ROW_LOADS = 16, 17

        zn = carve(mix, 0, TT, 512)
        xpad = carve(mix, 1024, 8, 259)
        xbcT = carve(mix, 3096, 8, T)
        uT = carve(mix, 5144, 4, T)
        xsn = carve(mix, 6168, TT, 512)
        xdt = carve(mix, 7192, TT, 512)
        G = carve(mix, 8216, 2, 384)
        W = carve(mix, 8984, 2, 384)
        cumT = mix[0:8, 9752:10008]
        dtT = mix[0:8, 10008:10264]
        sp8 = [xsn[0:8, i, 0:T] for i in range(2)] + [xdt[0:8, i, 0:T] for i in range(2)]
        BP = carve(mix, 8216, 2, 16, 32)
        Cpad = carve(mix, 9240, 2, 4, P)
        RB = carve(late, 8192, 2, 4, P)
        CT = carve(late, 9216, 2, 4, P)
        cosT = carve(late, 0, 16, T)
        sinT = carve(late, 4096, 16, T)
        s5w = [carve(mix, 2560 * i, 5, 512) for i in range(2)]
        yT = carve(mix, 6168, 4, T)
        gl = carve(mix, 7192, 4, T)
        wglu = carve(mix, 8216, 4, 512)
        bbin = carve(mix, 2048, 2, 16, 16)
        bbt = carve(mix, 2560, 2, 16, 16)
        tabt = carve(mix, 3072, 2, 16, P)
        qn, kn = carve(mix, 1024, TT, 512), carve(mix, 3072, TT, 512)
        uTo = carve(mix, 8192, 4, T)
        pool_s = [carve(late, 1024 * i, 4, T) for i in range(3)]
        wpool = carve(late, 3072, 4, P)
        sig = carve(mix, 0, 4, T)

        def head_bcast(h):
            return ident[0:8, h:h + 1].to_broadcast([8, P])


        TRD, n_groups = {}, 0
        for name in TR:
            TRD[name] = n_groups
            n_groups += 2 if name in ("o_even", "o_odd") else 4
        LN_TR = {0: TR["ff0"], 1: TR["cd"], 2: TR["ff1"]}
        F8 = [late[0:8, 5632 + T * i:5632 + T * i + T] for i in range(4)]
        sq8 = carve(late, 5632, TT, 512)
        rows_c = mix[0:8, SET + 2080:SET + 2208]

        def even_pe(pe, mm, transposed, attention):
            u0 = PROJ["even"]
            pe.wait_ge(proj_evac, u0 + 8 + EVAC0)
            pe.wait_ge(ev("dt_cum"), 1)
            for tt in range(TT):
                for i, src in enumerate((cumT, dtT)):
                    at = 16 * tt + 8 * i
                    last = pe.transpose(bank[2][:, at:at + 8], src[:, tt * P:tt * P + P], ident[0:8, 0:8])
            last.then_inc(ev("dtc_tr"), 1)
            pe.wait_ge(ev("xbc_silu"), 4)
            for tt in range(TT):
                for c in range(4):
                    last = pe.transpose(bank[tt][:, c * P:c * P + P], xbcT[:, c, tt * P:tt * P + P], ident[:])
            last.then_inc(ev("xs_tr"), 1)
            for g in range(2):
                B, C = xbcT[:, 4 + g, :], xbcT[:, 6 + g, :]
                mm(bank[3 + g][:, 0:T], B[:, 0:P], C, start=True, stop=True)
                mm(bank[3 + g][:, T:T + P], B[:, P:T], C[:, P:T], start=True, stop=True).then_inc(ev("g_mm"), 1)
            pe.wait_ge(ev("xsn_ready"), 1)
            for s in range(9):
                if s < 8:
                    if s >= 2:
                        pe.wait_ge(ev("arg_done"), s - 1)
                    mm(bank[5 + s % 2][:, 0:T], head_bcast(s), cumT, start=True, stop=True).then_inc(ev("bc_ready"), 1)
                if s >= 1:
                    h = s - 1
                    pe.wait_ge(ev("w_done"), h + 1)
                    w, c = W[:, h % 2, :], slice(HD * h, HD * h + HD)
                    mm(bank[0][:, c], w[:, 0:P], xdt[:, 0, c], start=True, stop=True)
                    mm(bank[1][:, c], w[:, P:2 * P], xdt[:, 0, c], start=True, stop=False)
                    mm(bank[1][:, c], w[:, 2 * P:3 * P], xdt[:, 1, c], start=False, stop=True).then_inc(ev("y_mm"), 1)
            transposed("o_even", nat, 4)

            def drive(i):
                if i >= 2:
                    pe.wait_ge(ev("s5_prod"), i - 1)
                m, j = i // 4, 32 * (i % 4)
                for ri in range(2):
                    last = mm(bank[6 + i % 2][:, T * ri:T * ri + T], RB[j:j + 32, ri, m, :], uT[j:j + 32, m, :],
                              start=True, stop=True)
                last.then_inc(ev("s5_drive"), 1)

            drive(0)
            for i in range(16):
                if i < 15:
                    drive(i + 1)
                m, j = i // 4, 32 * (i % 4)
                pe.wait_ge(ev("s5_prod"), i + 1)
                if m >= 2 and j == 0:
                    pe.wait_ge(ev("s5_y"), m - 1)
                pc, ps = s5w[i % 2][:, 3, :], s5w[i % 2][:, 4, :]
                for n, (ri, z) in enumerate(((0, pc[:, 0:T]), (0, ps[:, T:2 * T]), (1, ps[:, 0:T]), (1, pc[:, T:2 * T]))):
                    last = mm(bank[2 + m % 2][j:j + 32, 0:T], CT[:, ri, m, j:j + 32], z, start=(n == 0), stop=(n == 3))
                last.then_inc(ev("s5_used"), 1)
            pe.wait_ge(ev("gelu_done"), 4)
            pe.wait_ge(ev("glu_in"), 16)
            for o in range(4):
                if o >= 2:
                    pe.wait_ge(ev("sig_done"), o - 1)
                for k in range(4):
                    last = mm(bank[o % 2][:, 0:T], wglu[:, k, o * P:o * P + P], gl[:, k, :], start=(k == 0), stop=(k == 3))
                last.then_inc(ev("glu_mm"), 1)

        def even_act(act_e, A, upper_part):
            for k in range(4):
                act_e.wait_ge(ev("conv_done"), k + 1)
                xs = xbcT[:, 2 * k:2 * k + 2, :]
                A(xs, xs, ACT.Silu).then_inc(ev("xbc_silu"), 1)
            A(zn, zn, ACT.Silu).then_inc(ev("z_silu"), 1)
            act_e.wait_ge(ev("dtc_ready"), 1)
            act_e.wait_ge(ev("xs_tr"), 1)
            A(xsn[:, 0, :], bank[0][:], ACT.Copy)
            A(xsn[:, 1, :], bank[1][:], ACT.Copy).then_inc(ev("xsn_ready"), 1)
            act_e.wait_ge(ev("g_mm"), 2)
            A(G[:, 0, :], bank[3][:, 0:384], ACT.Copy)
            A(G[:, 1, :], bank[4][:, 0:384], ACT.Copy).then_inc(ev("g_ready"), 1)
            for h in range(8):
                act_e.wait_ge(ev("arg_done"), h + 1)
                A(W[:, h % 2, :], W[:, h % 2, :], ACT.Exp).then_inc(ev("dec_done"), 1)
            act_e.wait_ge(ev("ssd_var"), 1)
            A(hstd[:, 0, 0:4], hstat[:, 0, 0:4], ACT.Sqrt, bias=eps_rms, scale=1.0 / 256).then_inc(ev("ssd_std"), 1)
            upper_part("o_even", 0)
            upper_part("o_even", 1)
            for m in range(4):
                act_e.wait_ge(ev("s5_y"), m + 1)
                A(gl[:, m, :], yT[:, m, :], ACT.Gelu_apprx_tanh).then_inc(ev("gelu_done"), 1)
            for o in range(4):
                act_e.wait_ge(ev("glu_mm"), o + 1)
                A(sig[:, o, :], bank[o % 2][:, 0:T], ACT.Sigmoid, bias=cols[:, C_GLUB + o:C_GLUB + o + 1])\
                    .then_inc(ev("sig_done"), 1)
            upper_part("o_even", 2)
            upper_part("o_even", 3)

        def even_dve(dve, step, split_py, transposed, lower_part):
            TTn, TS, STT = dve.tensor_tensor, dve.tensor_scalar, dve.scalar_tensor_tensor
            u0, n0 = PROJ["even"], START["even"]
            dve.wait_ge(ev("dt_mm"), 1)
            step(TS(sp8[1], bank[7][0:8, 0:T], a8[:, 1:2], None, ALU.add))
            STT(sp8[0], sp8[1], -1.0, sp8[1], ALU.mult, ALU.min).then_inc(ev("dt_abs"), 1)
            dve.wait_ge(ev("dt_ln"), 1)
            step(STT(dtT, sp8[1], 0.0, sp8[0], ALU.max, ALU.add))
            step(TS(sp8[2], dtT, small[0:8, 175:176], -1.0, ALU.mult, ALU.mult))
            dve.tensor_tensor_scan(cumT, ones[0:8, 0:1].to_broadcast([8, T]), sp8[2], 0.0, ALU.mult, ALU.add)\
                .then_inc(ev("dt_cum"), 1)
            step(dve.memset(xpad[:, :, 0:3], 0.0))

            def conv(u):
                dve.wait_ge(proj_evac, u0 + u + 1 + EVAC0)
                for tap in range(4):
                    for c in (2 * u - 4, 2 * u - 3):
                        w = cols[:, C_CONVW + 8 * tap + c:C_CONVW + 8 * tap + c + 1]
                        src = xpad[:, c, tap:tap + T]
                        if tap == 0:
                            last = TS(xbcT[:, c, :], src, w, cols[:, C_CONVB + c:C_CONVB + c + 1], ALU.mult, ALU.add)
                        else:
                            last = STT(xbcT[:, c, :], src, w, xbcT[:, c, :], ALU.mult, ALU.add)
                    if tap < 3:
                        step(last)
                last.then_inc(ev("conv_done"), 1)

            for u in range(8):
                split_py(n0 + u + RING)
                if 3 <= u <= 6:
                    conv(u - 1)
            dve.wait_ge(ev("dtc_tr"), 1)
            dve.tensor_copy(ccol, bank[2][:, 0:32].rearrange("p (a n) -> p a n", a=TT)).then_inc(ev("dtc_ready"), 1)
            dve.wait_ge(ev("dtc_ready"), 1)
            dve.wait_ge(ev("xsn_ready"), 1)
            for tt in range(TT):
                step(TTn(xdt[:, tt, :].rearrange("p (h d) -> p h d", d=HD), xsn[:, tt, :].rearrange("p (h d) -> p h d", d=HD),
                         ccol[:, tt, 8:16].unsqueeze(2).to_broadcast([P, 8, HD]), ALU.mult))
            dve.wait_ge(ev("g_ready"), 1)
            for s in range(9):
                if s < 8:
                    dve.wait_ge(ev("bc_ready"), s + 1)
                    if s >= 2:
                        dve.wait_ge(ev("y_mm"), s - 1)
                    w, bc = W[:, s % 2, :], bank[5 + s % 2]
                    c0, c1 = ccol[:, 0, s:s + 1], ccol[:, 1, s:s + 1]
                    STT(w[:, 0:P], upper[:], c0, bc[:, 0:P], ALU.subtract, ALU.add)
                    TS(w[:, P:2 * P], bc[:, P:T], c0, None, ALU.subtract)
                    STT(w[:, 2 * P:3 * P], upper[:], c1, bc[:, P:T], ALU.subtract, ALU.add).then_inc(ev("arg_done"), 1)
                if s >= 1:
                    h = s - 1
                    dve.wait_ge(ev("dec_done"), h + 1)
                    TTn(W[:, h % 2, :], W[:, h % 2, :], G[:, h // 4, :], ALU.mult).then_inc(ev("w_done"), 1)
            dve.wait_ge(ev("y_mm"), 8)
            dve.wait_ge(ev("z_silu"), 1)
            for tt in range(TT):
                y = nat[:, tt, 0:512]
                heads = lambda z: z.rearrange("p (h d) -> p h d", d=HD)
                step(TTn(heads(y), heads(xsn[:, tt, :]), dsk.unsqueeze(2).to_broadcast([P, 8, HD]), ALU.mult))
                step(TTn(y, y, bank[tt][:], ALU.add))
                step(TTn(y, y, zn[:, tt, :], ALU.mult))
                step(TTn(xdt[:, tt, :], y, y, ALU.mult))
            dve.reduce_sum(hstat[:, 0, 0:4], xdt.rearrange("p a (g d) -> p (a g) d", g=2), AX.X).then_inc(ev("ssd_var"), 1)
            dve.wait_ge(ev("ssd_std"), 1)
            step(dve.reciprocal(hstd[:, 1, 0:4], hstd[:, 0, 0:4]))
            for tt in range(TT):
                y = nat[:, tt, 0:512].rearrange("p (g d) -> p g d", g=2)
                TTn(y, y, hstd[:, 1, 2 * tt:2 * tt + 2].unsqueeze(2).to_broadcast([P, 2, 256]), ALU.mult).then_inc(nat_ready, 1)
            dve.wait_ge(nat_ready, 2 * TR["o_even"] + 2)
            dve.sem_inc(ev("ssd_done"), 1)
            transposed("o_even", lambda c: cols[:, C_SSDN + c:C_SSDN + c + 1], groups=2)

            def s5_out(m):
                dve.wait_ge(ev("s5_used"), 4 * m + 4)
                STT(yT[:, m, :], uT[:, m, :], cols[:, C_S5D + m:C_S5D + m + 1], bank[2 + m % 2][:, 0:T], ALU.mult, ALU.add)\
                    .then_inc(ev("s5_y"), 1)

            for i in range(16):
                a_, b_, g_, pc, ps = (s5w[i % 2][:, n, :] for n in range(5))
                two = lambda z: z.rearrange("p (r t) -> p r t", r=2)
                C2 = cosT[:, i, :].unsqueeze(1).to_broadcast([P, 2, T])
                S1, d = sinT[:, i, :], bank[6 + i % 2]
                lo, hi = slice(0, T), slice(T, 2 * T)
                dve.wait_ge(ev("s5_drive"), i + 1)
                if i >= 2:
                    dve.wait_ge(ev("s5_used"), i - 1)
                TTn(two(a_), two(d[:]), C2, ALU.mult)
                TTn(b_[:, lo], d[:, hi], S1, ALU.mult)
                step(STT(b_[:, hi], d[:, lo], -1.0, S1, ALU.mult, ALU.mult))
                step(TTn(a_, a_, b_, ALU.add))
                mag = s5c[:, 4, i:i + 1].to_broadcast([P, T])
                dve.tensor_tensor_scan(g_[:, lo], mag, a_[:, lo], 0.0, ALU.mult, ALU.add)
                step(dve.tensor_tensor_scan(g_[:, hi], mag, a_[:, hi], 0.0, ALU.mult, ALU.add))
                TTn(two(pc), two(g_), C2, ALU.mult)
                TTn(ps[:, lo], g_[:, lo], S1, ALU.mult)
                STT(ps[:, hi], g_[:, hi], -1.0, S1, ALU.mult, ALU.mult).then_inc(ev("s5_prod"), 1)
                if i % 4 == 0 and i:
                    s5_out(i // 4 - 1)
            s5_out(3)
            for o in range(4):
                dve.wait_ge(ev("sig_done"), o + 1)
                last = TTn(t32[:, 4 + o, :], yT[:, o, :], sig[:, o, :], ALU.mult)
                if o % 2:
                    last.then_inc(t32_ready, 1)
            for g in (2, 3):
                lower_part(TR["o_even"], g)

        def odd_pe(pe, mm, transposed, attention):
            pe.wait_ge(proj_evac, PROJ["odd"] + 8 + EVAC0)
            for i, src in enumerate((qn, kn)):
                pe.wait_ge(ev("qk_norm"), i + 1)
                for c in range(4):
                    b = bank[2 * i + c // 2]
                    for tt in range(TT):
                        at = (c % 2) * T + tt * P
                        last = pe.transpose(b[:, at:at + P], src[:, tt, c * P:c * P + P], ident[:])
                last.then_inc(ev("qk_tr"), 1)
            pe.wait_ge(ev("q_done"), 1)
            pe.wait_ge(ev("k_done"), 1)
            attention("odd")
            transposed("o_odd", nat, 4)
            pe.wait_ge(ev("pool_in"), 16)
            pe.wait_ge(ev("pooled"), 4)
            for g in range(4):
                last = mm(bank[6 + g // 2][:, (g % 2) * T:(g % 2) * T + T], wpool[:, g, :], pooled[g], start=True, stop=True)
            last.then_inc(ev("pool_mm"), 1)

        def odd_act(act_e, A, upper_part, attention):
            act_e.wait_ge(ev("qk_var"), 1)
            A(hstd[:], hstat[:], ACT.Sqrt, bias=eps_rms, scale=1.0 / HD).then_inc(ev("qk_std"), 1)
            act_e.wait_ge(ev("qk_tr"), 1)
            for b in range(2):
                last = A(qT[:, 2 * b:2 * b + 2, :], bank[b][:].rearrange("p (c t) -> p c t", c=2), ACT.Copy,
                         scale=cols[:, C_QN:C_QN + 1])
            last.then_inc(ev("q_done"), 1)
            attention("odd")
            upper_part("o_odd", 0)
            upper_part("o_odd", 1)
            act_e.wait_ge(ev("pool_mm"), 1)
            for g in range(4):
                last = A(t32[:, 4 + g, :], bank[6 + g // 2][:, (g % 2) * T:(g % 2) * T + T], ACT.Copy,
                         scale=cols[:, C_PSCALE + g:C_PSCALE + g + 1])
                if g % 2:
                    last.then_inc(t32_ready, 1)
            upper_part("o_odd", 2)
            upper_part("o_odd", 3)

        def odd_dve(dve, step, split_py, transposed, lower_part, attention):
            TTn, TS = dve.tensor_tensor, dve.tensor_scalar
            for u in range(8):
                split_py(START["odd"] + u + RING)
            dve.wait_ge(proj_evac, PROJ["odd"] + 4 + EVAC0)
            for i, z in enumerate((qn, kn)):
                step(TTn(sq8, z, z, ALU.mult))
                last = dve.reduce_sum(hstat[:, i, :], sq8.rearrange("p a (h d) -> p (a h) d", d=HD), AX.X)
                if i == 0:
                    step(last)
            last.then_inc(ev("qk_var"), 1)
            dve.wait_ge(ev("qk_std"), 1)
            step(dve.reciprocal(hstat[:], hstd[:]))
            for i, z in enumerate((qn, kn)):
                zh = z.rearrange("p a (h d) -> p (a h) d", d=HD)
                TTn(zh, zh, hstat[:, i, :].unsqueeze(2).to_broadcast([P, 16, HD]), ALU.mult).then_inc(ev("qk_norm"), 1)
            dve.wait_ge(ev("qk_tr"), 2)
            for b in range(2):
                last = TS(kT[:, 2 * b:2 * b + 2, :], bank[2 + b][:].rearrange("p (c t) -> p c t", c=2),
                          cols[:, C_KN:C_KN + 1], None, ALU.mult)
            last.then_inc(ev("k_done"), 1)
            dve.wait_ge(ev("band_mask"), 1)
            attention("odd")
            dve.wait_ge(o_done, HEAD0["odd"] + len(HEADS["odd"]))
            dve.sem_inc(nat_ready, 2)
            transposed("o_odd", groups=2)
            for g in (2, 3):
                lower_part(TR["o_odd"], g)

        POOL_WINDOWS = (2, 4, 8, 16)
        pooled = [pool_s[0][:, 0, :], pool_s[1][:, 1, :], pool_s[2][:, 2, :], pool_s[0][:, 3, :]]

        def pooling(pool, step):
            pool.wait_ge(proj_evac, PROJ["odd"] + 8 + EVAC0)
            src, at = uTo, 0
            for n, dst in enumerate((pool_s[0], pool_s[1], pool_s[2], pool_s[0])):
                k = 1 << n
                step(pool.tensor_copy(dst[:, n:4, 0:k], src[:, n:4, 0:k]))
                step(pool.tensor_tensor(dst[:, n:4, k:T], src[:, n:4, k:T], src[:, n:4, 0:T - k], ALU.add))
                src = dst
            for g, (w, z) in enumerate(zip(POOL_WINDOWS, pooled)):
                step(pool.tensor_scalar(z[:, 16:T], z[:, 16:T], 1.0 / w, None, ALU.mult))
                step(pool.tensor_tensor(z[:, 0:16], z[:, 0:16], poolc[:, 16 * g:16 * g + 16], ALU.mult))
                pool.tensor_tensor(z, z, uTo[:, g, :], ALU.subtract).then_inc(ev("pooled"), 1)

        block = ctx.enter_context(nc.Block())

        @block.sync
        def _(sp):
            def unit(slot, n, src):
                sp.wait_ge(lo_ready, n + (LO0 - RING + 1))
                sp.dma_start(raw[:, slot, :].rearrange("p (k c) -> p k c", k=src.shape[1]), src)\
                    .then_inc(raw_full[slot], 16)

            def qkv(name, w):
                n0 = START[name]
                with sp.Fori(0, 2) as m:
                    with sp.Fori(0, 2) as j:
                        it = m * 2 + j
                        for u in range(3):
                            unit((n0 + u) % RING, it * 3 + (n0 + u),
                                 col_unit(w, m * 1536 + j * 256 + 512 * u))

            def straight(name, units):
                for u, src in enumerate(units):
                    n = START[name] + u
                    unit(n % RING, n, src)

            def ffn(name):
                wg, g0, wu, u0, wd = ffn_w[name]
                n0 = START[name]
                unit(n0 % RING, n0, col_unit(wg, g0))
                unit((n0 + 1) % RING, n0 + 1, col_unit(wu, u0))

                def body(i):
                    n = i * 3 + (n0 - 1)
                    unit((n0 + 2) % RING, n, col_unit(wg, i * UC + g0))
                    unit((n0 + 3) % RING, n + 1, row_unit(wd, i * UC - UC))
                    unit((n0 + 4) % RING, n + 2, col_unit(wu, i * UC + u0))

                with sp.Fori(1, FC) as i:
                    body(i)
                n = n0 + 32
                unit(n % RING, n, row_unit(wd, FF - UC))

            sp.dma_start(x[:], a["x"][0].rearrange("(a p) d -> p a d", p=P)).then_inc(ev("x_in"), 16)
            qkv("ab", a["w_in_ab"][0])
            straight("o_ab", [row_unit(o_w["o_ab"], UC * u) for u in range(4)])
            ffn("ff0")
            qkv("cd", a["w_in_cd"][0])
            straight("o_cd", [row_unit(o_w["o_cd"], UC * u) for u in range(4)])
            ffn("ff1")
            ffn("f1a")
            straight("even", [col_unit(a["even_w_in_2"][0], c) for c in EVEN_COLS])
            straight("o_even", [row_unit(o_w["o_even"], UC * u) for u in range(4)])
            ffn("f2a")
            ffn("f1b")
            straight("odd", [col_unit(a["odd_w_in_2"][0], c) for c in ODD_COLS])
            straight("o_odd", [row_unit(o_w["o_odd"], UC * u) for u in range(4)])
            ffn("f2b")
            sp.wait_ge(ev("x_final"), 2)
            sp.dma_start(out[0].rearrange("(a p) d -> p a d", p=P), x[:]).then_inc(out_done, 16)
            sp.wait_ge(out_done, 16)

        @block.gpsimd
        def _(pool):
            step = Chain(pool, g_step)

            def load(dst, src, s=setup_in):
                pool.dma_start(dst, src).then_inc(s, 16)

            def ada(l, slot, c0, used):
                if used is not None:
                    pool.wait_ge(ada_step[slot], used)
                pool.dma_start(ada_b[0:1, slot, :], a["b_ada"][l:l + 1, bass.ds(c0, 512)]).then_inc(ada_full[slot], 16)
                pool.dma_start(ada_raw[:, slot, :].rearrange("p (k c) -> p k c", k=KC),
                               a["w_ada"][l][:, bass.ds(c0, 512)].rearrange("(k p) c -> p k c", p=P))\
                    .then_inc(ada_full[slot], 16)

            pool.wait_ge(ev("ada_b_zero"), 1)
            for b in range(2):
                ada(0, b, b * 512, None)
            load(flip[:], a["k_flip"])
            load(lower[:], a["k_lower"])
            load(upper[:], a["k_upper"])
            load(onehot, a["k_onehot"])
            load(addc, a["k_add"])
            load(table[:, 0:12], a["rel_bias"])
            load(table[:, 12:20], a["rel_bias"][:, 0:8])
            load(relrow, a["attn_rel_bias_2"][0])
            load(lamrow, a["diff_lambda"].rearrange("o a d -> o (a d)"))
            load(a8[:, 0:1], a["forget_b"].rearrange("o h -> h o"))
            load(a8[:, 1:2], a["ssd_dt_bias_2"].rearrange("o h -> h o"))
            load(a8[:, 2:3], a["ssd_a_log_2"].rearrange("o h -> h o"))
            load(dsk, a["ssd_d_2"].to_broadcast([P, 8]))
            load(poolc[:], a["k_pool"].to_broadcast([P, 64]))
            load(wsmall[:, 0], a["w_in_cd"][0][:, 3072:3080].rearrange("(k p) c -> p k c", p=P))
            load(wsmall[:, 1], a["even_w_in_2"][0][:, 1536:1544].rearrange("(k p) c -> p k c", p=P))
            for b in range(2):
                ada(0, b, b * 512 + 1024, 8)
            pool.wait_ge(ev("toep_rows"), 2)
            pool.dma_start(toep.ap()[0:20, :], toepA).then_inc(toep_out, 16)
            pool.dma_start(toep.ap()[20:28, :], toepE).then_inc(toep_out, 16)
            pool.wait_ge(toep_out, 32)
            pool.wait_ge(ev("cols_ready"), 2)
            pool.dma_start(bias[:, 0:12, :], toep_tile(0, 12)).then_inc(toep_in, 16)
            with pool.Fori(0, 2) as m:
                with pool.Fori(0, 2) as j:
                    it = m * 2 + j
                    ada(0, 0, m * 3072 + j * 512 + 2048, it * 8 + 16)
                    ada(0, 1, it * 512 + 3072, it * 8 + 16)

            def load_ln(l, n):
                pool.dma_start(lnv[:, 0, :], a["ln_g"][l, n:n + 1, :].to_broadcast([P, D])).then_inc(ln_loaded, 16)
                pool.dma_start(lnv[:, 1, :], a["ln_b"][l, n:n + 1, :].to_broadcast([P, D])).then_inc(ln_loaded, 16)

            for l in range(2):
                pool.wait_ge(nat_ready, 2 * TR[("o_ab", "o_cd")[l]] + 2)
                load_ln(l, 0)
                if l == 0:
                    pool.dma_start(bias[:, 0:8, :], toep_tile(12, 8)).then_inc(toep_in, 16)
                    with pool.Fori(0, 2) as m:
                        with pool.Fori(0, 4) as j:
                            ada(1, 1, m * 3072 + j * 512, (m * 4 + j) * 8 + 48)
                pool.wait_ge(ln_used, 2 * l + 1)
                load_ln(l, 1)
                if l == 0:
                    with pool.Fori(0, 2) as m:
                        with pool.Fori(0, 2) as j:
                            ada(1, 0, m * 3072 + j * 512 + 2048, (m * 2 + j) * 8 + 48)

            pool.wait_ge(nat_ready, 2 * TR["f1a"] + 2)
            load(bbin[:, 0], a["s5_b_re_2"][0].rearrange("(n g) p i -> (g p) n i", g=2), ev("s5_in"))
            load(bbin[:, 1], a["s5_b_im_2"][0].rearrange("(n g) p i -> (g p) n i", g=2), ev("s5_in"))
            pool.memset(Cpad[:], 0.0).then_inc(ev("cpad_zero"), 1)
            step(pool.memset(BP[:], 0.0))
            pool.wait_ge(ev("cpad_zero"), 1)
            for ri, c in enumerate(("s5_c_re_2", "s5_c_im_2")):
                for g in range(8):
                    load(Cpad[16 * g:16 * g + 16, ri, :, 64 * (g % 2):64 * (g % 2) + 64],
                         a[c][0].rearrange("(m g) i p -> g i m p", g=8)[g], ev("s5_in"))
            step(pool.memset(cosT[:, :, 0:1], 1.0))
            step(pool.memset(sinT[:, :, 0:1], 0.0))
            step(pool.tensor_copy(cosT[:, :, 1:2], s5c[:, 0, :].unsqueeze(2)))
            step(pool.tensor_copy(sinT[:, :, 1:2], s5c[:, 1, :].unsqueeze(2)))
            k = 1
            while k < T // 2:
                def times(dst, lo, hi, n):
                    c1, s1 = cosT[:, :, lo:lo + n], sinT[:, :, lo:lo + n]
                    ck, sk = (t[:, :, hi:hi + 1].to_broadcast([P, 16, n]) for t in (cosT, sinT))
                    p0, p1 = tabt[:, 0, :, 0:n], tabt[:, 1, :, 0:n]
                    step(pool.tensor_tensor(p0, c1, ck, ALU.mult))
                    step(pool.tensor_tensor(p1, s1, sk, ALU.mult))
                    step(pool.tensor_tensor(cosT[:, :, dst:dst + n], p0, p1, ALU.subtract))
                    step(pool.tensor_tensor(p0, c1, sk, ALU.mult))
                    step(pool.tensor_tensor(p1, s1, ck, ALU.mult))
                    step(pool.tensor_tensor(sinT[:, :, dst:dst + n], p0, p1, ALU.add))

                times(2 * k, k, k, 1)
                times(2 * k + 1, 1, 2 * k, 2 * k - 1)
                k *= 2
            pool.wait_ge(ev("s5_in"), 16 * 18)
            fr, fi = (s5c[:, n, :].unsqueeze(2).to_broadcast([P, 16, 16]) for n in (2, 3))
            br, bi = bbin[:, 0], bbin[:, 1]
            for ri, (one, two, op) in enumerate(((br, bi, ALU.subtract), (bi, br, ALU.add))):
                step(pool.tensor_tensor(bbt[:, 0], one, fr, ALU.mult))
                step(pool.tensor_tensor(bbt[:, 1], two, fi, ALU.mult))
                for g in range(2):
                    rows_g = slice(64 * g, 64 * g + 64)
                    last = pool.tensor_tensor(BP[rows_g, ri, :, 16 * g:16 * g + 16], bbt[rows_g, 0], bbt[rows_g, 1], op)
                    if g == 0 or ri == 0:
                        step(last)
            last.then_inc(ev("bp_ready"), 1)
            pool.wait_ge(ev("ssd_done"), 1)
            load(wglu, a["s5_w_glu_2"][0].rearrange("(k p) n -> p k n", p=P), ev("glu_in"))
            pool.wait_ge(nat_ready, 2 * TR["f2a"] + 2)
            pool.dma_start(bias[:, 0:8, :], toep_tile(20, 8)).then_inc(toep_in, 16)
            load(wpool, a["pool_w_2"][0].rearrange("g i o -> i g o"), ev("pool_in"))
            pool.wait_ge(flip_out, FLIP0["odd"] + 4)
            pool.memset(bias[0:64, 0:8, 192:256], NEG).then_inc(ev("band_mask"), 1)
            pooling(pool, step)

        @block.scalar
        def _(act_e):
            step = Chain(act_e, a_step)
            A = act_e.activation

            def split(slot, n, turn):
                if isinstance(n, int) and n >= UNITS:
                    return
                act_e.wait_ge(raw_full[slot], turn * 16)
                act_e.wait_ge(unit_used, n + (USED0 - RING + 1))
                A(wH[:, slot, :], raw[:, slot, :], ACT.Copy).then_inc(hi_ready, 1)

            def split_py(n):
                split(n % RING, n, n // RING + 1)

            def ada_evac(slot, cnt, gdst=None, cdst=None, b=None):
                act_e.wait_ge(ada_mm[slot], cnt + 2)
                if gdst is not None:
                    A(gdst, bank[7][:], ACT.Copy, bias=1.0).then_inc(ada_out[slot], 1)
                else:
                    A(cdst, bank[b or (7, 3)[slot]][:, 0:4], ACT.Copy).then_inc(ada_out[slot], 1)

            def upper_part(name, g):
                act_e.wait_ge(t32_ready, 4 * TR[name] + g + 1)
                A(hH[:, 2 * g:2 * g + 2, :], t32[:, 2 * g:2 * g + 2, :], ACT.Copy).then_inc(th_ready, 1)

            def transposed(name):
                for g in range(4):
                    upper_part(name, g)

            def qkv(name, l):
                n0, u0 = START[name], PROJ[name]
                with act_e.Fori(0, 2) as m:
                    with act_e.Fori(0, 2) as j:
                        it = m * 2 + j
                        for u in range(3):
                            n = n0 + u
                            act_e.wait_ge(unit_used, it * 3 + (n + USED0 + 1))
                            src = bank[4 + u][:].rearrange("p (a t) -> p a t", a=2)
                            if u == 0:
                                A(qT[:, bass.ds(it * 2, 2), :], src, ACT.Copy, scale=ATTN_SCALE).then_inc(proj_evac, 1)
                            elif u == 1:
                                A(kT[:, bass.ds(it * 2, 2), :], src, ACT.Copy).then_inc(proj_evac, 1)
                            else:
                                A(v[:, :, bass.ds(it * UC, UC)], src, ACT.Copy).then_inc(proj_evac, 1)
                            split(n % RING, it * 3 + (n + RING), it + ((n + RING) // RING + 1))
                        g1 = gate1[:, bass.ds(m, 1), bass.ds(j * 512, 512)]
                        if l == 0:
                            ada_evac(0, it + 2, gdst=g1)
                            ada_evac(1, it + 2, cdst=adaC[:, 0, bass.ds(it * 4 + 16, 4)])
                        else:
                            ada_evac(0, it + 6, gdst=g1)

            def flipped(name):
                for n in range(FLIPS[name]):
                    act_e.wait_ge(flip_mm, FLIP0[name] + n + 1)
                    A(bias[:, 2 * n:2 * n + 2, :], bank[4 + n % 3][:].rearrange("p (h t) -> p h t", h=2), ACT.Copy)\
                        .then_inc(flip_out, 1)

            def attention(name):
                g0, heads = HEAD0[name], HEADS[name]

                def probs(g):
                    act_e.wait_ge(s_max, g + 1)
                    for tt, (lo, hi) in enumerate(((0, 128), (128, 384))):
                        last = A(sP[:, g % 3, lo:hi], sP[:, g % 3, lo:hi], ACT.Exp, scale=-1.0,
                                 bias=mx[:, g % 3, tt:tt + 1], accum_out=sums[:, g % 4, tt:tt + 1])
                    last.then_inc(p_ready, 1)

                def copy_pT(g):
                    act_e.wait_ge(pT_ready, g + 1)
                    if g >= 2:
                        act_e.wait_ge(o_ready, g - 1)
                    A(PT[:, g % 2, :], bank[3 + g % 2][:, 0:384], ACT.Copy).then_inc(pT_copied, 1)

                for s in range(len(heads) + 2):
                    if s < len(heads):
                        probs(g0 + s)
                    if s >= 2:
                        copy_pT(g0 + s - 2)

            def ffn(name, with_ada=False):
                n0, f = START[name], 11 * FFN[name]

                def hidden(i):
                    act_e.wait_ge(act_mul, i + (f + 1))
                    A(aH[:], act.rearrange("p (a t) -> p a t", a=2), ACT.Copy).then_inc(act_hi, 1)

                def silu(i):
                    act_e.wait_ge(act_mul, i + f) if not (isinstance(i, int) and i + f == 0) else None
                    A(sil, bank[4][:], ACT.Silu).then_inc(sil_done, 1)

                act_e.wait_ge(unit_used, n0 + USED0 + 1)
                silu(0)
                split_py(n0 + 3)
                act_e.wait_ge(unit_used, n0 + USED0 + 2)
                hidden(0)
                split_py(n0 + 4)

                def body(i):
                    n = i * 3 + (n0 - 1)
                    s, turn = n0 + 2, i + ((n0 + 2) // RING + 1)
                    act_e.wait_ge(unit_used, n + (USED0 + 1))
                    silu(i)
                    split((s + 3) % RING, n + 3, i + ((n0 + 5) // RING))
                    split((s + 4) % RING, n + 4, i + ((n0 + 6) // RING))
                    hidden(i)
                    split((s + 5) % RING, n + 5, i + ((n0 + 7) // RING))

                if with_ada:
                    with act_e.Fori(0, 2) as m:
                        with act_e.Fori(0, 4) as j:
                            b = m * 4 + j
                            body(b + 1)
                            ada_evac(1, b + 6, cdst=adaC[:, 1, bass.ds(b * 4, 4)], b=7)
                with act_e.Fori(9 if with_ada else 1, FC - 1) as i:
                    body(i)
                body(FC - 1)
                split_py(n0 + 35)

            def root(e, scale, eps):
                for tt in range(TT):
                    act_e.wait_ge(var_ready, 2 * e + tt + 1)
                    src = mv[:, tt, 1:2] if scale is None else xss[:, tt:tt + 1]
                    A(std[:, tt:tt + 1], src, ACT.Sqrt, bias=eps, scale=scale or 1.0).then_inc(std_ready, 1)

            def load(dst, src):
                act_e.dma_start(dst, src).then_inc(ev("rows_in"), 16)

            act_e.dma_start(ident[:], a["k_ident"]).then_inc(ev("first_in"), 16)
            act_e.dma_start(rows_c, a["c"].rearrange("o (k p) -> (o k) p", p=P)).then_inc(ev("first_in"), 16)
            for at, src in ((C_FF1, a["ffn1_norm_2"]), (C_MIX, a["mix_norm_2"]), (C_FF2, a["ffn2_norm_2"]),
                            (C_CONVB, a["ssd_conv_b_2"]), (C_CONVW, a["ssd_conv_w_2"][0]), (C_SSDN, a["ssd_norm_2"]),
                            (C_GLUB, a["s5_b_glu_2"]), (C_PSCALE, a["pool_scale_2"]), (C_SUBLN, a["diff_subln_g"])):
                n = int(np.prod(src.shape)) // P
                load(rows[at:at + n, :], src.rearrange("a (k p) -> (a k) p", p=P))
            load(rows[C_S5D:C_S5D + 4, :], a["s5_d_2"][0].rearrange("(m g) i -> m (g i)", m=4))
            for at, src in ((C_QN, a["attn_q_norm_2"]), (C_KN, a["attn_k_norm_2"])):
                load(rows[at:at + 1, 0:HD], src)
                load(rows[at:at + 1, HD:P], src)
            load(rowC[0:16, :], a["s5_a_re_2"][0].rearrange("(n g) p -> n (g p)", g=2))
            load(rowC[16:32, :], a["s5_a_im_2"][0].rearrange("(n g) p -> n (g p)", g=2))
            load(dt2, a["s5_log_dt_2"][0].rearrange("(n g) -> n g", g=2))
            act_e.wait_ge(ev("c_cols"), 1)
            A(silc[:], bank[0][:, 0:8], ACT.Silu).then_inc(ev("silc"), 1)
            for b in range(4):
                ada_evac(b % 2, b // 2, cdst=adaC[:, 0, 4 * b:4 * b + 4])
            for n in range(RING):
                split_py(n)
            transposed("ab")
            act_e.wait_ge(ev("lam_sums"), 1)
            A(lam[0:1, 2:4], lam[0:1, 0:2], ACT.Exp).then_inc(ev("lam_exp"), 1)
            act_e.wait_ge(ev("cols_ready"), 2)
            step(A(s5c[:, 6, :], colC[:, 32:48], ACT.Exp))
            A(small[0:8, 175:176], a8[:, 2:3], ACT.Exp).then_inc(ev("s5_dt"), 1)
            act_e.wait_ge(ev("s5_angle"), 1)
            step(A(s5c[:, 4, :], s5c[:, 7, :], ACT.Exp))
            A(s5c[:, 9, :], s5c[:, 8, :], ACT.Sin, scale=0.5).then_inc(ev("s5_sin"), 1)
            A(s5c[:, 1, :], s5c[:, 8, :], ACT.Sin).then_inc(ev("s5_sin"), 1)

            flipped("ab")
            e = 0
            for l, (p, o, f) in enumerate((("ab", "o_ab", "ff0"), ("cd", "o_cd", "ff1"))):
                if l == 1:
                    transposed(p)
                    act_e.wait_ge(ev("fd_abs"), 1)
                    step(A(F8[0], F8[0], ACT.Exp))
                    A(F8[0], F8[0], ACT.Ln, bias=1.0).then_inc(ev("fd_ln"), 1)
                qkv(p, l)
                attention(p)
                if l == 0:
                    act_e.wait_ge(ev("sub_var"), 1)
                    A(hstd[:, 0, 0:8], hstat[:, 0, 0:8], ACT.Sqrt, bias=eps_ln, scale=1.0 / P).then_inc(ev("sub_std"), 1)
                transposed(o)
                for u in range(4):
                    split_py(START[o] + u + RING)
                if l == 0:
                    flipped("cd")
                root(e, None, eps_ln)
                transposed(f)
                ffn(f, with_ada=(l == 0))
                root(e + 1, None, eps_ln)
                e += 2
            for l, (f1, p, o, f2) in enumerate((("f1a", "even", "o_even", "f2a"), ("f1b", "odd", "o_odd", "f2b"))):
                if l == 1:
                    flipped("odd")
                root(e, 1.0 / D, eps_rms)
                transposed(f1)
                ffn(f1)
                root(e + 1, 1.0 / D, eps_rms)
                if l == 0:
                    act_e.wait_ge(ev("s5_tr"), 1)
                    A(RB[:, 0], bank[4][:].rearrange("p (m n) -> p m n", m=4), ACT.Copy)
                    A(RB[:, 1], bank[5][:].rearrange("p (m n) -> p m n", m=4), ACT.Copy)
                    A(CT[:, 0], bank[6][:].rearrange("p (m n) -> p m n", m=4), ACT.Copy)
                    A(CT[:, 1], bank[7][:].rearrange("p (m n) -> p m n", m=4), ACT.Copy, scale=-1.0).then_inc(ev("s5_bc"), 1)
                transposed(p)
                if l == 0:
                    act_e.wait_ge(ev("dt_abs"), 1)
                    step(A(sp8[0], sp8[0], ACT.Exp))
                    A(sp8[0], sp8[0], ACT.Ln, bias=1.0).then_inc(ev("dt_ln"), 1)
                for u in range(8):
                    n, k = START[p] + u, PROJ[p] + u
                    act_e.wait_ge(unit_used, n + USED0 + 1)
                    src = bank[4 + k % 3][:].rearrange("p (a t) -> p a t", a=2)
                    if l == 0:
                        dst = (zn[:, :, 256 * u:256 * u + 256] if u < 2 else
                               xpad[:, 2 * u - 4:2 * u - 2, 3:259] if u < 6 else uT[:, 2 * u - 12:2 * u - 10, :])
                    else:
                        dst = (qn, kn, v)[u // 2][:, :, 256 * (u % 2):256 * (u % 2) + 256] if u < 6 else \
                            uTo[:, 2 * u - 12:2 * u - 10, :]
                    A(dst, src, ACT.Copy).then_inc(proj_evac, 1)
                    split_py(n + RING)
                if l == 0:
                    even_act(act_e, A, upper_part)
                else:
                    odd_act(act_e, A, upper_part, attention)
                for u in range(4):
                    split_py(START[o] + u + RING)
                root(e + 2, 1.0 / D, eps_rms)
                transposed(f2)
                ffn(f2)
                e += 3

        @block.vector
        def _(dve):
            step = Chain(dve, v_step)
            TTn, TS, STT = dve.tensor_tensor, dve.tensor_scalar, dve.scalar_tensor_tensor

            def split(slot, n):
                if isinstance(n, int) and n >= UNITS:
                    return
                dve.wait_ge(hi_ready, n + 1)
                TTn(wL[:, slot, :], raw[:, slot, :], wH[:, slot, :].bitcast(F32), ALU.subtract).then_inc(lo_ready, 1)

            def split_py(n):
                split(n % RING, n)

            def ada(slot, cnt):
                dve.wait_ge(ada_full[slot], cnt * 32 + 32)
                dve.wait_ge(ada_mm[slot], cnt + 1)
                acc = ada_acc[:, slot, :]
                for k in range(KC):
                    src = ada_raw[:, slot, 512 * k:512 * k + 512]
                    if k:
                        dve.wait_ge(ada_step[slot], cnt * 8 + k)
                    STT(acc, src, silc[:, k:k + 1], ada_b[:, slot, :] if k == 0 else acc, ALU.mult, ALU.add)\
                        .then_inc(ada_step[slot], 1)

            def lower_part(r, g):
                dve.wait_ge(th_ready, 4 * r + g + 1)
                TTn(hL[:, 2 * g:2 * g + 2, :], t32[:, 2 * g:2 * g + 2, :], hH[:, 2 * g:2 * g + 2, :].bitcast(F32),
                    ALU.subtract).then_inc(tl_ready, 1)

            def transposed(name, scale=None, offset=None, whole=True, groups=4):
                r, base = TR[name], TRD[name]
                if whole:
                    dve.wait_ge(tr_done, base + groups)
                for g in range(groups):
                    dve.wait_ge(tr_done, base + g + 1)
                    for c in (2 * g, 2 * g + 1):
                        src, dst = bank[4 + g][:, (c % 2) * T:(c % 2) * T + T], t32[:, c, :]
                        sc = scale(c) if scale else None
                        if offset:
                            last = TS(dst, src, sc, offset(c), ALU.mult, ALU.add)
                        elif sc is not None:
                            last = TS(dst, src, sc, None, ALU.mult)
                        else:
                            last = dve.tensor_copy(dst, src)
                    last.then_inc(t32_ready, 1)
                    if g:
                        lower_part(r, g - 1)
                lower_part(r, groups - 1)

            def qkv(name, l):
                n0 = START[name]
                with dve.Fori(0, 2) as m:
                    with dve.Fori(0, 2) as j:
                        it = m * 2 + j
                        ada(0, it + (2 if l == 0 else 6))
                        split(n0 % RING, it * 3 + (n0 + 3))
                        if l == 0:
                            ada(1, it + 2)
                        split((n0 + 1) % RING, it * 3 + (n0 + 4))
                        split((n0 + 2) % RING, it * 3 + (n0 + 5))

            def attention(name):
                g0, heads = HEAD0[name], HEADS[name]
                nfox = [0]

                def maxima(i):
                    g = g0 + i
                    b = heads[i][4]
                    dve.wait_ge(s_ready, g + 1)
                    if b is None:
                        h, fb = nfox[0], foxb[:, g % 2, :]
                        nfox[0] += 1
                        STT(fb[:, 0:128], lower[:], ccol[:, 0, h:h + 1], bank[7][:, 0:128], ALU.add, ALU.subtract)
                        TS(fb[:, 128:256], bank[7][:, 0:128], -1.0, ccol[:, 1, h:h + 1], ALU.mult, ALU.add)
                        STT(fb[:, 256:384], lower[:], ccol[:, 1, h:h + 1], bank[7][:, 128:256], ALU.add, ALU.subtract)\
                            .then_inc(ev("fox_used"), 1)
                        dve.wait_ge(ev("fox_used"), h + 1)
                        b0, b1 = fb[:, 0:128], fb[:, 128:384]
                    else:
                        b0, b1 = bias[:, b, 128:256], bias[:, b, 0:256]
                    if i >= 3:
                        dve.wait_ge(pT_ready, g - 2)
                    for tt, (lo, hi, bb) in enumerate(((0, 128, b0), (128, 384, b1))):
                        last = dve.tensor_tensor_reduce(out=sP[:, g % 3, lo:hi], in0=bank[g % 3][:, lo:hi], in1=bb,
                                                        scale=-1.0, scalar=3.0e38, op0=ALU.add, op1=ALU.min,
                                                        accum_out=mx[:, g % 3, tt:tt + 1])
                    last.then_inc(s_max, 1)

                def normalise(i):
                    g = g0 + i
                    _, _, _, dv, _, oc = heads[i]
                    dve.wait_ge(o_ready, g + 1)
                    step(dve.reciprocal(rs[:, g % 4, :], sums[:, g % 4, :]))
                    second = name == "ab" and i < 8 and i % 2 == 1
                    if second:
                        step(TS(rs[:, g % 4, :], rs[:, g % 4, :], neg_lam, None, ALU.mult))
                    for tt in range(TT):
                        src, dst = bank[5 + g % 2][:, tt * dv:tt * dv + dv], nat[:, tt, oc:oc + dv]
                        r = rs[:, g % 4, tt:tt + 1]
                        if second:
                            last = STT(dst, src, r, dst, ALU.mult, ALU.add)
                        else:
                            last = TS(dst, src, r, None, ALU.mult)
                    last.then_inc(o_done, 1)
                    if name == "ab" and i < 8:
                        dve.wait_ge(o_done, g + 1)

                for s in range(len(heads) + 3):
                    if s < len(heads):
                        maxima(s)
                    if s >= 3:
                        normalise(s - 3)

            def ffn(name, with_ada=False):
                n0, f = START[name], 11 * FFN[name]

                def hidden(i, n, slot):
                    TTn(act, sil, bank[5][:], ALU.mult).then_inc(act_mul, 1)
                    dve.wait_ge(act_hi, i + (f + 1))
                    TTn(aL[:], act.rearrange("p (a t) -> p a t", a=2), aH[:].bitcast(F32), ALU.subtract).then_inc(act_lo, 1)
                    split(slot, n)

                split_py(n0 + 3)
                dve.wait_ge(sil_done, f + 1)
                dve.wait_ge(unit_used, n0 + USED0 + 2)
                hidden(0, n0 + 4, (n0 + 4) % RING)

                def body(i):
                    n = i * 3 + (n0 - 1)
                    split((n0 + 5) % RING, n + 3)
                    split((n0 + 6) % RING, n + 4)
                    dve.wait_ge(sil_done, i + (f + 1))
                    dve.wait_ge(unit_used, n + (USED0 + 3))
                    hidden(i, n + 5, (n0 + 7) % RING)

                if with_ada:
                    with dve.Fori(0, 2) as m:
                        with dve.Fori(0, 4) as j:
                            b = m * 4 + j
                            ada(1, b + 6)
                            body(b + 1)
                with dve.Fori(9 if with_ada else 1, FC - 1) as i:
                    body(i)
                body(FC - 1)
                split_py(n0 + 35)

            def used_all(name, count):
                dve.wait_ge(unit_used, START[name] + count + USED0)

            def layer_norm(e, gate):
                dve.wait_ge(ln_loaded, 32 * (e + 1))
                for tt in range(TT):
                    for h in range(2):
                        last = TTn(nat[:, tt, 512 * h:512 * h + 512], bank[2 * tt + h][:],
                                   gate1[:, gate, 512 * h:512 * h + 512], ALU.mult)
                    step(last)
                    step(STT(x[:, tt, :], x[:, tt, :], ALPHA, nat[:, tt, :], ALU.mult, ALU.add))
                    for h in range(2):
                        last = dve.bn_stats(stat[:, tt, 6 * h:6 * h + 6], x[:, tt, 512 * h:512 * h + 512])
                    step(last)
                    dve.bn_aggr(mv[:, tt, :], stat[:, tt, 0:12].rearrange("p (h s) -> p h s", h=2)).then_inc(var_ready, 1)
                for tt in range(TT):
                    dve.wait_ge(std_ready, 2 * e + tt + 1)
                    step(dve.reciprocal(rstd[:, tt:tt + 1], std[:, tt:tt + 1]))
                    step(TS(x[:, tt, :], x[:, tt, :], mv[:, tt, 0:1], rstd[:, tt:tt + 1], ALU.subtract, ALU.mult))
                    step(TTn(x[:, tt, :], x[:, tt, :], lnv[:, 0, :], ALU.mult))
                    TTn(x[:, tt, :], x[:, tt, :], lnv[:, 1, :], ALU.add).then_inc(nat_ready if e < 3 else ev("x_one"), 1)
                if e < 3:
                    dve.wait_ge(nat_ready, 2 * LN_TR[e] + 2)
                else:
                    dve.wait_ge(ev("x_one"), 2)
                dve.sem_inc(ln_used, 1)

            def rms(e, add=None, last=False):
                for tt in range(TT):
                    if add is not None:
                        for h in range(2):
                            xs = x[:, tt, 512 * h:512 * h + 512]
                            ins = STT(xs, bank[2 * tt + h][:], add, xs, ALU.mult, ALU.add)
                        if last:
                            ins.then_inc(ev("x_final"), 1)
                            continue
                        step(ins)
                    dve.tensor_tensor_reduce(out=nat[:, tt, :], in0=x[:, tt, :], in1=x[:, tt, :], scale=1.0, scalar=0.0,
                                             op0=ALU.mult, op1=ALU.add, accum_out=xss[:, tt:tt + 1]).then_inc(var_ready, 1)
                if last:
                    return
                for tt in range(TT):
                    dve.wait_ge(std_ready, 2 * e + tt + 1)
                    step(dve.reciprocal(rstd[:, tt:tt + 1], std[:, tt:tt + 1]))
                    TS(nat[:, tt, :], x[:, tt, :], rstd[:, tt:tt + 1], None, ALU.mult).then_inc(nat_ready, 1)

            for s, k in ((lo_ready, LO0), (unit_used, USED0), (proj_evac, EVAC0), (nat_ready, 2), (ada_mm[0], 1),
                         (ada_mm[1], 1), (ada_out[0], 1), (ada_out[1], 1)):
                dve.sem_inc(s, k)
            dve.memset(ones[:], 1.0)
            dve.memset(eps_ln, LN_EPS)
            dve.memset(eps_rms, RMS_EPS)
            dve.memset(zeros[:], 0.0).then_inc(ev("consts"), 1)
            dve.memset(ada_b[:], 0.0).then_inc(ev("ada_b_zero"), 1)
            dve.wait_ge(ev("silc"), 1)
            for b in range(4):
                ada(b % 2, b // 2)
            for n in range(RING):
                split_py(n)
            dve.wait_ge(ada_out[0], 3)
            dve.wait_ge(ada_out[1], 3)
            step(TS(adaC[:, 0, 8:16], adaC[:, 0, 8:16], 1.0, None, ALU.add))
            transposed("ab", lambda c: adaC[:, 0, 8 + c:9 + c], lambda c: adaC[:, 0, c:c + 1], whole=False)
            dve.wait_ge(setup_in, 16 * SETUP_LOADS)
            dve.wait_ge(ev("rows_in"), 16 * ROW_LOADS)
            dve.tensor_copy(rowC[32:48, :].rearrange("n (g p) -> n g p", g=2), dt2.unsqueeze(2).to_broadcast([16, 2, HD]))\
                .then_inc(ev("dt_rows"), 1)
            dve.wait_ge(ev("toep_mm"), 1)
            TTn(toepA, bank[1][0:20, 0:TOEP], addc, ALU.add).then_inc(ev("toep_rows"), 1)
            dve.tensor_copy(toepE[:, 0:128], relrow[:, 256:257].to_broadcast([8, 128]))
            step(dve.memset(toepE[:, 383:384], 0.0))
            dve.tensor_copy(toepE[:, 128:383], relrow[:, 255:0:-1]).then_inc(ev("toep_rows"), 1)
            dve.tensor_tensor_reduce(out=lamrow[:, 0:64], in0=lamrow[:, 0:64], in1=lamrow[:, 64:128], scale=1.0,
                                     scalar=0.0, op0=ALU.mult, op1=ALU.add, accum_out=lam[0:1, 0:1])
            dve.tensor_tensor_reduce(out=lamrow[:, 128:192], in0=lamrow[:, 128:192], in1=lamrow[:, 192:256], scale=1.0,
                                     scalar=0.0, op0=ALU.mult, op1=ALU.add, accum_out=lam[0:1, 1:2]).then_inc(ev("lam_sums"), 1)
            dve.wait_ge(ev("lam_exp"), 1)
            step(TTn(lam[0:1, 4:5], lam[0:1, 3:4], lam[0:1, 2:3], ALU.subtract))
            TS(lam[0:1, 5:6], lam[0:1, 4:5], -LAMBDA_INIT, None, ALU.add).then_inc(ev("lam_row"), 1)
            dve.wait_ge(ev("lam_col"), 1)
            dve.tensor_copy(neg_lam, bank[2][:, 256:257])
            dve.wait_ge(ev("cols_tr"), 1)
            dve.tensor_copy(colC[:], bank[2][:, 128:176]).then_inc(ev("cols_ready"), 1)
            step(dve.tensor_copy(cols[:], bank[2][:, 0:NCOL]))
            TS(cols[:, C_SUBLN:C_SUBLN + 1], cols[:, C_SUBLN:C_SUBLN + 1], 1.0 - LAMBDA_INIT, None, ALU.mult)
            TS(cols[:, C_QN:C_QN + 1], cols[:, C_QN:C_QN + 1], ATTN_SCALE, None, ALU.mult).then_inc(ev("cols_ready"), 1)
            ar, ai = colC[:, 0:16], colC[:, 16:32]
            co, si, fr, fi, mag, t5, dt, th, r, sh, t10, t11 = (s5c[:, n, :] for n in range(12))
            dve.wait_ge(ev("s5_dt"), 1)
            step(TTn(th, dt, ai, ALU.mult))
            step(TS(t10, th, 1.0 / (2.0 * np.pi), ROUND_MAGIC, ALU.mult, ALU.add))
            step(TS(t10, t10, ROUND_MAGIC, None, ALU.subtract))
            step(STT(r, t10, -TWO_PI_PARTS[0], th, ALU.mult, ALU.add))
            step(STT(r, t10, -TWO_PI_PARTS[1], r, ALU.mult, ALU.add))
            step(STT(r, t10, -TWO_PI_PARTS[2], r, ALU.mult, ALU.add))
            step(TS(r, r, 3.1415925, -3.1415925, ALU.min, ALU.max))
            TTn(th, dt, ar, ALU.mult).then_inc(ev("s5_angle"), 1)
            dve.wait_ge(ev("s5_sin"), 2)
            step(TTn(t10, sh, sh, ALU.mult))
            step(TS(co, t10, -2.0, 1.0, ALU.mult, ALU.add))
            step(TTn(t10, mag, co, ALU.mult))
            step(TS(t10, t10, -1.0, None, ALU.add))
            step(TTn(t11, mag, si, ALU.mult))
            step(TTn(th, ar, ar, ALU.mult))
            step(TTn(r, ai, ai, ALU.mult))
            step(TTn(th, th, r, ALU.add))
            step(dve.reciprocal(t5, th))
            step(TTn(th, t10, ar, ALU.mult))
            step(TTn(r, t11, ai, ALU.mult))
            step(TTn(th, th, r, ALU.add))
            step(TTn(fr, th, t5, ALU.mult))
            step(TTn(th, t11, ar, ALU.mult))
            step(TTn(r, t10, ai, ALU.mult))
            step(TTn(th, th, r, ALU.subtract))
            step(TTn(fi, th, t5, ALU.mult))

            e = 0
            for l, (p, o, f) in enumerate((("ab", "o_ab", "ff0"), ("cd", "o_cd", "ff1"))):
                col = lambda at, l=l: (lambda c: adaC[:, l, at + c:at + c + 1])
                if l == 1:
                    transposed(p, col(8), col(0), whole=False)
                if l == 1:
                    dve.wait_ge(ev("fd_mm"), 1)
                    step(TS(F8[1], bank[7][0:8, 0:T], a8[:, 0:1], -1.0, ALU.add, ALU.mult))
                    STT(F8[0], F8[1], -1.0, F8[1], ALU.mult, ALU.min).then_inc(ev("fd_abs"), 1)
                    dve.wait_ge(ev("fd_ln"), 1)
                    step(STT(F8[2], F8[1], 0.0, F8[0], ALU.max, ALU.add))
                    dve.tensor_tensor_scan(F8[3], ones[0:8, 0:1].to_broadcast([8, T]), F8[2], 0.0, ALU.mult, ALU.subtract)\
                        .then_inc(ev("fd_cum"), 1)
                qkv(p, l)
                if l == 0:
                    dve.wait_ge(ada_out[1], 7)
                    step(TS(adaC[:, 0, 24:32], adaC[:, 0, 24:32], 1.0, None, ALU.add))
                    dve.wait_ge(flip_out, FLIP0["ab"] + 6)
                else:
                    dve.wait_ge(flip_out, FLIP0["cd"] + 4)
                    dve.wait_ge(ev("fd_cols"), 1)
                    dve.tensor_copy(ccol[:, :, 0:8], bank[7][:, 0:16].rearrange("p (a h) -> p a h", a=TT))\
                        .then_inc(ev("ccol_ready"), 1)
                    dve.wait_ge(ev("ccol_ready"), 1)
                attention(p)
                if l == 0:
                    sq = carve(mix, 0, TT, 512)
                    oa = nat[:, :, 0:512]
                    step(TTn(sq, oa, oa, ALU.mult))
                    dve.reduce_sum(hstat[:, 0, 0:8], sq.rearrange("p a (h d) -> p (a h) d", d=P), AX.X)\
                        .then_inc(ev("sub_var"), 1)
                    dve.wait_ge(ev("sub_std"), 1)
                    step(dve.reciprocal(hstd[:, 1, 0:8], hstd[:, 0, 0:8]))
                    for tt in range(TT):
                        v4 = nat[:, tt, 0:512].rearrange("p (h d) -> p h d", d=P)
                        TTn(v4, v4, hstd[:, 1, 4 * tt:4 * tt + 4].unsqueeze(2).to_broadcast([P, 4, P]), ALU.mult)\
                            .then_inc(nat_ready, 1)
                    transposed(o, lambda c: cols[:, C_SUBLN:C_SUBLN + 1] if c < 4 else ones_col)
                else:
                    dve.wait_ge(o_done, HEAD0[p] + len(HEADS[p]))
                    dve.sem_inc(nat_ready, 2)
                    transposed(o)
                for u in range(4):
                    split_py(START[o] + u + RING)
                used_all(o, 4)
                layer_norm(e, 0)
                transposed(f, col(24), col(16), whole=False)
                ffn(f, with_ada=(l == 0))
                used_all(f, 33)
                layer_norm(e + 1, 1)
                e += 2
                if l == 0:
                    dve.wait_ge(ada_out[1], 15)
                    TS(adaC[:, 1, 8:16], adaC[:, 1, 8:16], 1.0, None, ALU.add)
                    step(TS(adaC[:, 1, 24:32], adaC[:, 1, 24:32], 1.0, None, ALU.add))
            add = None
            for l, (f1, p, o, f2) in enumerate((("f1a", "even", "o_even", "f2a"), ("f1b", "odd", "o_odd", "f2b"))):
                gain = lambda at, l=l: (lambda c: cols[:, at + 8 * l + c:at + 8 * l + c + 1])
                rms(e, add)
                transposed(f1, gain(C_FF1))
                ffn(f1)
                used_all(f1, 33)
                rms(e + 1, 0.5)
                transposed(p, gain(C_MIX))
                if l == 0:
                    even_dve(dve, step, split_py, transposed, lower_part)
                else:
                    odd_dve(dve, step, split_py, transposed, lower_part, attention)
                for u in range(4):
                    split_py(START[o] + u + RING)
                used_all(o, 4)
                rms(e + 2, 1.0)
                transposed(f2, gain(C_FF2))
                ffn(f2)
                used_all(f2, 33)
                add = 0.5
                e += 3
            rms(e, 0.5, last=True)

        @block.tensor
        def _(pe):
            mm = pe.matmul

            def unit_in(slot, n):
                pe.wait_ge(lo_ready, n + (LO0 + 1))
                return (wH[:, slot, :].rearrange("p (k c) -> p k c", k=KC), wL[:, slot, :].rearrange("p (k c) -> p k c", k=KC))

            def cols_unit(slot, n, dst):
                H, L = unit_in(slot, n)
                for ft in range(2):
                    for k in range(KC):
                        wh, wl = H[:, k, ft * P:ft * P + P], L[:, k, ft * P:ft * P + P]
                        for i, (w, h) in enumerate(((wh, hH), (wh, hL), (wl, hH))):
                            last = mm(dst[:, ft * T:ft * T + T], w, h[:, k, :], start=(k == 0 and i == 0),
                                      stop=(k == KC - 1 and i == 2))
                last.then_inc(unit_used, 1)

            def toks_unit(slot, n, dst):
                H, L = unit_in(slot, n)
                for tt in range(TT):
                    for k in range(KC):
                        hh, hl = hH[:, k, tt * P:tt * P + P], hL[:, k, tt * P:tt * P + P]
                        for i, (h, w) in enumerate(((hh, H), (hh, L), (hl, H))):
                            last = mm(dst[:, tt * UC:tt * UC + UC], h, w[:, k, :], start=(k == 0 and i == 0),
                                      stop=(k == KC - 1 and i == 2))
                last.then_inc(unit_used, 1)

            def rows_unit(slot, n, H, L, k0, start, stop):
                pe.wait_ge(lo_ready, n + (LO0 + 1))
                wh, wl = (w[:, slot, :].rearrange("p (k c) -> p k c", k=2) for w in (wH, wL))
                for tt in range(TT):
                    for h in range(2):
                        for k in range(2):
                            c = slice(512 * h, 512 * h + 512)
                            ah, al = (z[:, k0 + k, tt * P:tt * P + P] for z in (H, L))
                            for i, (s, w) in enumerate(((ah, wh), (ah, wl), (al, wh))):
                                last = mm(bank[2 * tt + h][:], s, w[:, k, c], start=(start and k == 0 and i == 0),
                                          stop=(stop and k == 1 and i == 2), skip_group_check=True)
                last.then_inc(unit_used, 1)

            def ada(l, slot, cnt, gate):
                pe.wait_ge(ada_step[slot], cnt * 8 + 8)
                pe.wait_ge(ada_out[slot], cnt + 1)
                acc = ada_acc[:, slot, :]
                if gate:
                    mm(bank[7][:], ones[:], acc, start=True, stop=True).then_inc(ada_mm[slot], 1)
                else:
                    b = bank[7 if slot == 0 else 3]
                    for u in range(4):
                        last = mm(b[:, u:u + 1], acc[:, u * P:u * P + P], ones_col, start=True, stop=True)
                    last.then_inc(ada_mm[slot], 1)

            def transposed(name, src, chunks=KC):
                pe.wait_ge(nat_ready, 2 * TR[name] + 2)
                for g in range(chunks // 2):
                    for c in range(2):
                        for tt in range(TT):
                            k = 2 * g + c
                            last = pe.transpose(bank[4 + g][:, c * T + tt * P:c * T + tt * P + P],
                                                src[:, tt, k * P:k * P + P], ident[:])
                    last.then_inc(tr_done, 1)

            def split_ready(name):
                pe.wait_ge(tl_ready, 4 * TR[name] + 4)

            def narrow(which):
                for k in range(KC):
                    last = mm(bank[7][0:8, 0:T], wsmall[:, which, k, :], t32[:, k, :], start=(k == 0), stop=(k == KC - 1))
                return last

            def qkv(name, l):
                n0, u0 = START[name], PROJ[name]
                with pe.Fori(0, 2) as m:
                    with pe.Fori(0, 2) as j:
                        it = m * 2 + j
                        for u in range(3):
                            pe.wait_ge(proj_evac, it * 3 + (u0 + u + EVAC0 - 2))
                            (toks_unit if u == 2 else cols_unit)((n0 + u) % RING, it * 3 + (n0 + u), bank[4 + u])
                        ada(l, 0, it + (2 if l == 0 else 6), True)
                        if l == 0:
                            ada(0, 1, it + 2, False)

            def flipped(name, arrived):
                pe.wait_ge(toep_in, arrived)
                for n in range(FLIPS[name]):
                    if n >= 3:
                        pe.wait_ge(flip_out, FLIP0[name] + n - 2)
                    mm(bank[4 + n % 3][:], flip[:], bias[:, 2 * n:2 * n + 2, :], start=True, stop=True).then_inc(flip_mm, 1)
                pe.wait_ge(flip_out, FLIP0[name] + FLIPS[name])

            def attention(name):
                g0, heads = HEAD0[name], HEADS[name]
                fox = [0]

                def scores(i):
                    g = g0 + i
                    tile, base, _, _, b, _ = heads[i]
                    if i >= 3:
                        pe.wait_ge(s_max, g - 2)
                    if b is None:
                        if fox[0]:
                            pe.wait_ge(ev("fox_used"), fox[0])
                        mm(bank[7][:, 0:T], head_bcast(fox[0]), F8[3], start=True, stop=True)
                        fox[0] += 1
                    q, k = qT[base:base + HD, tile, :], kT[base:base + HD, tile, :]
                    mm(bank[g % 3][:, 0:128], q[:, 0:P], k[:, 0:P], start=True, stop=True)
                    mm(bank[g % 3][:, 128:384], q[:, P:T], k, start=True, stop=True).then_inc(s_ready, 1)

                def turn(i):
                    g = g0 + i
                    pe.wait_ge(p_ready, g + 1)
                    if i >= 2:
                        pe.wait_ge(pT_copied, g - 1)
                    for b in range(3):
                        last = pe.transpose(bank[3 + g % 2][:, b * P:b * P + P], sP[:, g % 3, b * P:b * P + P], ident[:])
                    last.then_inc(pT_ready, 1)

                def values(i):
                    g = g0 + i
                    _, _, vc, dv, _, _ = heads[i]
                    pe.wait_ge(pT_copied, g + 1)
                    if i >= 2:
                        pe.wait_ge(o_done, g - 1)
                    o, w = bank[5 + g % 2], PT[:, g % 2, :]
                    mm(o[:, 0:dv], w[:, 0:P], v[:, 0, vc:vc + dv], start=True, stop=True)
                    mm(o[:, dv:2 * dv], w[:, P:2 * P], v[:, 0, vc:vc + dv], start=True, stop=False)
                    mm(o[:, dv:2 * dv], w[:, 2 * P:3 * P], v[:, 1, vc:vc + dv], start=False, stop=True).then_inc(o_ready, 1)

                for s in range(len(heads) + 3):
                    if s < len(heads):
                        scores(s)
                    if 2 <= s < len(heads) + 2:
                        turn(s - 2)
                    if s >= 3:
                        values(s - 3)

            def out_proj(name):
                split_ready(name)
                n0 = START[name]
                for u in range(4):
                    rows_unit((n0 + u) % RING, n0 + u, hH, hL, 2 * u, u == 0, u == 3)

            def ffn(name, with_ada=False):
                split_ready(name)
                n0, f = START[name], 11 * FFN[name]
                for b in range(4):
                    mm(bank[b][:], zeros[:, 0:128], zeros[:, 128:640], start=True, stop=False, skip_group_check=True)
                cols_unit(n0 % RING, n0, bank[4])
                cols_unit((n0 + 1) % RING, n0 + 1, bank[5])

                def body(i):
                    n = i * 3 + (n0 - 1)
                    pe.wait_ge(sil_done, i + f)
                    cols_unit((n0 + 2) % RING, n, bank[4])
                    pe.wait_ge(act_lo, i + f)
                    rows_unit((n0 + 3) % RING, n + 1, aH, aL, 0, False, False)
                    cols_unit((n0 + 4) % RING, n + 2, bank[5])

                if with_ada:
                    with pe.Fori(0, 2) as m:
                        with pe.Fori(0, 4) as j:
                            b = m * 4 + j
                            body(b + 1)
                            ada_late(b)
                with pe.Fori(9 if with_ada else 1, FC) as i:
                    body(i)
                pe.wait_ge(act_lo, FC + f)
                rows_unit((n0 + 32) % RING, n0 + 32, aH, aL, 0, False, True)

            def ada_late(b):
                pe.wait_ge(ada_step[1], b * 8 + 56)
                pe.wait_ge(ada_out[1], b + 7)
                for u in range(4):
                    last = mm(bank[7][:, u:u + 1], ada_acc[:, 1, u * P:u * P + P], ones_col, start=True, stop=True)
                last.then_inc(ada_mm[1], 1)

            pe.wait_ge(ev("first_in"), 32)
            pe.transpose(bank[0][:, 0:8], rows_c, ident[0:8, 0:8]).then_inc(ev("c_cols"), 1)
            pe.wait_ge(ev("consts"), 1)
            for b in range(4):
                ada(0, b % 2, b // 2, False)
            pe.wait_ge(ev("x_in"), 16)
            pe.wait_ge(ada_out[0], 3)
            transposed("ab", x)
            pe.wait_ge(setup_in, 16 * SETUP_LOADS)
            pe.wait_ge(ev("rows_in"), 16 * ROW_LOADS)
            mm(bank[1][0:20, 0:TOEP], table, onehot, start=True, stop=True).then_inc(ev("toep_mm"), 1)
            pe.wait_ge(ev("dt_rows"), 1)
            pe.transpose(bank[2][:, 0:NCOL], rows, ident[0:NCOL, 0:NCOL])
            pe.transpose(bank[2][:, 128:176], rowC, ident[0:48, 0:48]).then_inc(ev("cols_tr"), 1)
            pe.wait_ge(ev("lam_row"), 1)
            mm(bank[2][:, 256:257], ones[0:1, :], lam[0:1, 5:6], start=True, stop=True).then_inc(ev("lam_col"), 1)
            flipped("ab", 16)

            for l, (p, o, f) in enumerate((("ab", "o_ab", "ff0"), ("cd", "o_cd", "ff1"))):
                if l == 1:
                    transposed(p, x)
                    pe.wait_ge(t32_ready, 4 * TR["cd"] + 4)
                    narrow(0).then_inc(ev("fd_mm"), 1)
                split_ready(p)
                qkv(p, l)
                pe.wait_ge(proj_evac, PROJ[p] + 12 + EVAC0)
                if l == 1:
                    pe.wait_ge(ada_out[0], 11)
                    pe.wait_ge(ev("fd_cum"), 1)
                    for tt in range(TT):
                        last = pe.transpose(bank[7][:, 8 * tt:8 * tt + 8], F8[3][:, tt * P:tt * P + P], ident[0:8, 0:8])
                    last.then_inc(ev("fd_cols"), 1)
                    pe.wait_ge(ev("ccol_ready"), 1)
                attention(p)
                transposed(o, nat)
                out_proj(o)
                if l == 0:
                    flipped("cd", 32)
                transposed(f, x)
                ffn(f, with_ada=(l == 0))
            for l, (f1, p, o, f2) in enumerate((("f1a", "even", "o_even", "f2a"), ("f1b", "odd", "o_odd", "f2b"))):
                if l == 1:
                    flipped("odd", 48)
                transposed(f1, nat)
                ffn(f1)
                if l == 0:
                    pe.wait_ge(ev("bp_ready"), 1)
                    for i, src in enumerate((BP[:, 0].rearrange("p (m j) c -> p m (j c)", m=4),
                                             BP[:, 1].rearrange("p (m j) c -> p m (j c)", m=4), Cpad[:, 0], Cpad[:, 1])):
                        for m in range(4):
                            last = pe.transpose(bank[4 + i][:, m * P:m * P + P], src[:, m, :], ident[:])
                    last.then_inc(ev("s5_tr"), 1)
                    pe.wait_ge(ev("s5_bc"), 1)
                transposed(p, nat)
                if l == 0:
                    pe.wait_ge(t32_ready, 4 * TR["even"] + 4)
                    narrow(1).then_inc(ev("dt_mm"), 1)
                split_ready(p)
                for u in range(8):
                    n, k = START[p] + u, PROJ[p] + u
                    pe.wait_ge(proj_evac, k + EVAC0 - 2)
                    (toks_unit if u < (2, 6)[l] else cols_unit)(n % RING, n, bank[4 + k % 3])
                (even_pe if l == 0 else odd_pe)(pe, mm, transposed, attention)
                out_proj(o)
                transposed(f2, nat)
                ffn(f2)

    return nc


_SHAPE = (1, T, D)


def kernel(**inputs):
    import concourse.bacc as bacc
    from concourse.bass_utils import run_bass_kernel_spmd

    nc = bacc.Bacc("TRN2", target_bir_lowering=False, num_devices=1)
    arrays, args = {}, {}
    for name, value in {**inputs, **constants()}.items():
        value = np.ascontiguousarray(value)
        arrays[f"in_{name}"] = value
        args[name] = nc.dram_tensor(f"in_{name}", value.shape, mybir.dt.from_np(value.dtype), kind="ExternalInput").ap()
    out = nc.dram_tensor("out", _SHAPE, F32, kind="ExternalOutput").ap()
    build_program(nc, args, out)
    result = run_bass_kernel_spmd(nc, [arrays], core_ids=[0])
    return result.results[0]["out"]
```

```python
from contextlib import ExitStack

import numpy as np

import concourse.bass as bass
from concourse import mybir

F32 = mybir.dt.float32
F32R = mybir.dt.float32r
BF16 = mybir.dt.bfloat16
ACT = mybir.ActivationFunctionType
ALU = mybir.AluOpType
AX = mybir.AxisListType

P = 128
T = 256
TT = T // P
D = 1024
KC = D // P
FF = 2816
UC = 256
FC = FF // UC
UNIT = 2048
RING = 3
HD = 64
NUM_BUCKETS, MAX_DISTANCE = 32, 128
ATTN_SCALE = HD ** -0.5
ALPHA = 4 ** 0.25
LAMBDA_INIT = 0.2
LN_EPS, RMS_EPS = 1e-5, 1e-6
NEG = -1.0e30
TOEP = 384

_PHASES = [("ab", 12), ("o_ab", 4), ("ff0", 33), ("cd", 12), ("o_cd", 4), ("ff1", 33), ("f1a", 33), ("even", 8),
           ("o_even", 4), ("f2a", 33), ("f1b", 33), ("odd", 8), ("o_odd", 4), ("f2b", 33)]
START, _n = {}, 0
for _name, _count in _PHASES:
    START[_name] = _n
    _n += _count
UNITS = _n
PROJ = {"ab": 0, "cd": 12, "even": 24, "odd": 32}
TR = {n: i for i, n in enumerate(["ab", "o_ab", "ff0", "cd", "o_cd", "ff1", "f1a", "even", "o_even", "f2a", "f1b",
                                  "odd", "o_odd", "f2b"])}
SUMS = {n: i for i, n in enumerate(["o_ab", "ff0", "o_cd", "ff1", "f1a", "o_even", "f2a", "f1b", "o_odd", "f2b"])}
FFN = {n: i for i, n in enumerate(["ff0", "ff1", "f1a", "f2a", "f1b", "f2b"])}
LO0 = USED0 = EVAC0 = 3

C_FF1, C_MIX, C_FF2, C_CONVB, C_CONVW, C_SSDN, C_GLUB, C_PSCALE, C_S5D, C_SUBLN, C_QN, C_KN = (
    0, 16, 32, 48, 56, 88, 92, 96, 100, 104, 105, 106)
NCOL = 107
TWO_PI_PARTS = (6.28125, 1.93500518798828125e-3, 3.0199159819567528e-7)
ROUND_MAGIC = 12582912.0


def constants():
    d = 255 - np.arange(TOEP)
    n = np.maximum(d, 0)
    nf = np.maximum(n, 1).astype(np.float32)
    exact = NUM_BUCKETS // 2
    large = exact + (np.log(nf / np.float32(exact)) / np.float32(np.log(MAX_DISTANCE / exact))
                     * np.float32(NUM_BUCKETS - exact)).astype(np.int32)
    bucket = np.where(n < exact, n, np.minimum(large, NUM_BUCKETS - 1))
    onehot = ((bucket[None, :] == np.arange(NUM_BUCKETS)[:, None]) & (d >= 0)).astype(np.float32)
    causal = np.where(d >= 0, 0.0, NEG)
    many = (d <= 128).astype(int) + (d % 4 == 0) + (d % 16 == 0)
    many = np.where(d >= 0, many, 0)
    dilated = np.where(many > 0, np.log(np.maximum(many, 1)), NEG)
    add = np.stack([causal] * 4 + [dilated] * 8 + [causal] * 8).astype(np.float32)
    i = np.arange(P)
    lower = np.where(i[None, :] <= i[:, None], 0.0, NEG).astype(np.float32)
    t = np.arange(16)
    pool = np.stack([1.0 / np.minimum(t + 1, w) for w in (2, 4, 8, 16)]).astype(np.float32).reshape(1, 64)
    return {"k_flip": np.ascontiguousarray(np.eye(P, dtype=np.float32)[::-1]), "k_ident": np.eye(P, dtype=np.float32), "k_onehot": onehot, "k_add": add, "k_lower": lower,
            "k_upper": np.ascontiguousarray(lower.T), "k_pool": pool}


def build_program(nc, a, out):
    ctx = ExitStack()
    with ctx:
        def sb(name, shape, dt=F32):
            return ctx.enter_context(nc.sbuf_tensor("s_" + name, shape, dt))

        def sem(name):
            return ctx.enter_context(nc.semaphore(name))

        bank = [ctx.enter_context(nc.psum_tensor(f"bank{i}", [P, 512], F32)) for i in range(8)]

        raw = sb("raw", [P, RING, UNIT])
        wH = sb("wH", [P, RING, UNIT], F32R)
        wL = sb("wL", [P, RING, UNIT], F32R)
        x = sb("x", [P, TT, D])
        t32 = sb("t32", [P, KC, T])
        hH = sb("hH", [P, KC, T], F32R)
        hL = sb("hL", [P, KC, T], F32R)
        mix = sb("mix", [P, 10368])
        aH = sb("aH", [P, 2, T], F32R)
        aL = sb("aL", [P, 2, T], F32R)
        late = sb("late", [P, 10240])
        ident = sb("ident", [P, P])
        ones = sb("ones", [P, P])
        zeros = sb("zeros", [P, 640], BF16)
        cols = sb("cols", [P, NCOL])
        colC = sb("colC", [P, 48])
        adaC = sb("adaC", [P, 2, 32])
        flip = sb("flip", [P, P])
        lower = sb("lower", [P, P])
        upper = sb("upper", [P, P])
        silc = sb("silc", [P, KC])
        wsmall = sb("wsmall", [P, 2, KC, 8])
        small = sb("small", [P, 512])
        s5c = sb("s5c", [P, 12, 16])
        poolc = sb("poolc", [P, 64])
        diag = sb("diag", [P, TT, P])
        lnC = sb("lnC", [P, 64])
        lnS = sb("lnS", [P, 3, 16])
        nat = t32[:].rearrange("p k t -> p (k t)").rearrange("p (a n) -> p a n", a=TT)

        def carve(region, at, *shape):
            size = int(np.prod(shape))
            v = region[:, at:at + size]
            if len(shape) == 2:
                return v.rearrange("p (a b) -> p a b", a=shape[0])
            if len(shape) == 3:
                return v.rearrange("p (a b c) -> p a b c", a=shape[0], b=shape[1])
            return v

        qT = carve(mix, 0, KC, T)
        kT = carve(mix, 2048, KC, T)
        v = carve(mix, 4096, TT, D)
        bias = carve(mix, 6144, 12, T)
        sP = carve(mix, 9216, 3, 384)
        sil = carve(mix, 0, 512)
        act = carve(mix, 512, 512)
        ada_raw = carve(late, 0, 2, KC * 512)
        ada_acc = carve(late, 8192, 2, 512)
        first_raw = [z.rearrange("p (k c) -> p k c", k=KC) for z in
                     (ada_raw[:, 0, :], ada_raw[:, 1, :], mix[:, 0:KC * 512], ada_raw[:, 0, :])]
        lnv = carve(mix, 1024, 2, D)
        PT = carve(late, 4096, 2, 384)
        foxb = carve(late, 4096 + 768, 2, 384)
        gate1 = sb("gate1", [P, 2, D])
        ada_b = carve(late, 9216, 2, 512)

        raw_full = [sem(f"raw_full{i}") for i in range(RING)]
        ada_full = [sem(f"ada_full{i}") for i in range(2)]
        hi_ready, lo_ready, unit_used = sem("hi_ready"), sem("lo_ready"), sem("unit_used")
        proj_evac = sem("proj_evac")
        ada_step = [sem(f"ada_step{i}") for i in range(2)]
        ada_mm = [sem(f"ada_mm{i}") for i in range(2)]
        ada_out = [sem(f"ada_out{i}") for i in range(2)]
        nat_ready, tr_done, t32_ready, t32_odd, th_ready, tl_ready = (
            sem(s) for s in ("nat_ready", "tr_done", "t32_ready", "t32_odd", "th_ready", "tl_ready"))
        y_first = sem("y_first")
        sil_done, act_mul, act_hi, act_lo = (sem(s) for s in ("sil_done", "act_mul", "act_hi", "act_lo"))
        flip_mm, flip_out = sem("flip_mm"), sem("flip_out")
        s_ready, s_max, p_ready, pT_ready, pT_copied, o_ready, o_done = (
            sem(s) for s in ("s_ready", "s_max", "p_ready", "pT_ready", "pT_copied", "o_ready", "o_done"))
        var_ready, std_ready, ln_loaded, ln_used = (sem(s) for s in ("var_ready", "std_ready", "ln_loaded", "ln_used"))
        v_step, a_step, g_step, p_step = sem("v_step"), sem("a_step"), sem("g_step"), sem("p_step")
        setup_in, toep_out, toep_in, out_done = (sem(s) for s in ("setup_in", "toep_out", "toep_in", "out_done"))
        events = {}

        def ev(name):
            if name not in events:
                events[name] = sem("e_" + name)
            return events[name]

        class Chain:

            def __init__(self, eng, s):
                self.eng, self.s, self.n = eng, s, 0

            def __call__(self, ins):
                ins.then_inc(self.s, 1)
                self.n += 1
                self.eng.wait_ge(self.s, self.n)

        def col_unit(w, c0):
            return w[:, bass.ds(c0, UC)].rearrange("(k p) c -> p k c", p=P)

        def row_unit(w, r0):
            return w[bass.ds(r0, UC), :].rearrange("(k p) c -> p k c", p=P)

        ffn_w = {
            "ff0": (a["w_ffn_in"][0], 0, a["w_ffn_in"][0], FF, a["w_ffn_out"][0]),
            "ff1": (a["w_ffn_in"][1], 0, a["w_ffn_in"][1], FF, a["w_ffn_out"][1]),
        }
        for l, s in ((0, "a"), (1, "b")):
            for f in ("1", "2"):
                ffn_w[f"f{f}{s}"] = (a[f"ffn{f}_w_gate_2"][l], 0, a[f"ffn{f}_w_up_2"][l], 0, a[f"ffn{f}_w_down_2"][l])
        o_w = {"o_ab": a["w_o"][0], "o_cd": a["w_o"][1], "o_even": a["even_w_out_2"][0], "o_odd": a["odd_w_out_2"][0]}
        EVEN_COLS = [0, 256] + [512 + 256 * i for i in range(4)] + [1544, 1800]
        ODD_COLS = [256 * i for i in range(8)]

        toep = nc.dram_tensor("toep_scratch", [28, TOEP], F32, kind="Internal")

        def toep_tile(row, heads):
            return bass.AP(toep, row * TOEP, [[1, P], [TOEP, heads], [1, T]])

        HEADS = {
            "ab": [(h, 64 * m, 128 * h, 128, h, 128 * h) for h in range(4) for m in range(2)]
            + [(4 + b // 2, 64 * (b % 2), 512 + 64 * b, 64, 4 + b, 512 + 64 * b) for b in range(8)],
            "cd": [(h // 2, 64 * (h % 2), 64 * h, 64, h, 64 * h) for h in range(8)]
            + [(4 + h // 2, 64 * (h % 2), 512 + 64 * h, 64, None, 512 + 64 * h) for h in range(8)],
            "odd": [(h // 2, 64 * (h % 2), 64 * h, 64, h, 64 * h) for h in range(8)],
        }
        HEAD0 = {"ab": 0, "cd": 16, "odd": 32}
        FLIPS = {"ab": 6, "cd": 4, "odd": 4}
        FLIP_BANK = {"ab": 0, "cd": 4, "odd": 4}
        FLIP0 = {"ab": 0, "cd": 6, "odd": 10}

        ones_col = ones[:, 0:1]
        mx = carve(small, 0, 3, 2)
        sums = carve(small, 8, 4, 2)
        rs = carve(small, 16, 4, 2)
        stat = carve(small, 24, 2, 16)
        mv = carve(small, 56, 2, 2)
        std = carve(small, 60, 2)
        rstd = carve(small, 62, 2)
        lam = carve(small, 64, 8)
        hstat = carve(small, 72, 2, 16)
        hstd = carve(small, 104, 2, 16)
        eps_ln = small[:, 136:137]
        eps_rms = small[:, 137:138]
        neg_lam = small[:, 138:139]
        ccol = carve(small, 140, 2, 16)
        a8 = small[0:8, 172:175]
        dsk = carve(small, 176, 8)
        lamrow = small[0:1, 192:448]
        xss = carve(small, 448, 2)

        SET = 6144
        rows = mix[0:NCOL, SET:SET + P]
        rowC = mix[0:48, SET + 128:SET + 256]
        onehot = mix[0:NUM_BUCKETS, SET + 256:SET + 640]
        addc = mix[0:20, SET + 640:SET + 1024]
        table = mix[0:NUM_BUCKETS, SET + 1024:SET + 1044]
        relrow = mix[0:8, SET + 1044:SET + 1301]
        toepA = mix[0:20, SET + 1304:SET + 1688]
        toepE = mix[0:8, SET + 1688:SET + 2072]
        dt2 = mix[32:48, SET + 2072:SET + 2074]
        SETUP_LOADS, ROW_LOADS = 14, 19

        zn = carve(mix, 0, TT, 512)
        xpad = carve(mix, 1024, 8, 259)
        xbcT = carve(mix, 3096, 8, T)
        uT = carve(mix, 5144, 4, T)
        xsn = carve(mix, 6168, TT, 512)
        xdt = carve(mix, 7192, TT, 512)
        G = carve(mix, 8216, 2, 384)
        W = carve(mix, 8984, 2, 384)
        cumT = mix[0:8, 9752:10008]
        dtT = mix[0:8, 10008:10264]
        sp8 = [xsn[0:8, i, 0:T] for i in range(2)] + [xdt[0:8, i, 0:T] for i in range(2)]
        BP = carve(mix, 8216, 2, 16, 32)
        Cpad = carve(mix, 9240, 2, 4, P)
        RB = carve(late, 8192, 2, 4, P)
        CT = carve(late, 9216, 2, 4, P)
        cosT = carve(late, 0, 16, T)
        sinT = carve(late, 4096, 16, T)
        s5w = [carve(mix, 2560 * i, 5, 512) for i in range(2)]
        yT = carve(mix, 6168, 4, T)
        gl = carve(mix, 7192, 4, T)
        wglu = carve(mix, 8216, 4, 512)
        bbin = carve(mix, 2048, 2, 16, 16)
        bbt = carve(mix, 2560, 2, 16, 16)
        tabt = carve(mix, 3072, 2, 16, P)
        qn, kn = carve(mix, 1024, TT, 512), carve(mix, 3072, TT, 512)
        uTo = carve(mix, 8192, 4, T)
        pool_s = [carve(late, 1024 * i, 4, T) for i in range(3)]
        wpool = carve(late, 3072, 4, P)
        sig = carve(mix, 0, 4, T)

        def head_bcast(h):
            return ident[0:8, h:h + 1].to_broadcast([8, P])


        TRD, n_groups = {}, 0
        for name in TR:
            TRD[name] = n_groups
            n_groups += 2 if name in ("o_even", "o_odd") else 4
        T32 = {"ab": 0, "ff0": 2, "cd": 4, "ff1": 6, "even": 8, "o_even": 8, "o_odd": 10}
        T32_ODD = {"ab": 0, "ff0": 2, "cd": 4, "ff1": 6, "even": 8}
        LN_TR = {0: "ff0", 1: "cd", 2: "ff1"}
        F8 = [late[0:8, 5632 + T * i:5632 + T * i + T] for i in range(4)]
        F8H, F8L = aH[0:8, 0, :], aL[0:8, 0, :]
        head_one = aH[0:8, 1, 0:8]
        sq8 = carve(late, 5632, TT, 512)
        rows_c = mix[0:8, SET + 2080:SET + 2208]
        rowL = mix[0:64, SET + 2208:SET + 2336]

        def even_pe(pe, mm, transposed, attention):
            u0 = PROJ["even"]
            pe.wait_ge(proj_evac, u0 + 8 + EVAC0)
            pe.wait_ge(ev("dt_cum"), 1)
            for tt in range(TT):
                for i, src in enumerate((cumT, dtT)):
                    at = 16 * tt + 8 * i
                    last = pe.transpose(bank[2][:, at:at + 8], src[:, tt * P:tt * P + P], ident[0:8, 0:8])
            last.then_inc(ev("dtc_tr"), 1)
            pe.wait_ge(ev("xbc_silu"), 4)
            for tt in range(TT):
                for c in range(4):
                    last = pe.transpose(bank[tt][:, c * P:c * P + P], xbcT[:, c, tt * P:tt * P + P], ident[:])
            last.then_inc(ev("xs_tr"), 1)
            for g in range(2):
                B, C = xbcT[:, 4 + g, :], xbcT[:, 6 + g, :]
                mm(bank[3 + g][:, 0:T], B[:, 0:P], C, start=True, stop=True)
                mm(bank[3 + g][:, T:T + P], B[:, P:T], C[:, P:T], start=True, stop=True).then_inc(ev("g_mm"), 1)
            pe.wait_ge(ev("xsn_ready"), 1)
            for s in range(9):
                if s < 8:
                    if s >= 2:
                        pe.wait_ge(ev("arg_done"), s - 1)
                    mm(bank[5 + s % 2][:, 0:T], head_bcast(s), cumT, start=True, stop=True).then_inc(ev("bc_ready"), 1)
                if s >= 1:
                    h = s - 1
                    pe.wait_ge(ev("w_done"), h + 1)
                    w, c = W[:, h % 2, :], slice(HD * h, HD * h + HD)
                    mm(bank[0][:, c], w[:, 0:P], xdt[:, 0, c], start=True, stop=True)
                    mm(bank[1][:, c], w[:, P:2 * P], xdt[:, 0, c], start=True, stop=False)
                    mm(bank[1][:, c], w[:, 2 * P:3 * P], xdt[:, 1, c], start=False, stop=True).then_inc(ev("y_mm"), 1)
            transposed("o_even", nat, 4)

            def drive(i):
                if i >= 2:
                    pe.wait_ge(ev("s5_state"), i - 1)
                m, j = i // 4, 32 * (i % 4)
                for ri in range(2):
                    last = mm(bank[6 + i % 2][:, T * ri:T * ri + T], RB[j:j + 32, ri, m, :], uT[j:j + 32, m, :],
                              start=True, stop=True)
                last.then_inc(ev("s5_drive"), 1)

            drive(0)
            for i in range(16):
                if i < 15:
                    drive(i + 1)
                m, j = i // 4, 32 * (i % 4)
                pe.wait_ge(ev("s5_cos"), i + 1)
                pe.wait_ge(ev("s5_sine"), i + 1)
                if m >= 2 and j == 0:
                    pe.wait_ge(ev("s5_y"), m - 1)
                pc, ps = s5w[i % 2][:, 3, :], s5w[i % 2][:, 4, :]
                for n, (ri, z) in enumerate(((0, pc[:, 0:T]), (0, ps[:, T:2 * T]), (1, ps[:, 0:T]), (1, pc[:, T:2 * T]))):
                    last = mm(bank[2 + m % 2][j:j + 32, 0:T], CT[:, ri, m, j:j + 32], z, start=(n == 0), stop=(n == 3))
                last.then_inc(ev("s5_used"), 1)
            pe.wait_ge(ev("gelu_done"), 4)
            pe.wait_ge(ev("glu_in"), 16)
            for o in range(4):
                if o >= 2:
                    pe.wait_ge(ev("sig_done"), o - 1)
                for k in range(4):
                    last = mm(bank[o % 2][:, 0:T], wglu[:, k, o * P:o * P + P], gl[:, k, :], start=(k == 0), stop=(k == 3))
                last.then_inc(ev("glu_mm"), 1)

        def even_act(act_e, A, transposed, upper_part):
            for k in range(4):
                act_e.wait_ge(ev("conv_done"), k + 1)
                xs = xbcT[:, 2 * k:2 * k + 2, :]
                A(xs, xs, ACT.Silu).then_inc(ev("xbc_silu"), 1)
            A(zn, zn, ACT.Silu).then_inc(ev("z_silu"), 1)
            act_e.wait_ge(ev("dtc_ready"), 1)
            act_e.wait_ge(ev("xs_tr"), 1)
            A(xsn[:, 0, :], bank[0][:], ACT.Copy)
            A(xsn[:, 1, :], bank[1][:], ACT.Copy).then_inc(ev("xsn_ready"), 1)
            act_e.wait_ge(ev("g_mm"), 2)
            A(G[:, 0, :], bank[3][:, 0:384], ACT.Copy)
            A(G[:, 1, :], bank[4][:, 0:384], ACT.Copy).then_inc(ev("g_ready"), 1)
            for h in range(8):
                act_e.wait_ge(ev("arg_done"), h + 1)
                A(W[:, h % 2, :], W[:, h % 2, :], ACT.Exp).then_inc(ev("dec_done"), 1)
            act_e.wait_ge(ev("ssd_var"), 1)
            A(hstd[:, 0, 0:4], hstat[:, 0, 0:4], ACT.Sqrt, bias=eps_rms, scale=1.0 / 256).then_inc(ev("ssd_std"), 1)
            transposed("o_even", lambda c: cols[:, C_SSDN + c:C_SSDN + c + 1], groups=2, direct=True)
            for m in range(4):
                act_e.wait_ge(ev("s5_y"), m + 1)
                A(gl[:, m, :], yT[:, m, :], ACT.Gelu_apprx_tanh).then_inc(ev("gelu_done"), 1)
            for o in range(4):
                act_e.wait_ge(ev("glu_mm"), o + 1)
                A(sig[:, o, :], bank[o % 2][:, 0:T], ACT.Sigmoid, bias=cols[:, C_GLUB + o:C_GLUB + o + 1])\
                    .then_inc(ev("sig_done"), 1)
            upper_part("o_even", 2)
            upper_part("o_even", 3)

        def even_dve(dve, step, split_py, transposed, lower_part):
            TTn, TS, STT = dve.tensor_tensor, dve.tensor_scalar, dve.scalar_tensor_tensor
            u0, n0 = PROJ["even"], START["even"]
            dve.wait_ge(ev("dt_mm"), 1)
            step(TS(sp8[1], bank[7][0:8, 0:T], a8[:, 1:2], None, ALU.add))
            STT(sp8[0], sp8[1], -1.0, sp8[1], ALU.mult, ALU.min).then_inc(ev("dt_abs"), 1)
            dve.wait_ge(ev("dt_ln"), 1)
            step(STT(dtT, sp8[1], 0.0, sp8[0], ALU.max, ALU.add))
            step(TS(sp8[2], dtT, small[0:8, 175:176], -1.0, ALU.mult, ALU.mult))
            dve.tensor_tensor_scan(cumT, ones[0:8, 0:1].to_broadcast([8, T]), sp8[2], 0.0, ALU.mult, ALU.add)\
                .then_inc(ev("dt_cum"), 1)
            step(dve.memset(xpad[:, :, 0:3], 0.0))

            def conv(u):
                dve.wait_ge(proj_evac, u0 + u + 1 + EVAC0)
                for tap in range(4):
                    for c in (2 * u - 4, 2 * u - 3):
                        w = cols[:, C_CONVW + 8 * tap + c:C_CONVW + 8 * tap + c + 1]
                        src = xpad[:, c, tap:tap + T]
                        if tap == 0:
                            last = TS(xbcT[:, c, :], src, w, cols[:, C_CONVB + c:C_CONVB + c + 1], ALU.mult, ALU.add)
                        else:
                            last = STT(xbcT[:, c, :], src, w, xbcT[:, c, :], ALU.mult, ALU.add)
                    if tap < 3:
                        step(last)
                last.then_inc(ev("conv_done"), 1)

            for u in range(8):
                split_py(n0 + u + RING)
                if 3 <= u <= 6:
                    conv(u - 1)
            dve.wait_ge(ev("dtc_tr"), 1)
            dve.tensor_copy(ccol, bank[2][:, 0:32].rearrange("p (a n) -> p a n", a=TT)).then_inc(ev("dtc_ready"), 1)
            dve.wait_ge(ev("dtc_ready"), 1)
            dve.wait_ge(ev("xsn_ready"), 1)
            for tt in range(TT):
                step(TTn(xdt[:, tt, :].rearrange("p (h d) -> p h d", d=HD), xsn[:, tt, :].rearrange("p (h d) -> p h d", d=HD),
                         ccol[:, tt, 8:16].unsqueeze(2).to_broadcast([P, 8, HD]), ALU.mult))
            dve.wait_ge(ev("g_ready"), 1)
            for s in range(9):
                if s < 8:
                    dve.wait_ge(ev("bc_ready"), s + 1)
                    if s >= 2:
                        dve.wait_ge(ev("y_mm"), s - 1)
                    w, bc = W[:, s % 2, :], bank[5 + s % 2]
                    c0, c1 = ccol[:, 0, s:s + 1], ccol[:, 1, s:s + 1]
                    STT(w[:, 0:P], upper[:], c0, bc[:, 0:P], ALU.subtract, ALU.add)
                    TS(w[:, P:2 * P], bc[:, P:T], c0, None, ALU.subtract)
                    STT(w[:, 2 * P:3 * P], upper[:], c1, bc[:, P:T], ALU.subtract, ALU.add).then_inc(ev("arg_done"), 1)
                if s >= 1:
                    h = s - 1
                    dve.wait_ge(ev("dec_done"), h + 1)
                    TTn(W[:, h % 2, :], W[:, h % 2, :], G[:, h // 4, :], ALU.mult).then_inc(ev("w_done"), 1)
            dve.wait_ge(ev("y_mm"), 8)
            dve.wait_ge(ev("z_silu"), 1)
            for tt in range(TT):
                y = nat[:, tt, 0:512]
                heads = lambda z: z.rearrange("p (h d) -> p h d", d=HD)
                step(TTn(heads(y), heads(xsn[:, tt, :]), dsk.unsqueeze(2).to_broadcast([P, 8, HD]), ALU.mult))
                step(TTn(y, y, bank[tt][:], ALU.add))
                step(TTn(y, y, zn[:, tt, :], ALU.mult))
                step(TTn(xdt[:, tt, :], y, y, ALU.mult))
            dve.reduce_sum(hstat[:, 0, 0:4], xdt.rearrange("p a (g d) -> p (a g) d", g=2), AX.X).then_inc(ev("ssd_var"), 1)
            dve.wait_ge(ev("ssd_std"), 1)
            step(dve.reciprocal(hstd[:, 1, 0:4], hstd[:, 0, 0:4]))
            for tt in range(TT):
                y = nat[:, tt, 0:512].rearrange("p (g d) -> p g d", g=2)
                TTn(y, y, hstd[:, 1, 2 * tt:2 * tt + 2].unsqueeze(2).to_broadcast([P, 2, 256]), ALU.mult).then_inc(nat_ready, 1)
            dve.wait_ge(nat_ready, 2 * TR["o_even"] + 2)
            dve.sem_inc(ev("ssd_done"), 1)
            transposed("o_even", lambda c: cols[:, C_SSDN + c:C_SSDN + c + 1], groups=2, direct=True)

            def s5_out(m):
                dve.wait_ge(ev("s5_used"), 4 * m + 4)
                STT(yT[:, m, :], uT[:, m, :], cols[:, C_S5D + m:C_S5D + m + 1], bank[2 + m % 2][:, 0:T], ALU.mult, ALU.add)\
                    .then_inc(ev("s5_y"), 1)

            for i in range(16):
                a_, b_, g_, pc, ps = (s5w[i % 2][:, n, :] for n in range(5))
                two = lambda z: z.rearrange("p (r t) -> p r t", r=2)
                C2 = cosT[:, i, :].unsqueeze(1).to_broadcast([P, 2, T])
                S1, d = sinT[:, i, :], bank[6 + i % 2]
                lo, hi = slice(0, T), slice(T, 2 * T)
                dve.wait_ge(ev("s5_drive"), i + 1)
                if i >= 2:
                    dve.wait_ge(ev("s5_used"), i - 1)
                TTn(two(a_), two(d[:]), C2, ALU.mult)
                STT(b_[:, lo], d[:, hi], -1.0, S1, ALU.mult, ALU.mult)
                step(TTn(b_[:, hi], d[:, lo], S1, ALU.mult))
                step(TTn(a_, a_, b_, ALU.add))
                mag = s5c[:, 4, i:i + 1].to_broadcast([P, T])
                dve.tensor_tensor_scan(g_[:, lo], mag, a_[:, lo], 0.0, ALU.mult, ALU.add)
                dve.tensor_tensor_scan(g_[:, hi], mag, a_[:, hi], 0.0, ALU.mult, ALU.add).then_inc(ev("s5_state"), 1)
                dve.wait_ge(ev("s5_state"), i + 1)
                TTn(pc[:, lo], g_[:, lo], cosT[:, i, :], ALU.mult)
                STT(pc[:, hi], g_[:, hi], -1.0, cosT[:, i, :], ALU.mult, ALU.mult).then_inc(ev("s5_cos"), 1)
                if i % 4 == 0 and i:
                    s5_out(i // 4 - 1)
            s5_out(3)
            for o in range(4):
                dve.wait_ge(ev("sig_done"), o + 1)
                last = TTn(t32[:, 4 + o, :], yT[:, o, :], sig[:, o, :], ALU.mult)
                if o % 2:
                    last.then_inc(t32_ready, 1)
            for g in (2, 3):
                lower_part(TR["o_even"], g)

        def odd_pe(pe, mm, transposed, attention):
            pe.wait_ge(proj_evac, PROJ["odd"] + 8 + EVAC0)
            for i, src in enumerate((qn, kn)):
                pe.wait_ge(ev("qk_norm"), i + 1)
                for c in range(4):
                    b = bank[2 * i + c // 2]
                    for tt in range(TT):
                        at = (c % 2) * T + tt * P
                        last = pe.transpose(b[:, at:at + P], src[:, tt, c * P:c * P + P], ident[:])
                last.then_inc(ev("qk_tr"), 1)
            pe.wait_ge(ev("q_done"), 1)
            pe.wait_ge(ev("k_done"), 1)
            attention("odd")
            transposed("o_odd", nat, 4)
            pe.wait_ge(ev("pool_in"), 16)
            pe.wait_ge(ev("pooled"), 4)
            for g in range(4):
                last = mm(bank[6 + g // 2][:, (g % 2) * T:(g % 2) * T + T], wpool[:, g, :], pooled[g], start=True, stop=True)
            last.then_inc(ev("pool_mm"), 1)

        def odd_act(act_e, A, transposed, upper_part, attention):
            act_e.wait_ge(ev("qk_var"), 1)
            A(hstd[:], hstat[:], ACT.Sqrt, bias=eps_rms, scale=1.0 / HD).then_inc(ev("qk_std"), 1)
            act_e.wait_ge(ev("qk_tr"), 1)
            for b in range(2):
                last = A(qT[:, 2 * b:2 * b + 2, :], bank[b][:].rearrange("p (c t) -> p c t", c=2), ACT.Copy,
                         scale=cols[:, C_QN:C_QN + 1])
            last.then_inc(ev("q_done"), 1)
            attention("odd")
            transposed("o_odd", groups=2, direct=True)
            act_e.wait_ge(ev("pool_mm"), 1)
            for g in range(4):
                last = A(t32[:, 4 + g, :], bank[6 + g // 2][:, (g % 2) * T:(g % 2) * T + T], ACT.Copy,
                         scale=cols[:, C_PSCALE + g:C_PSCALE + g + 1])
                if g % 2:
                    last.then_inc(t32_ready, 1)
            upper_part("o_odd", 2)
            upper_part("o_odd", 3)

        def odd_dve(dve, step, split_py, transposed, lower_part, attention):
            TTn, TS = dve.tensor_tensor, dve.tensor_scalar
            for u in range(8):
                split_py(START["odd"] + u + RING)
            dve.wait_ge(proj_evac, PROJ["odd"] + 4 + EVAC0)
            for i, z in enumerate((qn, kn)):
                step(TTn(sq8, z, z, ALU.mult))
                last = dve.reduce_sum(hstat[:, i, :], sq8.rearrange("p a (h d) -> p (a h) d", d=HD), AX.X)
                if i == 0:
                    step(last)
            last.then_inc(ev("qk_var"), 1)
            dve.wait_ge(ev("qk_std"), 1)
            step(dve.reciprocal(hstat[:], hstd[:]))
            for i, z in enumerate((qn, kn)):
                zh = z.rearrange("p a (h d) -> p (a h) d", d=HD)
                TTn(zh, zh, hstat[:, i, :].unsqueeze(2).to_broadcast([P, 16, HD]), ALU.mult).then_inc(ev("qk_norm"), 1)
            dve.wait_ge(ev("qk_tr"), 2)
            for b in range(2):
                last = TS(kT[:, 2 * b:2 * b + 2, :], bank[2 + b][:].rearrange("p (c t) -> p c t", c=2),
                          cols[:, C_KN:C_KN + 1], None, ALU.mult)
            last.then_inc(ev("k_done"), 1)
            dve.wait_ge(ev("band_mask"), 1)
            attention("odd")
            dve.wait_ge(o_done, HEAD0["odd"] + len(HEADS["odd"]))
            dve.sem_inc(nat_ready, 2)
            transposed("o_odd", groups=2, direct=True)
            for g in (2, 3):
                lower_part(TR["o_odd"], g)

        POOL_WINDOWS = (2, 4, 8, 16)
        pooled = [pool_s[0][:, 0, :], pool_s[1][:, 1, :], pool_s[2][:, 2, :], pool_s[0][:, 3, :]]

        def pooling(pool, step):
            pool.wait_ge(proj_evac, PROJ["odd"] + 8 + EVAC0)
            src, at = uTo, 0
            for n, dst in enumerate((pool_s[0], pool_s[1], pool_s[2], pool_s[0])):
                k = 1 << n
                step(pool.tensor_copy(dst[:, n:4, 0:k], src[:, n:4, 0:k]))
                step(pool.tensor_tensor(dst[:, n:4, k:T], src[:, n:4, k:T], src[:, n:4, 0:T - k], ALU.add))
                src = dst
            for g, (w, z) in enumerate(zip(POOL_WINDOWS, pooled)):
                step(pool.tensor_scalar(z[:, 16:T], z[:, 16:T], 1.0 / w, None, ALU.mult))
                step(pool.tensor_tensor(z[:, 0:16], z[:, 0:16], poolc[:, 16 * g:16 * g + 16], ALU.mult))
                pool.tensor_tensor(z, z, uTo[:, g, :], ALU.subtract).then_inc(ev("pooled"), 1)

        block = ctx.enter_context(nc.Block())

        @block.sync
        def _(sp):
            def unit(slot, n, src):
                sp.wait_ge(lo_ready, n + (LO0 - RING + 1))
                sp.dma_start(raw[:, slot, :].rearrange("p (k c) -> p k c", k=src.shape[1]), src)\
                    .then_inc(raw_full[slot], 16)

            def qkv(name, w):
                n0 = START[name]
                with sp.Fori(0, 2) as m:
                    with sp.Fori(0, 2) as j:
                        it = m * 2 + j
                        for u in range(3):
                            unit((n0 + u) % RING, it * 3 + (n0 + u),
                                 col_unit(w, m * 1536 + j * 256 + 512 * u))

            def straight(name, units):
                for u, src in enumerate(units):
                    n = START[name] + u
                    unit(n % RING, n, src)

            def ffn(name):
                wg, g0, wu, u0, wd = ffn_w[name]
                n0 = START[name]
                unit(n0 % RING, n0, col_unit(wg, g0))
                unit((n0 + 1) % RING, n0 + 1, col_unit(wu, u0))

                def body(i):
                    n = i * 3 + (n0 - 1)
                    unit((n0 + 2) % RING, n, col_unit(wg, i * UC + g0))
                    unit((n0 + 3) % RING, n + 1, row_unit(wd, i * UC - UC))
                    unit((n0 + 4) % RING, n + 2, col_unit(wu, i * UC + u0))

                with sp.Fori(1, FC) as i:
                    body(i)
                n = n0 + 32
                unit(n % RING, n, row_unit(wd, FF - UC))

            def first_ada(b, reused):
                if reused:
                    sp.wait_ge(ada_step[b % 2], 8)
                sp.dma_start(ada_b[0:1, b % 2, :], a["b_ada"][0:1, 512 * b:512 * b + 512]).then_inc(ev(f"ada_in{b}"), 16)
                sp.dma_start(first_raw[b], a["w_ada"][0][:, 512 * b:512 * b + 512].rearrange("(k p) c -> p k c", p=P))\
                    .then_inc(ev(f"ada_in{b}"), 16)

            sp.wait_ge(ev("ada_b_zero"), 1)
            first_ada(0, False)
            first_ada(1, False)
            sp.dma_start(x[:], a["x"][0].rearrange("(a p) d -> p a d", p=P)).then_inc(ev("x_in"), 16)
            first_ada(2, True)
            first_ada(3, True)
            qkv("ab", a["w_in_ab"][0])
            straight("o_ab", [row_unit(o_w["o_ab"], UC * u) for u in range(4)])
            ffn("ff0")
            qkv("cd", a["w_in_cd"][0])
            straight("o_cd", [row_unit(o_w["o_cd"], UC * u) for u in range(4)])
            ffn("ff1")
            ffn("f1a")
            straight("even", [col_unit(a["even_w_in_2"][0], c) for c in EVEN_COLS])
            straight("o_even", [row_unit(o_w["o_even"], UC * u) for u in range(4)])
            ffn("f2a")
            ffn("f1b")
            straight("odd", [col_unit(a["odd_w_in_2"][0], c) for c in ODD_COLS])
            straight("o_odd", [row_unit(o_w["o_odd"], UC * u) for u in range(4)])
            ffn("f2b")
            sp.wait_ge(ev("x_final"), 2)
            sp.dma_start(out[0].rearrange("(a p) d -> p a d", p=P), x[:]).then_inc(out_done, 16)
            sp.wait_ge(out_done, 16)

        @block.gpsimd
        def _(pool):
            step = Chain(pool, g_step)

            def load(dst, src, s=setup_in):
                pool.dma_start(dst, src).then_inc(s, 16)

            def ada(l, slot, c0, used):
                pool.wait_ge(ada_step[slot], used)
                pool.dma_start(ada_b[0:1, slot, :], a["b_ada"][l:l + 1, bass.ds(c0, 512)]).then_inc(ada_full[slot], 16)
                pool.dma_start(ada_raw[:, slot, :].rearrange("p (k c) -> p k c", k=KC),
                               a["w_ada"][l][:, bass.ds(c0, 512)].rearrange("(k p) c -> p k c", p=P))\
                    .then_inc(ada_full[slot], 16)

            load(onehot, a["k_onehot"])
            load(addc, a["k_add"])
            load(table[:, 0:12], a["rel_bias"])
            load(table[:, 12:20], a["rel_bias"][:, 0:8])
            load(relrow, a["attn_rel_bias_2"][0])
            load(lamrow, a["diff_lambda"].rearrange("o a d -> o (a d)"))
            load(a8[:, 0:1], a["forget_b"].rearrange("o h -> h o"))
            load(a8[:, 1:2], a["ssd_dt_bias_2"].rearrange("o h -> h o"))
            load(a8[:, 2:3], a["ssd_a_log_2"].rearrange("o h -> h o"))
            load(dsk, a["ssd_d_2"].to_broadcast([P, 8]))
            load(poolc[:], a["k_pool"].to_broadcast([P, 64]))
            load(flip[:], a["k_flip"])
            load(lower[:], a["k_lower"])
            load(upper[:], a["k_upper"])
            load(wsmall[:, 0], a["w_in_cd"][0][:, 3072:3080].rearrange("(k p) c -> p k c", p=P), ev("narrow_in"))
            load(wsmall[:, 1], a["even_w_in_2"][0][:, 1536:1544].rearrange("(k p) c -> p k c", p=P), ev("narrow_in"))
            pool.wait_ge(ev("toep_rows"), 2)
            pool.dma_start(toep.ap()[0:20, :], toepA).then_inc(toep_out, 16)
            pool.dma_start(toep.ap()[20:28, :], toepE).then_inc(toep_out, 16)
            pool.wait_ge(toep_out, 32)
            pool.wait_ge(ev("cols_ready"), 2)
            pool.dma_start(bias[:, 0:12, :], toep_tile(0, 12)).then_inc(toep_in, 16)
            pool.wait_ge(ada_step[1], 16)
            with pool.Fori(0, 2) as m:
                with pool.Fori(0, 2) as j:
                    it = m * 2 + j
                    ada(0, 0, m * 3072 + j * 512 + 2048, it * 8 + 16)
                    ada(0, 1, it * 512 + 3072, it * 8 + 16)

            def load_ln(l, n):
                pool.dma_start(lnv[:, 0, :], a["ln_g"][l, n:n + 1, :].to_broadcast([P, D])).then_inc(ln_loaded, 16)
                pool.dma_start(lnv[:, 1, :], a["ln_b"][l, n:n + 1, :].to_broadcast([P, D])).then_inc(ln_loaded, 16)

            for l in range(2):
                pool.wait_ge(nat_ready, 2 * TR[("o_ab", "o_cd")[l]] + 2)
                load_ln(l, 0)
                if l == 0:
                    pool.dma_start(bias[:, 0:8, :], toep_tile(12, 8)).then_inc(toep_in, 16)
                    with pool.Fori(0, 2) as m:
                        with pool.Fori(0, 4) as j:
                            ada(1, 1, m * 3072 + j * 512, (m * 4 + j) * 8 + 48)
                pool.wait_ge(ln_used, 2 * l + 1)
                load_ln(l, 1)
                if l == 0:
                    with pool.Fori(0, 2) as m:
                        with pool.Fori(0, 2) as j:
                            ada(1, 0, m * 3072 + j * 512 + 2048, (m * 2 + j) * 8 + 48)

            pool.wait_ge(nat_ready, 2 * TR["f1a"] + 2)
            load(bbin[:, 0], a["s5_b_re_2"][0].rearrange("(n g) p i -> (g p) n i", g=2), ev("s5_in"))
            load(bbin[:, 1], a["s5_b_im_2"][0].rearrange("(n g) p i -> (g p) n i", g=2), ev("s5_in"))
            pool.memset(Cpad[:], 0.0).then_inc(ev("cpad_zero"), 1)
            step(pool.memset(BP[:], 0.0))
            pool.wait_ge(ev("cpad_zero"), 1)
            for ri, c in enumerate(("s5_c_re_2", "s5_c_im_2")):
                for g in range(8):
                    load(Cpad[16 * g:16 * g + 16, ri, :, 64 * (g % 2):64 * (g % 2) + 64],
                         a[c][0].rearrange("(m g) i p -> g i m p", g=8)[g], ev("s5_in"))
            step(pool.memset(cosT[:, :, 0:1], 1.0))
            step(pool.memset(sinT[:, :, 0:1], 0.0))
            step(pool.tensor_copy(cosT[:, :, 1:2], s5c[:, 0, :].unsqueeze(2)))
            step(pool.tensor_copy(sinT[:, :, 1:2], s5c[:, 1, :].unsqueeze(2)))
            k = 1
            while k < T // 2:
                def times(dst, lo, hi, n):
                    c1, s1 = cosT[:, :, lo:lo + n], sinT[:, :, lo:lo + n]
                    ck, sk = (t[:, :, hi:hi + 1].to_broadcast([P, 16, n]) for t in (cosT, sinT))
                    p0, p1 = tabt[:, 0, :, 0:n], tabt[:, 1, :, 0:n]
                    step(pool.tensor_tensor(p0, c1, ck, ALU.mult))
                    step(pool.tensor_tensor(p1, s1, sk, ALU.mult))
                    step(pool.tensor_tensor(cosT[:, :, dst:dst + n], p0, p1, ALU.subtract))
                    step(pool.tensor_tensor(p0, c1, sk, ALU.mult))
                    step(pool.tensor_tensor(p1, s1, ck, ALU.mult))
                    step(pool.tensor_tensor(sinT[:, :, dst:dst + n], p0, p1, ALU.add))

                times(2 * k, k, k, 1)
                times(2 * k + 1, 1, 2 * k, 2 * k - 1)
                k *= 2
            pool.wait_ge(ev("s5_in"), 16 * 18)
            fr, fi = (s5c[:, n, :].unsqueeze(2).to_broadcast([P, 16, 16]) for n in (2, 3))
            br, bi = bbin[:, 0], bbin[:, 1]
            for ri, (one, two, op) in enumerate(((br, bi, ALU.subtract), (bi, br, ALU.add))):
                step(pool.tensor_tensor(bbt[:, 0], one, fr, ALU.mult))
                step(pool.tensor_tensor(bbt[:, 1], two, fi, ALU.mult))
                for g in range(2):
                    rows_g = slice(64 * g, 64 * g + 64)
                    last = pool.tensor_tensor(BP[rows_g, ri, :, 16 * g:16 * g + 16], bbt[rows_g, 0], bbt[rows_g, 1], op)
                    if g == 0 or ri == 0:
                        step(last)
            last.then_inc(ev("bp_ready"), 1)
            pool.wait_ge(ev("ssd_done"), 1)
            load(wglu, a["s5_w_glu_2"][0].rearrange("(k p) n -> p k n", p=P), ev("glu_in"))
            for i in range(16):
                pool.wait_ge(ev("s5_state"), i + 1)
                g_, ps = (s5w[i % 2][:, n, :].rearrange("p (r t) -> p r t", r=2) for n in (2, 4))
                pool.tensor_tensor(ps, g_, sinT[:, i, :].unsqueeze(1).to_broadcast([P, 2, T]), ALU.mult)\
                    .then_inc(ev("s5_sine"), 1)
            pool.wait_ge(nat_ready, 2 * TR["f2a"] + 2)
            pool.dma_start(bias[:, 0:8, :], toep_tile(20, 8)).then_inc(toep_in, 16)
            load(wpool, a["pool_w_2"][0].rearrange("g i o -> i g o"), ev("pool_in"))
            pool.wait_ge(flip_out, FLIP0["odd"] + 4)
            pool.memset(bias[0:64, 0:8, 192:256], NEG).then_inc(ev("band_mask"), 1)
            pooling(pool, step)

        @block.scalar
        def _(act_e):
            step = Chain(act_e, a_step)
            A = act_e.activation

            def split(slot, n, turn):
                if isinstance(n, int) and n >= UNITS:
                    return
                act_e.wait_ge(raw_full[slot], turn * 16)
                act_e.wait_ge(unit_used, n + (USED0 - RING + 1))
                A(wH[:, slot, :], raw[:, slot, :], ACT.Copy).then_inc(hi_ready, 1)

            def split_py(n):
                split(n % RING, n, n // RING + 1)

            def ada_evac(slot, cnt, gdst=None, cdst=None, b=None):
                act_e.wait_ge(ada_mm[slot], cnt + 2)
                if gdst is not None:
                    A(gdst, bank[7][:], ACT.Copy, bias=1.0).then_inc(ada_out[slot], 1)
                else:
                    A(cdst, bank[b or (0, 3)[slot]][:, 0:4], ACT.Copy).then_inc(ada_out[slot], 1)

            def upper_part(name, g):
                if name in T32_ODD and g % 2:
                    act_e.wait_ge(t32_odd, T32_ODD[name] + g // 2 + 1)
                else:
                    act_e.wait_ge(t32_ready, T32[name] + (g // 2 if name in T32_ODD else g) + 1)
                A(hH[:, 2 * g:2 * g + 2, :], t32[:, 2 * g:2 * g + 2, :], ACT.Copy).then_inc(th_ready, 1)

            def transposed(name, scale=None, offset=0.0, groups=4, direct=False):
                for g in range(groups):
                    if not direct:
                        if g % 2 == 0:
                            act_e.wait_ge(tr_done, TRD[name] + g + 2)
                            for c in (2 * g + 2, 2 * g + 3):
                                last = A(t32[:, c, :], bank[5 + g][:, (c % 2) * T:(c % 2) * T + T], ACT.Identity,
                                         scale=scale(c), bias=offset(c) if offset else 0.0)
                            last.then_inc(t32_odd, 1)
                        upper_part(name, g)
                        continue
                    act_e.wait_ge(tr_done, TRD[name] + g + 1)
                    for c in (2 * g, 2 * g + 1):
                        last = A(hH[:, c, :], bank[4 + g][:, (c % 2) * T:(c % 2) * T + T], ACT.Copy,
                                 scale=scale(c) if scale else 1.0)
                    last.then_inc(th_ready, 1)

            def sqrt_table():
                step(A(small[:, 139:140], eps_ln, ACT.Sqrt))

            def qkv(name, l):
                n0, u0 = START[name], PROJ[name]
                with act_e.Fori(0, 2) as m:
                    with act_e.Fori(0, 2) as j:
                        it = m * 2 + j
                        for u in range(3):
                            n = n0 + u
                            act_e.wait_ge(unit_used, it * 3 + (n + USED0 + 1))
                            src = bank[4 + u][:].rearrange("p (a t) -> p a t", a=2)
                            if u == 0:
                                A(qT[:, bass.ds(it * 2, 2), :], src, ACT.Copy, scale=ATTN_SCALE).then_inc(proj_evac, 1)
                            elif u == 1:
                                A(kT[:, bass.ds(it * 2, 2), :], src, ACT.Copy).then_inc(proj_evac, 1)
                            else:
                                A(v[:, :, bass.ds(it * UC, UC)], src, ACT.Copy).then_inc(proj_evac, 1)
                            split(n % RING, it * 3 + (n + RING), it + ((n + RING) // RING + 1))
                        g1 = gate1[:, bass.ds(m, 1), bass.ds(j * 512, 512)]
                        if l == 0:
                            ada_evac(0, it + 2, gdst=g1)
                            ada_evac(1, it + 2, cdst=adaC[:, 0, bass.ds(it * 4 + 16, 4)])
                        else:
                            ada_evac(0, it + 6, gdst=g1)

            def flipped(name):
                for n in range(FLIPS[name]):
                    act_e.wait_ge(flip_mm, FLIP0[name] + n + 1)
                    A(bias[:, 2 * n:2 * n + 2, :], bank[FLIP_BANK[name] + n % 3][:].rearrange("p (h t) -> p h t", h=2), ACT.Copy)\
                        .then_inc(flip_out, 1)

            def attention(name):
                g0, heads = HEAD0[name], HEADS[name]

                def probs(g):
                    act_e.wait_ge(s_max, g + 1)
                    for tt, (lo, hi) in enumerate(((0, 128), (128, 384))):
                        last = A(sP[:, g % 3, lo:hi], sP[:, g % 3, lo:hi], ACT.Exp, scale=-1.0,
                                 bias=mx[:, g % 3, tt:tt + 1], accum_out=sums[:, g % 4, tt:tt + 1])
                    last.then_inc(p_ready, 1)

                def copy_pT(g):
                    act_e.wait_ge(pT_ready, g + 1)
                    if g >= 2:
                        act_e.wait_ge(o_ready, g - 1)
                    A(PT[:, g % 2, :], bank[3 + g % 2][:, 0:384], ACT.Copy).then_inc(pT_copied, 1)

                for s in range(len(heads) + 2):
                    if s < len(heads):
                        probs(g0 + s)
                    if s >= 2:
                        copy_pT(g0 + s - 2)

            def ffn(name, with_ada=False):
                n0, f = START[name], 11 * FFN[name]

                def hidden(i):
                    act_e.wait_ge(act_mul, i + (f + 1))
                    A(aH[:], act.rearrange("p (a t) -> p a t", a=2), ACT.Copy).then_inc(act_hi, 1)

                def silu(i):
                    act_e.wait_ge(act_mul, i + f) if not (isinstance(i, int) and i + f == 0) else None
                    A(sil, bank[4][:], ACT.Silu).then_inc(sil_done, 1)

                act_e.wait_ge(unit_used, n0 + USED0 + 1)
                silu(0)
                split_py(n0 + 3)
                act_e.wait_ge(unit_used, n0 + USED0 + 2)
                hidden(0)
                split_py(n0 + 4)

                def body(i):
                    n = i * 3 + (n0 - 1)
                    s, turn = n0 + 2, i + ((n0 + 2) // RING + 1)
                    act_e.wait_ge(unit_used, n + (USED0 + 1))
                    silu(i)
                    split((s + 3) % RING, n + 3, i + ((n0 + 5) // RING))
                    split((s + 4) % RING, n + 4, i + ((n0 + 6) // RING))
                    hidden(i)
                    split((s + 5) % RING, n + 5, i + ((n0 + 7) // RING))

                if with_ada:
                    with act_e.Fori(0, 2) as m:
                        with act_e.Fori(0, 4) as j:
                            b = m * 4 + j
                            body(b + 1)
                            ada_evac(1, b + 6, cdst=adaC[:, 1, bass.ds(b * 4, 4)], b=7)
                with act_e.Fori(9 if with_ada else 1, FC - 1) as i:
                    body(i)
                body(FC - 1)
                sqrt_table()

            def root(e, scale, eps):
                for tt in range(TT):
                    if e < 4:
                        act_e.wait_ge(var_ready, 2 * e + tt + 1)
                        src = mv[:, tt, 1:2]
                    else:
                        if e == 4:
                            act_e.wait_ge(ev("x_done"), 7 + tt)
                        else:
                            act_e.wait_ge(ev("x_sum"), 2 * (e - 5) + tt + 1)
                        src = xss[:, tt:tt + 1]
                        step(A(nat[:, tt, :], x[:, tt, :], ACT.Square, accum_out=src))
                    A(std[:, tt:tt + 1], src, ACT.Sqrt, bias=eps, scale=scale or 1.0).then_inc(std_ready, 1)

            def load(dst, src):
                act_e.dma_start(dst, src).then_inc(ev("rows_in"), 16)

            act_e.dma_start(ident[:], a["k_ident"]).then_inc(ev("first_in"), 16)
            act_e.dma_start(rows_c, a["c"].rearrange("o (k p) -> (o k) p", p=P)).then_inc(ev("first_in"), 16)
            for at, src in ((C_FF1, a["ffn1_norm_2"]), (C_MIX, a["mix_norm_2"]), (C_FF2, a["ffn2_norm_2"]),
                            (C_CONVB, a["ssd_conv_b_2"]), (C_CONVW, a["ssd_conv_w_2"][0]), (C_SSDN, a["ssd_norm_2"]),
                            (C_GLUB, a["s5_b_glu_2"]), (C_PSCALE, a["pool_scale_2"]), (C_SUBLN, a["diff_subln_g"])):
                n = int(np.prod(src.shape)) // P
                load(rows[at:at + n, :], src.rearrange("a (k p) -> (a k) p", p=P))
            load(rows[C_S5D:C_S5D + 4, :], a["s5_d_2"][0].rearrange("(m g) i -> m (g i)", m=4))
            for at, src in ((C_QN, a["attn_q_norm_2"]), (C_KN, a["attn_k_norm_2"])):
                load(rows[at:at + 1, 0:HD], src)
                load(rows[at:at + 1, HD:P], src)
            load(rowC[0:16, :], a["s5_a_re_2"][0].rearrange("(n g) p -> n (g p)", g=2))
            load(rowC[16:32, :], a["s5_a_im_2"][0].rearrange("(n g) p -> n (g p)", g=2))
            load(rowL[0:32, :], a["ln_g"].rearrange("l n (k p) -> (l n k) p", p=P))
            load(rowL[32:64, :], a["ln_b"].rearrange("l n (k p) -> (l n k) p", p=P))
            load(dt2, a["s5_log_dt_2"][0].rearrange("(n g) -> n g", g=2))
            act_e.wait_ge(ev("c_cols"), 1)
            A(silc[:], bank[0][:, 0:8], ACT.Silu).then_inc(ev("silc"), 1)
            def first_ada(b):
                ada_evac(b % 2, b // 2, cdst=adaC[:, 0, 4 * b:4 * b + 4])

            first_ada(0)
            first_ada(1)
            act_e.wait_ge(ev("lam_sums"), 1)
            A(lam[0:1, 2:4], lam[0:1, 0:2], ACT.Exp).then_inc(ev("lam_exp"), 1)
            act_e.wait_ge(ev("cols_ready"), 2)
            step(A(s5c[:, 6, :], colC[:, 32:48], ACT.Exp))
            A(small[0:8, 175:176], a8[:, 2:3], ACT.Exp).then_inc(ev("s5_dt"), 1)
            act_e.wait_ge(ev("s5_angle"), 1)
            step(A(s5c[:, 4, :], s5c[:, 7, :], ACT.Exp))
            first_ada(2)
            A(s5c[:, 9, :], s5c[:, 8, :], ACT.Sin, scale=0.5).then_inc(ev("s5_sin"), 1)
            A(s5c[:, 1, :], s5c[:, 8, :], ACT.Sin).then_inc(ev("s5_sin"), 1)
            first_ada(3)
            act_e.wait_ge(ev("scale_ready"), 1)
            transposed("ab", lambda c: adaC[:, 0, 8 + c:9 + c], lambda c: adaC[:, 0, c:c + 1])
            for n in range(RING):
                split_py(n)

            flipped("ab")
            e = 0
            for l, (p, o, f) in enumerate((("ab", "o_ab", "ff0"), ("cd", "o_cd", "ff1"))):
                joined = lambda at, e: (lambda c: lnS[:, e, at + c:at + c + 1])
                if l == 1:
                    transposed(p, joined(0, 1), joined(8, 1))
                    split_py(START[p] + 2)
                    act_e.wait_ge(ev("fd_abs"), 1)
                    step(A(F8[0], F8[0], ACT.Exp))
                    A(F8[0], F8[0], ACT.Ln, bias=1.0).then_inc(ev("fd_ln"), 1)
                    act_e.wait_ge(ev("fd_cum"), 1)
                    A(head_one, ident[0:8, 0:8], ACT.Copy)
                    A(F8H, F8[3], ACT.Copy).then_inc(ev("forget_hi"), 1)
                qkv(p, l)
                attention(p)
                if l == 0:
                    act_e.wait_ge(ev("sub_var"), 1)
                    A(hstd[:, 0, 0:8], hstat[:, 0, 0:8], ACT.Sqrt, bias=eps_ln, scale=1.0 / P).then_inc(ev("sub_std"), 1)
                transposed(o, (lambda c: cols[:, C_SUBLN:C_SUBLN + 1] if c < 4 else 1.0) if l == 0 else None, direct=True)
                sqrt_table()
                for u in range(3):
                    split_py(START[o] + u + RING)
                if l == 0:
                    flipped("cd")
                root(e, None, eps_ln)
                transposed(f, joined(0, e), joined(8, e))
                split_py(START[f] + 2)
                ffn(f, with_ada=(l == 0))
                root(e + 1, None, eps_ln)
                e += 2
            for l, (f1, p, o, f2) in enumerate((("f1a", "even", "o_even", "f2a"), ("f1b", "odd", "o_odd", "f2b"))):
                if l == 1:
                    flipped("odd")
                gain = lambda at, l=l: (lambda c: cols[:, at + 8 * l + c:at + 8 * l + c + 1])
                root(e, 1.0 / D, eps_rms)
                transposed(f1, gain(C_FF1), direct=True)
                split_py(START[f1] + 2)
                ffn(f1)
                root(e + 1, 1.0 / D, eps_rms)
                if l == 0:
                    act_e.wait_ge(ev("s5_tr"), 1)
                    A(RB[:, 0], bank[4][:].rearrange("p (m n) -> p m n", m=4), ACT.Copy)
                    A(RB[:, 1], bank[5][:].rearrange("p (m n) -> p m n", m=4), ACT.Copy, scale=-1.0)
                    A(CT[:, 0], bank[6][:].rearrange("p (m n) -> p m n", m=4), ACT.Copy)
                    A(CT[:, 1], bank[7][:].rearrange("p (m n) -> p m n", m=4), ACT.Copy, scale=-1.0).then_inc(ev("s5_bc"), 1)
                transposed(p, gain(C_MIX), direct=(l == 1))
                split_py(START[p] + 2)
                if l == 0:
                    act_e.wait_ge(ev("dt_abs"), 1)
                    step(A(sp8[0], sp8[0], ACT.Exp))
                    A(sp8[0], sp8[0], ACT.Ln, bias=1.0).then_inc(ev("dt_ln"), 1)
                for u in range(8):
                    n, k = START[p] + u, PROJ[p] + u
                    act_e.wait_ge(unit_used, n + USED0 + 1)
                    src = bank[4 + k % 3][:].rearrange("p (a t) -> p a t", a=2)
                    if l == 0:
                        dst = (zn[:, :, 256 * u:256 * u + 256] if u < 2 else
                               xpad[:, 2 * u - 4:2 * u - 2, 3:259] if u < 6 else uT[:, 2 * u - 12:2 * u - 10, :])
                    else:
                        dst = (qn, kn, v)[u // 2][:, :, 256 * (u % 2):256 * (u % 2) + 256] if u < 6 else \
                            uTo[:, 2 * u - 12:2 * u - 10, :]
                    A(dst, src, ACT.Copy).then_inc(proj_evac, 1)
                    split_py(n + RING)
                if l == 0:
                    even_act(act_e, A, transposed, upper_part)
                else:
                    odd_act(act_e, A, transposed, upper_part, attention)
                sqrt_table()
                for u in range(3):
                    split_py(START[o] + u + RING)
                root(e + 2, 1.0 / D, eps_rms)
                transposed(f2, gain(C_FF2), direct=True)
                split_py(START[f2] + 2)
                ffn(f2)
                e += 3

        @block.vector
        def _(dve):
            step = Chain(dve, v_step)
            TTn, TS, STT = dve.tensor_tensor, dve.tensor_scalar, dve.scalar_tensor_tensor

            def split(slot, n):
                if isinstance(n, int) and n >= UNITS:
                    return
                dve.wait_ge(hi_ready, n + 1)
                TTn(wL[:, slot, :], raw[:, slot, :], wH[:, slot, :].bitcast(F32), ALU.subtract).then_inc(lo_ready, 1)

            def split_py(n):
                split(n % RING, n)

            def ada(slot, cnt, first=None):
                if first is None:
                    dve.wait_ge(ada_full[slot], cnt * 32 - 32)
                else:
                    dve.wait_ge(ev(f"ada_in{first}"), 32)
                dve.wait_ge(ada_mm[slot], cnt + 1)
                acc = ada_acc[:, slot, :]
                for k in range(KC):
                    src = ada_raw[:, slot, 512 * k:512 * k + 512] if first is None else first_raw[first][:, k, :]
                    if k:
                        dve.wait_ge(ada_step[slot], cnt * 8 + k)
                    STT(acc, src, silc[:, k:k + 1], ada_b[:, slot, :] if k == 0 else acc, ALU.mult, ALU.add)\
                        .then_inc(ada_step[slot], 1)

            def lower_part(r, g):
                dve.wait_ge(th_ready, 4 * r + g + 1)
                TTn(hL[:, 2 * g:2 * g + 2, :], t32[:, 2 * g:2 * g + 2, :], hH[:, 2 * g:2 * g + 2, :].bitcast(F32),
                    ALU.subtract).then_inc(tl_ready, 1)

            def transposed(name, scale=None, offset=None, whole=True, groups=4, direct=False):
                r, base = TR[name], TRD[name]
                if direct:
                    for g in range(groups):
                        dve.wait_ge(th_ready, 4 * r + g + 1)
                        for c in (2 * g, 2 * g + 1):
                            src, upper_c = bank[4 + g][:, (c % 2) * T:(c % 2) * T + T], hH[:, c, :].bitcast(F32)
                            if scale:
                                last = STT(hL[:, c, :], src, scale(c), upper_c, ALU.mult, ALU.subtract)
                            else:
                                last = TTn(hL[:, c, :], src, upper_c, ALU.subtract)
                        last.then_inc(tl_ready, 1)
                    return
                if whole:
                    dve.wait_ge(tr_done, base + groups)
                for g in range(groups):
                    if g % 2 and groups == 4:
                        lower_part(r, g - 1)
                        continue
                    dve.wait_ge(tr_done, base + g + 1)
                    for c in (2 * g, 2 * g + 1):
                        src, dst = bank[4 + g][:, (c % 2) * T:(c % 2) * T + T], t32[:, c, :]
                        sc = scale(c) if scale else None
                        if offset:
                            last = TS(dst, src, sc, offset(c), ALU.mult, ALU.add)
                        elif sc is not None:
                            last = TS(dst, src, sc, None, ALU.mult)
                        else:
                            last = dve.tensor_copy(dst, src)
                    last.then_inc(t32_ready, 1)
                    if g:
                        lower_part(r, g - 1)
                lower_part(r, groups - 1)

            def qkv(name, l):
                n0 = START[name]
                with dve.Fori(0, 2) as m:
                    with dve.Fori(0, 2) as j:
                        it = m * 2 + j
                        ada(0, it + (2 if l == 0 else 6))
                        split(n0 % RING, it * 3 + (n0 + 3))
                        if l == 0:
                            ada(1, it + 2)
                        split((n0 + 1) % RING, it * 3 + (n0 + 4))
                        split((n0 + 2) % RING, it * 3 + (n0 + 5))

            def attention(name):
                g0, heads = HEAD0[name], HEADS[name]
                nfox = [0]

                def maxima(i):
                    g = g0 + i
                    b = heads[i][4]
                    dve.wait_ge(s_ready, g + 1)
                    if b is None:
                        h, fb = nfox[0], foxb[:, g % 2, :]
                        nfox[0] += 1
                        STT(fb[:, 0:128], lower[:], ccol[:, 0, h:h + 1], bank[7][:, 0:128], ALU.add, ALU.subtract)
                        TS(fb[:, 128:256], bank[7][:, 0:128], -1.0, ccol[:, 1, h:h + 1], ALU.mult, ALU.add)
                        STT(fb[:, 256:384], lower[:], ccol[:, 1, h:h + 1], bank[7][:, 128:256], ALU.add, ALU.subtract)\
                            .then_inc(ev("fox_used"), 1)
                        dve.wait_ge(ev("fox_used"), h + 1)
                        b0, b1 = fb[:, 0:128], fb[:, 128:384]
                    else:
                        b0, b1 = bias[:, b, 128:256], bias[:, b, 0:256]
                    if i >= 3:
                        dve.wait_ge(pT_ready, g - 2)
                    for tt, (lo, hi, bb) in enumerate(((0, 128, b0), (128, 384, b1))):
                        last = dve.tensor_tensor_reduce(out=sP[:, g % 3, lo:hi], in0=bank[g % 3][:, lo:hi], in1=bb,
                                                        scale=-1.0, scalar=3.0e38, op0=ALU.add, op1=ALU.min,
                                                        accum_out=mx[:, g % 3, tt:tt + 1])
                    last.then_inc(s_max, 1)

                def normalise(i):
                    g = g0 + i
                    _, _, _, dv, _, oc = heads[i]
                    dve.wait_ge(o_ready, g + 1)
                    step(dve.reciprocal(rs[:, g % 4, :], sums[:, g % 4, :]))
                    second = name == "ab" and i < 8 and i % 2 == 1
                    if second:
                        step(TS(rs[:, g % 4, :], rs[:, g % 4, :], neg_lam, None, ALU.mult))
                    for tt in range(TT):
                        src, dst = bank[5 + g % 2][:, tt * dv:tt * dv + dv], nat[:, tt, oc:oc + dv]
                        r = rs[:, g % 4, tt:tt + 1]
                        if second:
                            last = STT(dst, src, r, dst, ALU.mult, ALU.add)
                        else:
                            last = TS(dst, src, r, None, ALU.mult)
                    last.then_inc(o_done, 1)
                    if name == "ab" and i < 8:
                        dve.wait_ge(o_done, g + 1)

                for s in range(len(heads) + 3):
                    if s < len(heads):
                        maxima(s)
                    if s >= 3:
                        normalise(s - 3)

            def ffn(name, with_ada=False):
                n0, f = START[name], 11 * FFN[name]

                def hidden(i, n, slot):
                    TTn(act, sil, bank[5][:], ALU.mult).then_inc(act_mul, 1)
                    dve.wait_ge(act_hi, i + (f + 1))
                    TTn(aL[:], act.rearrange("p (a t) -> p a t", a=2), aH[:].bitcast(F32), ALU.subtract).then_inc(act_lo, 1)
                    split(slot, n)

                split_py(n0 + 3)
                dve.wait_ge(sil_done, f + 1)
                dve.wait_ge(unit_used, n0 + USED0 + 2)
                hidden(0, n0 + 4, (n0 + 4) % RING)

                def body(i):
                    n = i * 3 + (n0 - 1)
                    split((n0 + 5) % RING, n + 3)
                    split((n0 + 6) % RING, n + 4)
                    dve.wait_ge(sil_done, i + (f + 1))
                    dve.wait_ge(unit_used, n + (USED0 + 3))
                    hidden(i, n + 5, (n0 + 7) % RING)

                if with_ada:
                    with dve.Fori(0, 2) as m:
                        with dve.Fori(0, 4) as j:
                            b = m * 4 + j
                            ada(1, b + 6)
                            body(b + 1)
                with dve.Fori(9 if with_ada else 1, FC - 1) as i:
                    body(i)
                body(FC - 1)

            def y_in(tt, name):
                if tt == 0:
                    dve.wait_ge(y_first, SUMS[name] + 1)
                else:
                    dve.wait_ge(unit_used, START[name] + (33 if name in FFN else 4) + USED0)

            def layer_norm(e, gate, y):
                def residual(tt):
                    y_in(tt, y)
                    for h in range(2):
                        last = TTn(nat[:, tt, 512 * h:512 * h + 512], bank[2 * tt + h][:],
                                   gate1[:, gate, 512 * h:512 * h + 512], ALU.mult)
                    step(last)
                    step(STT(x[:, tt, :], x[:, tt, :], ALPHA, nat[:, tt, :], ALU.mult, ALU.add))

                def stats(tt):
                    for h in range(2):
                        last = dve.bn_stats(stat[:, tt, 6 * h:6 * h + 6], x[:, tt, 512 * h:512 * h + 512])
                    step(last)
                    dve.bn_aggr(mv[:, tt, :], stat[:, tt, 0:12].rearrange("p (h s) -> p h s", h=2)).then_inc(var_ready, 1)

                def normalise(tt):
                    dve.wait_ge(std_ready, 2 * e + tt + 1)
                    step(dve.reciprocal(rstd[:, tt:tt + 1], std[:, tt:tt + 1]))
                    TS(x[:, tt, :], x[:, tt, :], mv[:, tt, 0:1], rstd[:, tt:tt + 1], ALU.subtract, ALU.mult)\
                        .then_inc(nat_ready if e < 3 else ev("x_norm"), 1)

                residual(0)
                stats(0)
                residual(1)
                normalise(0)
                stats(1)
                normalise(1)
                if e == 3:
                    affine(e)

            def affine(e):
                dve.wait_ge(ln_loaded, 32 * (e + 1))
                if e == 3:
                    dve.wait_ge(ev("x_norm"), 2)
                else:
                    dve.wait_ge(tr_done, TRD[LN_TR[e]] + 4)
                for tt in range(TT):
                    TTn(x[:, tt, :], x[:, tt, :], lnv[:, 0, :], ALU.mult).then_inc(ev("x_gain"), 1)
                for tt in range(TT):
                    dve.wait_ge(ev("x_gain"), 2 * e + tt + 1)
                    TTn(x[:, tt, :], x[:, tt, :], lnv[:, 1, :], ALU.add).then_inc(ev("x_done"), 1)
                dve.wait_ge(ev("x_done"), 2 * e + 2)
                dve.sem_inc(ln_used, 1)

            def rms(e, add=None, y=None, last=False):
                for tt in range(TT):
                    if add is not None:
                        y_in(tt, y)
                        for h in range(2):
                            xs = x[:, tt, 512 * h:512 * h + 512]
                            ins = STT(xs, bank[2 * tt + h][:], add, xs, ALU.mult, ALU.add)
                        ins.then_inc(ev("x_final" if last else "x_sum"), 1)
                if last:
                    return
                for tt in range(TT):
                    dve.wait_ge(std_ready, 2 * e + tt + 1)
                    step(dve.reciprocal(rstd[:, tt:tt + 1], std[:, tt:tt + 1]))
                    TS(diag[:, tt, :], ident[:], rstd[:, tt:tt + 1], None, ALU.mult).then_inc(nat_ready, 1)

            for s, k in ((lo_ready, LO0), (unit_used, USED0), (proj_evac, EVAC0), (nat_ready, 2), (ada_mm[0], 1),
                         (ada_mm[1], 1), (ada_out[0], 1), (ada_out[1], 1)):
                dve.sem_inc(s, k)
            dve.memset(ada_b[:], 0.0).then_inc(ev("ada_b_zero"), 1)
            dve.memset(ones[:], 1.0)
            dve.memset(eps_ln, LN_EPS)
            dve.memset(eps_rms, RMS_EPS)
            dve.memset(zeros[:], 0.0).then_inc(ev("consts"), 1)
            dve.wait_ge(ev("silc"), 1)
            ada(0, 0, 0)
            ada(1, 0, 1)
            dve.wait_ge(setup_in, 16 * SETUP_LOADS)
            dve.wait_ge(ev("rows_in"), 16 * ROW_LOADS)
            dve.tensor_copy(rowC[32:48, :].rearrange("n (g p) -> n g p", g=2), dt2.unsqueeze(2).to_broadcast([16, 2, HD]))\
                .then_inc(ev("dt_rows"), 1)
            dve.wait_ge(ev("toep_mm"), 1)
            TTn(toepA, bank[1][0:20, 0:TOEP], addc, ALU.add).then_inc(ev("toep_rows"), 1)
            dve.tensor_copy(toepE[:, 0:128], relrow[:, 256:257].to_broadcast([8, 128]))
            step(dve.memset(toepE[:, 383:384], 0.0))
            dve.tensor_copy(toepE[:, 128:383], relrow[:, 255:0:-1]).then_inc(ev("toep_rows"), 1)
            dve.tensor_tensor_reduce(out=lamrow[:, 0:64], in0=lamrow[:, 0:64], in1=lamrow[:, 64:128], scale=1.0,
                                     scalar=0.0, op0=ALU.mult, op1=ALU.add, accum_out=lam[0:1, 0:1])
            dve.tensor_tensor_reduce(out=lamrow[:, 128:192], in0=lamrow[:, 128:192], in1=lamrow[:, 192:256], scale=1.0,
                                     scalar=0.0, op0=ALU.mult, op1=ALU.add, accum_out=lam[0:1, 1:2]).then_inc(ev("lam_sums"), 1)
            dve.wait_ge(ev("cols_tr"), 1)
            dve.tensor_copy(lnC[:], bank[2][:, 176:240])
            dve.tensor_copy(colC[:], bank[2][:, 128:176]).then_inc(ev("cols_ready"), 1)
            step(dve.tensor_copy(cols[:], bank[2][:, 0:NCOL]))
            TS(cols[:, C_SUBLN:C_SUBLN + 1], cols[:, C_SUBLN:C_SUBLN + 1], 1.0 - LAMBDA_INIT, None, ALU.mult)
            TS(cols[:, C_QN:C_QN + 1], cols[:, C_QN:C_QN + 1], ATTN_SCALE, None, ALU.mult).then_inc(ev("cols_ready"), 1)
            dve.wait_ge(ev("lam_exp"), 1)
            step(TTn(lam[0:1, 4:5], lam[0:1, 3:4], lam[0:1, 2:3], ALU.subtract))
            TS(lam[0:1, 5:6], lam[0:1, 4:5], -LAMBDA_INIT, None, ALU.add).then_inc(ev("lam_row"), 1)
            dve.wait_ge(ev("lam_col"), 1)
            dve.tensor_copy(neg_lam, bank[2][:, 256:257])
            ar, ai = colC[:, 0:16], colC[:, 16:32]
            co, si, fr, fi, mag, t5, dt, th, r, sh, t10, t11 = (s5c[:, n, :] for n in range(12))
            dve.wait_ge(ev("s5_dt"), 1)
            step(TTn(th, dt, ai, ALU.mult))
            step(TS(t10, th, 1.0 / (2.0 * np.pi), ROUND_MAGIC, ALU.mult, ALU.add))
            step(TS(t10, t10, ROUND_MAGIC, None, ALU.subtract))
            step(STT(r, t10, -TWO_PI_PARTS[0], th, ALU.mult, ALU.add))
            step(STT(r, t10, -TWO_PI_PARTS[1], r, ALU.mult, ALU.add))
            step(STT(r, t10, -TWO_PI_PARTS[2], r, ALU.mult, ALU.add))
            step(TS(r, r, 3.1415925, -3.1415925, ALU.min, ALU.max))
            TTn(th, dt, ar, ALU.mult).then_inc(ev("s5_angle"), 1)
            ada(0, 1, 2)
            ada(1, 1, 3)
            dve.wait_ge(ada_out[0], 3)
            dve.wait_ge(ada_out[1], 3)
            step(TS(adaC[:, 0, 8:16], adaC[:, 0, 8:16], 1.0, None, ALU.add))
            dve.sem_inc(ev("scale_ready"), 1)
            transposed("ab", lambda c: adaC[:, 0, 8 + c:9 + c], lambda c: adaC[:, 0, c:c + 1], whole=False)
            for n in range(RING):
                split_py(n)
            dve.wait_ge(ev("s5_sin"), 2)
            step(TTn(t10, sh, sh, ALU.mult))
            step(TS(co, t10, -2.0, 1.0, ALU.mult, ALU.add))
            step(TTn(t10, mag, co, ALU.mult))
            step(TS(t10, t10, -1.0, None, ALU.add))
            step(TTn(t11, mag, si, ALU.mult))
            step(TTn(th, ar, ar, ALU.mult))
            step(TTn(r, ai, ai, ALU.mult))
            step(TTn(th, th, r, ALU.add))
            step(dve.reciprocal(t5, th))
            step(TTn(th, t10, ar, ALU.mult))
            step(TTn(r, t11, ai, ALU.mult))
            step(TTn(th, th, r, ALU.add))
            step(TTn(fr, th, t5, ALU.mult))
            step(TTn(th, t11, ar, ALU.mult))
            step(TTn(r, t10, ai, ALU.mult))
            step(TTn(th, th, r, ALU.subtract))
            step(TTn(fi, th, t5, ALU.mult))

            def join(e, l, at):
                sh, sc = adaC[:, l, at:at + 8], adaC[:, l, at + 8:at + 16]
                step(TS(sc, sc, 1.0, None, ALU.add))
                step(TTn(lnS[:, e, 0:8], lnC[:, 8 * e:8 * e + 8], sc, ALU.mult))
                step(TTn(lnS[:, e, 8:16], lnC[:, 32 + 8 * e:40 + 8 * e], sc, ALU.mult))
                step(TTn(lnS[:, e, 8:16], lnS[:, e, 8:16], sh, ALU.add))

            def normed(e):
                name = LN_TR[e]
                transposed(name, lambda c: lnS[:, e, c:c + 1], lambda c: lnS[:, e, 8 + c:9 + c], whole=False)
                split_py(START[name] + 2)
                affine(e)

            e = 0
            for l, (p, o, f) in enumerate((("ab", "o_ab", "ff0"), ("cd", "o_cd", "ff1"))):
                if l == 1:
                    normed(1)
                if l == 1:
                    dve.wait_ge(ev("fd_mm"), 1)
                    step(TS(F8[1], bank[7][0:8, 0:T], a8[:, 0:1], -1.0, ALU.add, ALU.mult))
                    STT(F8[0], F8[1], -1.0, F8[1], ALU.mult, ALU.min).then_inc(ev("fd_abs"), 1)
                    dve.wait_ge(ev("fd_ln"), 1)
                    step(STT(F8[2], F8[1], 0.0, F8[0], ALU.max, ALU.add))
                    dve.tensor_tensor_scan(F8[3], ones[0:8, 0:1].to_broadcast([8, T]), F8[2], 0.0, ALU.mult, ALU.subtract)\
                        .then_inc(ev("fd_cum"), 1)
                    dve.wait_ge(ev("fd_cum"), 1)
                    dve.wait_ge(ev("forget_hi"), 1)
                    TTn(F8L, F8[3], F8H.bitcast(F32), ALU.subtract).then_inc(ev("forget_lo"), 1)
                qkv(p, l)
                if l == 0:
                    dve.wait_ge(ada_out[1], 7)
                    join(0, 0, 16)
                    dve.wait_ge(flip_out, FLIP0["ab"] + 6)
                else:
                    dve.wait_ge(flip_out, FLIP0["cd"] + 4)
                    dve.wait_ge(ev("fd_cols"), 1)
                    dve.tensor_copy(ccol[:, :, 0:8], bank[7][:, 0:16].rearrange("p (a h) -> p a h", a=TT))\
                        .then_inc(ev("ccol_ready"), 1)
                    dve.wait_ge(ev("ccol_ready"), 1)
                attention(p)
                if l == 0:
                    sq = carve(mix, 0, TT, 512)
                    oa = nat[:, :, 0:512]
                    step(TTn(sq, oa, oa, ALU.mult))
                    dve.reduce_sum(hstat[:, 0, 0:8], sq.rearrange("p a (h d) -> p (a h) d", d=P), AX.X)\
                        .then_inc(ev("sub_var"), 1)
                    dve.wait_ge(ev("sub_std"), 1)
                    step(dve.reciprocal(hstd[:, 1, 0:8], hstd[:, 0, 0:8]))
                    for tt in range(TT):
                        v4 = nat[:, tt, 0:512].rearrange("p (h d) -> p h d", d=P)
                        TTn(v4, v4, hstd[:, 1, 4 * tt:4 * tt + 4].unsqueeze(2).to_broadcast([P, 4, P]), ALU.mult)\
                            .then_inc(nat_ready, 1)
                    transposed(o, lambda c: cols[:, C_SUBLN:C_SUBLN + 1] if c < 4 else ones_col, direct=True)
                else:
                    dve.wait_ge(o_done, HEAD0[p] + len(HEADS[p]))
                    dve.sem_inc(nat_ready, 2)
                    transposed(o, direct=True)
                for u in range(3):
                    split_py(START[o] + u + RING)
                layer_norm(e, 0, o)
                normed(e)
                ffn(f, with_ada=(l == 0))
                if l == 0:
                    dve.wait_ge(ada_out[1], 15)
                    join(1, 1, 0)
                    join(2, 1, 16)
                layer_norm(e + 1, 1, f)
                e += 2
            for l, (f1, p, o, f2) in enumerate((("f1a", "even", "o_even", "f2a"), ("f1b", "odd", "o_odd", "f2b"))):
                gain = lambda at, l=l: (lambda c: cols[:, at + 8 * l + c:at + 8 * l + c + 1])
                rms(e, 0.5 if l else None, "f2a")
                transposed(f1, gain(C_FF1), direct=True)
                split_py(START[f1] + 2)
                ffn(f1)
                rms(e + 1, 0.5, f1)
                transposed(p, gain(C_MIX), direct=(l == 1), whole=False)
                split_py(START[p] + 2)
                if l == 0:
                    even_dve(dve, step, split_py, transposed, lower_part)
                else:
                    odd_dve(dve, step, split_py, transposed, lower_part, attention)
                for u in range(3):
                    split_py(START[o] + u + RING)
                rms(e + 2, 1.0, o)
                transposed(f2, gain(C_FF2), direct=True)
                split_py(START[f2] + 2)
                ffn(f2)
                e += 3
            rms(e, 0.5, "f2b", last=True)

        @block.tensor
        def _(pe):
            mm = pe.matmul

            def unit_in(slot, n):
                pe.wait_ge(lo_ready, n + (LO0 + 1))
                return (wH[:, slot, :].rearrange("p (k c) -> p k c", k=KC), wL[:, slot, :].rearrange("p (k c) -> p k c", k=KC))

            def cols_unit(slot, n, dst):
                H, L = unit_in(slot, n)
                for ft in range(2):
                    for k in range(KC):
                        wh, wl = H[:, k, ft * P:ft * P + P], L[:, k, ft * P:ft * P + P]
                        for i, (w, h) in enumerate(((wh, hH), (wh, hL), (wl, hH))):
                            last = mm(dst[:, ft * T:ft * T + T], w, h[:, k, :], start=(k == 0 and i == 0),
                                      stop=(k == KC - 1 and i == 2))
                last.then_inc(unit_used, 1)

            def toks_unit(slot, n, dst):
                H, L = unit_in(slot, n)
                for tt in range(TT):
                    for k in range(KC):
                        hh, hl = hH[:, k, tt * P:tt * P + P], hL[:, k, tt * P:tt * P + P]
                        for i, (h, w) in enumerate(((hh, H), (hh, L), (hl, H))):
                            last = mm(dst[:, tt * UC:tt * UC + UC], h, w[:, k, :], start=(k == 0 and i == 0),
                                      stop=(k == KC - 1 and i == 2))
                last.then_inc(unit_used, 1)

            def rows_unit(slot, n, H, L, k0, start, stop):
                pe.wait_ge(lo_ready, n + (LO0 + 1))
                wh, wl = (w[:, slot, :].rearrange("p (k c) -> p k c", k=2) for w in (wH, wL))
                for tt in range(TT):
                    for h in range(2):
                        for k in range(2):
                            c = slice(512 * h, 512 * h + 512)
                            ah, al = (z[:, k0 + k, tt * P:tt * P + P] for z in (H, L))
                            for i, (s, w) in enumerate(((ah, wh), (ah, wl), (al, wh))):
                                last = mm(bank[2 * tt + h][:], s, w[:, k, c], start=(start and k == 0 and i == 0),
                                          stop=(stop and k == 1 and i == 2), skip_group_check=True)
                    if stop and tt == 0:
                        last.then_inc(y_first, 1)
                last.then_inc(unit_used, 1)

            def ada(l, slot, cnt, gate):
                pe.wait_ge(ada_step[slot], cnt * 8 + 8)
                pe.wait_ge(ada_out[slot], cnt + 1)
                acc = ada_acc[:, slot, :]
                if gate:
                    mm(bank[7][:], ones[:], acc, start=True, stop=True).then_inc(ada_mm[slot], 1)
                else:
                    b = bank[0 if slot == 0 else 3]
                    for u in range(4):
                        last = mm(b[:, u:u + 1], acc[:, u * P:u * P + P], ones_col, start=True, stop=True)
                    last.then_inc(ada_mm[slot], 1)

            def transposed(name, src, chunks=KC, scaled=False):
                for tt in range(TT):
                    pe.wait_ge(nat_ready, 2 * TR[name] + tt + 1)
                    for k in range(chunks):
                        at = (k % 2) * T + tt * P
                        dst, piece = bank[4 + k // 2][:, at:at + P], src[:, tt, k * P:k * P + P]
                        if scaled:
                            last = mm(dst, piece, diag[:, tt, :], start=True, stop=True)
                        else:
                            last = pe.transpose(dst, piece, ident[:])
                        if tt and k % 2:
                            last.then_inc(tr_done, 1)

            def split_ready(name):
                pe.wait_ge(tl_ready, 4 * TR[name] + 4)

            def narrow(which):
                pe.wait_ge(ev("narrow_in"), 32)
                for k in range(KC):
                    last = mm(bank[7][0:8, 0:T], wsmall[:, which, k, :], t32[:, k, :], start=(k == 0), stop=(k == KC - 1))
                return last

            def qkv(name, l):
                n0, u0 = START[name], PROJ[name]
                with pe.Fori(0, 2) as m:
                    with pe.Fori(0, 2) as j:
                        it = m * 2 + j
                        for u in range(3):
                            pe.wait_ge(proj_evac, it * 3 + (u0 + u + EVAC0 - 2))
                            (toks_unit if u == 2 else cols_unit)((n0 + u) % RING, it * 3 + (n0 + u), bank[4 + u])
                        ada(l, 0, it + (2 if l == 0 else 6), True)
                        if l == 0:
                            ada(0, 1, it + 2, False)

            def flipped(name, arrived):
                pe.wait_ge(toep_in, arrived)
                for n in range(FLIPS[name]):
                    if n >= 3:
                        pe.wait_ge(flip_out, FLIP0[name] + n - 2)
                    mm(bank[FLIP_BANK[name] + n % 3][:], flip[:], bias[:, 2 * n:2 * n + 2, :], start=True, stop=True).then_inc(flip_mm, 1)
                pe.wait_ge(flip_out, FLIP0[name] + FLIPS[name])

            def attention(name):
                g0, heads = HEAD0[name], HEADS[name]
                fox = [0]

                def scores(i):
                    g = g0 + i
                    tile, base, _, _, b, _ = heads[i]
                    if i >= 3:
                        pe.wait_ge(s_max, g - 2)
                    if b is None:
                        if fox[0]:
                            pe.wait_ge(ev("fox_used"), fox[0])
                        pick = head_one[0:8, fox[0]:fox[0] + 1].to_broadcast([8, P])
                        mm(bank[7][:, 0:T], pick, F8H, start=True, stop=False)
                        mm(bank[7][:, 0:T], pick, F8L, start=False, stop=True)
                        fox[0] += 1
                    q, k = qT[base:base + HD, tile, :], kT[base:base + HD, tile, :]
                    mm(bank[g % 3][:, 0:128], q[:, 0:P], k[:, 0:P], start=True, stop=True)
                    mm(bank[g % 3][:, 128:384], q[:, P:T], k, start=True, stop=True).then_inc(s_ready, 1)

                def turn(i):
                    g = g0 + i
                    pe.wait_ge(p_ready, g + 1)
                    if i >= 2:
                        pe.wait_ge(pT_copied, g - 1)
                    for b in range(3):
                        last = pe.transpose(bank[3 + g % 2][:, b * P:b * P + P], sP[:, g % 3, b * P:b * P + P], ident[:])
                    last.then_inc(pT_ready, 1)

                def values(i):
                    g = g0 + i
                    _, _, vc, dv, _, _ = heads[i]
                    pe.wait_ge(pT_copied, g + 1)
                    if i >= 2:
                        pe.wait_ge(o_done, g - 1)
                    o, w = bank[5 + g % 2], PT[:, g % 2, :]
                    mm(o[:, 0:dv], w[:, 0:P], v[:, 0, vc:vc + dv], start=True, stop=True)
                    mm(o[:, dv:2 * dv], w[:, P:2 * P], v[:, 0, vc:vc + dv], start=True, stop=False)
                    mm(o[:, dv:2 * dv], w[:, 2 * P:3 * P], v[:, 1, vc:vc + dv], start=False, stop=True).then_inc(o_ready, 1)

                for s in range(len(heads) + 3):
                    if s < len(heads):
                        scores(s)
                    if 2 <= s < len(heads) + 2:
                        turn(s - 2)
                    if s >= 3:
                        values(s - 3)

            def out_proj(name):
                split_ready(name)
                n0 = START[name]
                for u in range(4):
                    rows_unit((n0 + u) % RING, n0 + u, hH, hL, 2 * u, u == 0, u == 3)

            def ffn(name, with_ada=False):
                split_ready(name)
                n0, f = START[name], 11 * FFN[name]
                for b in range(4):
                    mm(bank[b][:], zeros[:, 0:128], zeros[:, 128:640], start=True, stop=False, skip_group_check=True)
                cols_unit(n0 % RING, n0, bank[4])
                cols_unit((n0 + 1) % RING, n0 + 1, bank[5])

                def body(i):
                    n = i * 3 + (n0 - 1)
                    pe.wait_ge(sil_done, i + f)
                    cols_unit((n0 + 2) % RING, n, bank[4])
                    pe.wait_ge(act_lo, i + f)
                    rows_unit((n0 + 3) % RING, n + 1, aH, aL, 0, False, False)
                    cols_unit((n0 + 4) % RING, n + 2, bank[5])

                if with_ada:
                    with pe.Fori(0, 2) as m:
                        with pe.Fori(0, 4) as j:
                            b = m * 4 + j
                            body(b + 1)
                            ada_late(b)
                with pe.Fori(9 if with_ada else 1, FC) as i:
                    body(i)
                pe.wait_ge(act_lo, FC + f)
                rows_unit((n0 + 32) % RING, n0 + 32, aH, aL, 0, False, True)

            def ada_late(b):
                pe.wait_ge(ada_step[1], b * 8 + 56)
                pe.wait_ge(ada_out[1], b + 7)
                for u in range(4):
                    last = mm(bank[7][:, u:u + 1], ada_acc[:, 1, u * P:u * P + P], ones_col, start=True, stop=True)
                last.then_inc(ada_mm[1], 1)

            pe.wait_ge(ev("first_in"), 32)
            pe.transpose(bank[0][:, 0:8], rows_c, ident[0:8, 0:8]).then_inc(ev("c_cols"), 1)
            pe.wait_ge(ev("consts"), 1)
            ada(0, 0, 0, False)
            ada(0, 1, 0, False)
            pe.wait_ge(setup_in, 16 * SETUP_LOADS)
            pe.wait_ge(ev("rows_in"), 16 * ROW_LOADS)
            mm(bank[1][0:20, 0:TOEP], table, onehot, start=True, stop=True).then_inc(ev("toep_mm"), 1)
            pe.wait_ge(ev("dt_rows"), 1)
            pe.transpose(bank[2][:, 0:NCOL], rows, ident[0:NCOL, 0:NCOL])
            pe.transpose(bank[2][:, 176:240], rowL, ident[0:64, 0:64])
            pe.transpose(bank[2][:, 128:176], rowC, ident[0:48, 0:48]).then_inc(ev("cols_tr"), 1)
            pe.wait_ge(ev("lam_row"), 1)
            mm(bank[2][:, 256:257], ones[0:1, :], lam[0:1, 5:6], start=True, stop=True).then_inc(ev("lam_col"), 1)
            ada(0, 0, 1, False)
            pe.wait_ge(ev("x_in"), 16)
            transposed("ab", x)
            ada(0, 1, 1, False)
            pe.wait_ge(ada_out[0], 3)
            flipped("ab", 16)

            for l, (p, o, f) in enumerate((("ab", "o_ab", "ff0"), ("cd", "o_cd", "ff1"))):
                if l == 1:
                    transposed(p, x)
                    pe.wait_ge(t32_ready, T32["cd"] + 2)
                    pe.wait_ge(t32_odd, T32_ODD["cd"] + 2)
                    narrow(0).then_inc(ev("fd_mm"), 1)
                split_ready(p)
                qkv(p, l)
                pe.wait_ge(proj_evac, PROJ[p] + 12 + EVAC0)
                if l == 1:
                    pe.wait_ge(ada_out[0], 11)
                    pe.wait_ge(ev("fd_cum"), 1)
                    pe.wait_ge(ev("forget_lo"), 1)
                    for tt in range(TT):
                        last = pe.transpose(bank[7][:, 8 * tt:8 * tt + 8], F8[3][:, tt * P:tt * P + P], ident[0:8, 0:8])
                    last.then_inc(ev("fd_cols"), 1)
                    pe.wait_ge(ev("ccol_ready"), 1)
                attention(p)
                transposed(o, nat)
                out_proj(o)
                if l == 0:
                    flipped("cd", 32)
                transposed(f, x)
                ffn(f, with_ada=(l == 0))
            for l, (f1, p, o, f2) in enumerate((("f1a", "even", "o_even", "f2a"), ("f1b", "odd", "o_odd", "f2b"))):
                if l == 1:
                    flipped("odd", 48)
                transposed(f1, x, scaled=True)
                ffn(f1)
                if l == 0:
                    pe.wait_ge(ev("bp_ready"), 1)
                    for i, src in enumerate((BP[:, 0].rearrange("p (m j) c -> p m (j c)", m=4),
                                             BP[:, 1].rearrange("p (m j) c -> p m (j c)", m=4), Cpad[:, 0], Cpad[:, 1])):
                        for m in range(4):
                            last = pe.transpose(bank[4 + i][:, m * P:m * P + P], src[:, m, :], ident[:])
                    last.then_inc(ev("s5_tr"), 1)
                    pe.wait_ge(ev("s5_bc"), 1)
                transposed(p, x, scaled=True)
                if l == 0:
                    pe.wait_ge(t32_ready, T32["even"] + 2)
                    pe.wait_ge(t32_odd, T32_ODD["even"] + 2)
                    narrow(1).then_inc(ev("dt_mm"), 1)
                split_ready(p)
                for u in range(8):
                    n, k = START[p] + u, PROJ[p] + u
                    pe.wait_ge(proj_evac, k + EVAC0 - 2)
                    (toks_unit if u < (2, 6)[l] else cols_unit)(n % RING, n, bank[4 + k % 3])
                (even_pe if l == 0 else odd_pe)(pe, mm, transposed, attention)
                out_proj(o)
                transposed(f2, x, scaled=True)
                ffn(f2)

    return nc


_SHAPE = (1, T, D)


def kernel(**inputs):
    import concourse.bacc as bacc
    from concourse.bass_utils import run_bass_kernel_spmd

    nc = bacc.Bacc("TRN2", target_bir_lowering=False, num_devices=1)
    arrays, args = {}, {}
    for name, value in {**inputs, **constants()}.items():
        value = np.ascontiguousarray(value)
        arrays[f"in_{name}"] = value
        args[name] = nc.dram_tensor(f"in_{name}", value.shape, mybir.dt.from_np(value.dtype), kind="ExternalInput").ap()
    out = nc.dram_tensor("out", _SHAPE, F32, kind="ExternalOutput").ap()
    build_program(nc, args, out)
    result = run_bass_kernel_spmd(nc, [arrays], core_ids=[0])
    return result.results[0]["out"]
```
